# Optimizing a Trainium2 kernel written in Bass

```python
import jax, jax.numpy as jnp
from jax import lax
import numpy as np
import math

D_MODEL = 1024
BATCH = 1
SEQ = 512
DEPTH = 1

SB_HEADS = 8
SB_HEAD_DIM = 64
SB_WIDTH = SB_HEADS * SB_HEAD_DIM
SB_BLOCK = 128

GLA_HEADS = 4
GLA_DK = 64
GLA_DV = 128
GLA_KW = GLA_HEADS * GLA_DK
GLA_VW = GLA_HEADS * GLA_DV
GLA_RANK = 16
GLA_TAU = 16.0
GLA_CHUNK = 64

D_FF = 2816
CONV_WIDTH = 3

EPS = 1e-6

IN_SIZES = (SB_WIDTH, SB_WIDTH, SB_WIDTH,
            GLA_KW, GLA_KW, GLA_VW, GLA_VW,
            GLA_RANK,
            D_MODEL, D_MODEL)
IN_TOTAL = sum(IN_SIZES)


def rms_norm(x, g):
    xf = x.astype(jnp.float32)
    xf = xf * lax.rsqrt(jnp.mean(xf * xf, axis=-1, keepdims=True) + EPS)
    return xf.astype(x.dtype) * g

def to_heads(t, n_heads):
    b, s, _ = t.shape
    return t.reshape(b, s, n_heads, -1).transpose(0, 2, 1, 3)

def from_heads(t):
    b, h, s, d = t.shape
    return t.transpose(0, 2, 1, 3).reshape(b, s, h * d)

def stick_breaking_attention(q, k, v):
    s_len, dh = q.shape[2], q.shape[3]
    scale = dh ** -0.5
    outs = []
    for i0 in range(0, s_len, SB_BLOCK):
        end = i0 + SB_BLOCK
        qb = q[:, :, i0:end]
        kb = k[:, :, :end]
        vb = v[:, :, :end]
        z = jnp.einsum('bhqd,bhkd->bhqk', qb, kb).astype(jnp.float32) * scale
        t_idx = i0 + jnp.arange(SB_BLOCK)[:, None]
        s_idx = jnp.arange(end)[None, :]
        strict = s_idx < t_idx
        log_keep = jnp.where(strict, jax.nn.log_sigmoid(-z), 0.0)
        tail = lax.cumsum(log_keep, axis=3, reverse=True) - log_keep
        log_w = jax.nn.log_sigmoid(z) + tail
        w = jnp.where(strict, jnp.exp(log_w), 0.0)
        outs.append(jnp.einsum('bhqk,bhkd->bhqd', w.astype(v.dtype), vb))
    return jnp.concatenate(outs, axis=2)

def gla_chunked(q, k, v, log_a):
    b, h, s_len, dk = q.shape
    dv = v.shape[-1]
    c = GLA_CHUNK
    n = s_len // c
    qf = q.astype(jnp.float32).reshape(b, h, n, c, dk)
    kf = k.astype(jnp.float32).reshape(b, h, n, c, dk)
    vf = v.astype(jnp.float32).reshape(b, h, n, c, dv)
    cum = jnp.cumsum(log_a.reshape(b, h, n, c, dk), axis=3)
    cum_last = cum[:, :, :, -1:]
    q_dec = qf * jnp.exp(cum)
    k_inv = kf * jnp.exp(-cum)
    k_to_end = kf * jnp.exp(cum_last - cum)
    att = jnp.einsum('bhnck,bhnsk->bhncs', q_dec, k_inv)
    causal = jnp.tril(jnp.ones((c, c), dtype=bool))
    att = jnp.where(causal, att, 0.0)
    o_intra = jnp.einsum('bhncs,bhnsv->bhncv', att, vf)
    d_state = jnp.einsum('bhnck,bhncv->bhnkv', k_to_end, vf)
    chunk_decay = jnp.exp(cum_last[:, :, :, 0])

    def step(state, inp):
        dec, ds = inp
        return dec[..., None] * state + ds, state

    init = jnp.zeros((b, h, dk, dv), jnp.float32)
    _, states_before = lax.scan(step, init,
                                (jnp.moveaxis(chunk_decay, 2, 0), jnp.moveaxis(d_state, 2, 0)))
    states_before = jnp.moveaxis(states_before, 0, 2)
    o_inter = jnp.einsum('bhnck,bhnkv->bhncv', q_dec, states_before)
    return (o_intra + o_inter).reshape(b, h, s_len, dv)

def mixing_sublayer(xn, w_in, b_gate, w_alpha_up, b_alpha, gla_norm_g,
                    w_branch_sb, w_branch_gla, w_out):
    proj = xn @ w_in
    offsets = np.cumsum(IN_SIZES)[:-1].tolist()
    (sb_q, sb_k, sb_v, g_q, g_k, g_v, g_r, g_a,
     gate_sb, gate_gla) = jnp.split(proj, offsets, axis=-1)

    o_sb = stick_breaking_attention(to_heads(sb_q, SB_HEADS),
                                    to_heads(sb_k, SB_HEADS),
                                    to_heads(sb_v, SB_HEADS))
    o_sb = from_heads(o_sb)

    a_pre = (g_a @ w_alpha_up + b_alpha).astype(jnp.float32)
    log_a = jax.nn.log_sigmoid(a_pre) / GLA_TAU
    o_gla = gla_chunked(to_heads(g_q, GLA_HEADS) * (GLA_DK ** -0.5),
                        to_heads(g_k, GLA_HEADS),
                        to_heads(g_v, GLA_HEADS),
                        to_heads(log_a, GLA_HEADS))
    o_gla = o_gla * lax.rsqrt(jnp.mean(o_gla * o_gla, axis=-1, keepdims=True) + EPS)
    o_gla = from_heads(o_gla).astype(xn.dtype) * gla_norm_g * jax.nn.silu(g_r)

    y = (jax.nn.sigmoid(gate_sb + b_gate[0]) * (o_sb @ w_branch_sb)
         + jax.nn.sigmoid(gate_gla + b_gate[1]) * (o_gla @ w_branch_gla))
    return y @ w_out

def causal_depthwise_conv(u, w, bias):
    k_w = w.shape[0]
    s_len = u.shape[1]
    up = jnp.pad(u, ((0, 0), (k_w - 1, 0), (0, 0)))
    out = bias
    for i in range(k_w):
        out = out + up[:, i:i + s_len] * w[i]
    return out

def conv_ffn(hn, w_ffn_in, conv_w, conv_b, w_ffn_out):
    u = hn @ w_ffn_in
    a, g = jnp.split(u, 2, axis=-1)
    a = causal_depthwise_conv(a, conv_w, conv_b)
    return (jax.nn.gelu(a) * g) @ w_ffn_out

def first_inputs(seed: int = 0) -> dict:
    key = jax.random.key(seed)
    ks = jax.random.split(key, 16)
    f32 = jnp.float32

    def nrm(k, shape, scale):
        return jax.random.normal(k, shape, f32) * scale

    return {
        "x": jax.random.normal(ks[0], (BATCH, SEQ, D_MODEL), f32),
        "norm_mix_g": 1.0 + nrm(ks[1], (DEPTH, D_MODEL), 0.02),
        "w_in": nrm(ks[2], (DEPTH, D_MODEL, IN_TOTAL), D_MODEL ** -0.5),
        "b_gate": nrm(ks[3], (DEPTH, 2, D_MODEL), 0.02),
        "w_alpha_up": nrm(ks[4], (DEPTH, GLA_RANK, GLA_KW), GLA_RANK ** -0.5),
        "b_alpha": nrm(ks[5], (DEPTH, GLA_KW), 0.1),
        "gla_norm_g": 1.0 + nrm(ks[6], (DEPTH, GLA_VW), 0.02),
        "w_branch_sb": nrm(ks[7], (DEPTH, SB_WIDTH, D_MODEL), SB_WIDTH ** -0.5),
        "w_branch_gla": nrm(ks[8], (DEPTH, GLA_VW, D_MODEL), GLA_VW ** -0.5),
        "w_out": nrm(ks[9], (DEPTH, D_MODEL, D_MODEL), D_MODEL ** -0.5),
        "norm_ffn_g": 1.0 + nrm(ks[10], (DEPTH, D_MODEL), 0.02),
        "w_ffn_in": nrm(ks[11], (DEPTH, D_MODEL, 2 * D_FF), D_MODEL ** -0.5),
        "conv_w": nrm(ks[12], (DEPTH, CONV_WIDTH, D_FF), CONV_WIDTH ** -0.5),
        "conv_b": nrm(ks[13], (DEPTH, D_FF), 0.01),
        "w_ffn_out": nrm(ks[14], (DEPTH, D_FF, D_MODEL), D_FF ** -0.5),
        "norm_final_g": 1.0 + nrm(ks[15], (D_MODEL,), 0.02),
    }

def first_block(x, norm_mix_g, w_in, b_gate, w_alpha_up, b_alpha, gla_norm_g,
              w_branch_sb, w_branch_gla, w_out, norm_ffn_g, w_ffn_in, conv_w,
              conv_b, w_ffn_out, norm_final_g):
    h = x
    for i in range(DEPTH):
        xn = rms_norm(h, norm_mix_g[i])
        h = h + mixing_sublayer(xn, w_in[i], b_gate[i], w_alpha_up[i], b_alpha[i],
                                gla_norm_g[i], w_branch_sb[i], w_branch_gla[i], w_out[i])
        hn = rms_norm(h, norm_ffn_g[i])
        h = h + conv_ffn(hn, w_ffn_in[i], conv_w[i], conv_b[i], w_ffn_out[i])
    return rms_norm(h, norm_final_g)


DEPTH_2 = 2

N_MIXERS = 2
N_A_LAYERS = (DEPTH_2 + 1) // 2
N_B_LAYERS = DEPTH_2 // 2

CHUNK = 128
GATE_WIDTH = D_MODEL
GATE_GROUPS = 8
GATE_GROUP_DIM = GATE_WIDTH // GATE_GROUPS

WINDOW_DILATIONS = ((128, 1), (512, 4), (2048, 16))
N_DIL_GROUPS = len(WINDOW_DILATIONS)
ATT_HEADS = 8
HEAD_DIM = 64
ATT_WIDTH = ATT_HEADS * HEAD_DIM

N_BUCKETS = 32
MAX_EXACT = N_BUCKETS // 2
REL_MAX_DISTANCE = max(w for w, _ in WINDOW_DILATIONS)

D_FF_2 = 4 * D_MODEL

NEG_INF = -1e30


def _rms_norm(x, g):
    xf = x.astype(jnp.float32)
    y = xf * lax.rsqrt(jnp.mean(xf * xf, axis=-1, keepdims=True) + EPS)
    return (y * g.astype(jnp.float32)).astype(x.dtype)

def _layer_norm(x, g, b):
    xf = x.astype(jnp.float32)
    mu = jnp.mean(xf, axis=-1, keepdims=True)
    xc = xf - mu
    y = xc * lax.rsqrt(jnp.mean(xc * xc, axis=-1, keepdims=True) + EPS)
    return (y * g.astype(jnp.float32) + b.astype(jnp.float32)).astype(x.dtype)

def _t5_bucket(distance):
    small = distance < MAX_EXACT
    nf = jnp.maximum(distance, 1).astype(jnp.float32)
    large = MAX_EXACT + (jnp.log(nf / MAX_EXACT) / math.log(REL_MAX_DISTANCE / MAX_EXACT)
                         * (N_BUCKETS - MAX_EXACT)).astype(jnp.int32)
    large = jnp.minimum(large, N_BUCKETS - 1)
    return jnp.where(small, distance, large)

def _chunk_gating_mixer(h, w_in, ln_g, ln_b, w_s, b_s, w_out):
    B_, S_, _ = h.shape
    uv = jax.nn.gelu(h @ w_in, approximate=False)
    u, v = jnp.split(uv, 2, axis=-1)
    v = _layer_norm(v, ln_g, ln_b)
    nc = S_ // CHUNK
    v = v.reshape(B_, nc, CHUNK, GATE_GROUPS, GATE_GROUP_DIM)
    causal = jnp.tril(jnp.ones((CHUNK, CHUNK), dtype=bool))
    w = jnp.where(causal[None], w_s, 0.0)
    mixed = jnp.einsum('gts,bnsgc->bntgc', w, v) + b_s.T[None, None, :, :, None]
    gate = mixed.reshape(B_, S_, GATE_WIDTH)
    return (u * gate) @ w_out

def _dilated_group(q, k, v, bias_table, window, dilation):
    B_, S_, H, hd = q.shape
    blk = window // dilation
    span = blk * dilation
    Sp = -(-S_ // span) * span
    nb = Sp // span

    def split(t):
        t = jnp.pad(t, ((0, 0), (0, Sp - S_), (0, 0), (0, 0)))
        return t.reshape(B_, nb, blk, dilation, H, hd)

    def with_prev(t):
        prev = jnp.pad(t, ((0, 0), (1, 0), (0, 0), (0, 0), (0, 0), (0, 0)))[:, :-1]
        return jnp.concatenate([prev, t], axis=2)

    qb = split(q)
    kc = with_prev(split(k))
    vc = with_prev(split(v))

    s = jnp.einsum('bnqrhc,bnkrhc->bnrhqk', qb, kc) * (HEAD_DIM ** -0.5)
    rel = blk + jnp.arange(blk)[:, None] - jnp.arange(2 * blk)[None, :]
    band = (rel >= 0) & (rel <= blk)
    bucket = _t5_bucket(jnp.clip(rel, 0, blk) * dilation)
    bias = jnp.transpose(bias_table[bucket], (2, 0, 1))
    first = (jnp.arange(nb)[:, None, None] == 0) & (jnp.arange(2 * blk)[None, None, :] < blk)
    valid = band[None] & ~first
    logits = jnp.where(valid[None, :, None, None], s + bias[None, None, None], NEG_INF)

    m = jnp.max(logits, axis=-1)
    p = jnp.exp(logits - m[..., None])
    den = jnp.sum(p, axis=-1)
    num = jnp.einsum('bnrhqk,bnkrhc->bnqrhc', p, vc)

    num = num.reshape(B_, Sp, H, hd)[:, :S_]
    den = jnp.transpose(den, (0, 1, 4, 2, 3)).reshape(B_, Sp, H)[:, :S_]
    m = jnp.transpose(m, (0, 1, 4, 2, 3)).reshape(B_, Sp, H)[:, :S_]
    return num, den, m

def _dilated_attention_mixer(h, w_qkv, w_out, rel_bias):
    B_, S_, _ = h.shape
    qkv = (h @ w_qkv).astype(jnp.float32).reshape(B_, S_, 3, N_DIL_GROUPS, ATT_HEADS, HEAD_DIM)
    rb = rel_bias.astype(jnp.float32)
    nums, dens, maxs = [], [], []
    for g, (window, dil) in enumerate(WINDOW_DILATIONS):
        n_, d_, m_ = _dilated_group(qkv[:, :, 0, g], qkv[:, :, 1, g], qkv[:, :, 2, g],
                                    rb[:, g * ATT_HEADS:(g + 1) * ATT_HEADS], window, dil)
        nums.append(n_)
        dens.append(d_)
        maxs.append(m_)
    m_all = jnp.max(jnp.stack(maxs), axis=0)
    scales = [jnp.exp(m_ - m_all) for m_ in maxs]
    num_sum = sum(n_ * c[..., None] for n_, c in zip(nums, scales))
    den_sum = sum(d_ * c for d_, c in zip(dens, scales))
    o = (num_sum / den_sum[..., None]).astype(h.dtype).reshape(B_, S_, ATT_WIDTH)
    return o @ w_out

def second_inputs(seed: int = 0) -> dict:
    key = jax.random.key(seed)
    ks = jax.random.split(key, 16)
    f32 = jnp.float32
    nrm = lambda k, shape, s: jax.random.normal(k, shape, f32) * s
    qkv_cols = 3 * N_DIL_GROUPS * ATT_HEADS * HEAD_DIM
    return {
        "x": jax.random.normal(ks[0], (BATCH, SEQ, D_MODEL), f32),
        "mix_norm_g": 1.0 + nrm(ks[1], (DEPTH_2, D_MODEL), 0.05),
        "mlp_norm_g": 1.0 + nrm(ks[2], (DEPTH_2, D_MODEL), 0.05),
        "final_norm_g": 1.0 + nrm(ks[3], (D_MODEL,), 0.05),
        "a_w_in": nrm(ks[4], (N_A_LAYERS, D_MODEL, 2 * GATE_WIDTH), D_MODEL ** -0.5),
        "a_ln_g": 1.0 + nrm(ks[5], (N_A_LAYERS, GATE_WIDTH), 0.05),
        "a_ln_b": nrm(ks[6], (N_A_LAYERS, GATE_WIDTH), 0.02),
        "a_w_s": nrm(ks[7], (N_A_LAYERS, GATE_GROUPS, CHUNK, CHUNK), CHUNK ** -0.5),
        "a_b_s": 1.0 + nrm(ks[8], (N_A_LAYERS, GATE_GROUPS, CHUNK), 0.1),
        "a_w_out": nrm(ks[9], (N_A_LAYERS, GATE_WIDTH, D_MODEL), GATE_WIDTH ** -0.5),
        "b_w_qkv": nrm(ks[10], (N_B_LAYERS, D_MODEL, qkv_cols), D_MODEL ** -0.5),
        "b_w_out": nrm(ks[11], (N_B_LAYERS, ATT_WIDTH, D_MODEL), ATT_WIDTH ** -0.5),
        "rel_bias": nrm(ks[12], (N_BUCKETS, N_DIL_GROUPS * ATT_HEADS), 0.5),
        "w_up": nrm(ks[13], (DEPTH_2, D_MODEL, D_FF_2), D_MODEL ** -0.5),
        "w_down": nrm(ks[14], (DEPTH_2, D_FF_2, D_MODEL), D_FF_2 ** -0.5),
    }

def second_block(x, mix_norm_g, mlp_norm_g, final_norm_g, a_w_in, a_ln_g, a_ln_b, a_w_s, a_b_s,
              a_w_out, b_w_qkv, b_w_out, rel_bias, w_up, w_down):
    h = x
    for layer in range(DEPTH_2):
        y = _rms_norm(h, mix_norm_g[layer])
        j = layer // N_MIXERS
        if layer % N_MIXERS == 0:
            y = _chunk_gating_mixer(y, a_w_in[j], a_ln_g[j], a_ln_b[j], a_w_s[j], a_b_s[j], a_w_out[j])
        else:
            y = _dilated_attention_mixer(y, b_w_qkv[j], b_w_out[j], rel_bias)
        h = h + y
        y = _rms_norm(h, mlp_norm_g[layer])
        h = h + jnp.square(jax.nn.relu(y @ w_up[layer])) @ w_down[layer]
    return _rms_norm(h, final_norm_g)


def setup_inputs(seed=0):
    out = dict(first_inputs(seed))
    for name, value in second_inputs(seed + 1).items():
        if name != "x":
            out[name + "_2"] = value
    return out


def reference(
    x, norm_mix_g, w_in, b_gate, w_alpha_up, b_alpha, gla_norm_g, w_branch_sb, w_branch_gla,
    w_out, norm_ffn_g, w_ffn_in, conv_w, conv_b, w_ffn_out, norm_final_g, mix_norm_g_2,
    mlp_norm_g_2, final_norm_g_2, a_w_in_2, a_ln_g_2, a_ln_b_2, a_w_s_2, a_b_s_2, a_w_out_2,
    b_w_qkv_2, b_w_out_2, rel_bias_2, w_up_2, w_down_2,
):
    x = first_block(
        x, norm_mix_g, w_in, b_gate, w_alpha_up, b_alpha, gla_norm_g, w_branch_sb, w_branch_gla,
        w_out, norm_ffn_g, w_ffn_in, conv_w, conv_b, w_ffn_out, norm_final_g,
    )
    return second_block(
        x, mix_norm_g_2, mlp_norm_g_2, final_norm_g_2, a_w_in_2, a_ln_g_2, a_ln_b_2, a_w_s_2,
        a_b_s_2, a_w_out_2, b_w_qkv_2, b_w_out_2, rel_bias_2, w_up_2, w_down_2,
    )


_drawn_inputs = setup_inputs


def setup_inputs(seed=0):
    import zlib

    import numpy as np

    out = dict(_drawn_inputs(seed))
    spreads = {}
    factors = {'b_gate': 8.0,
     'b_alpha': 2.968,
     'gla_norm_g': 6.777,
     'norm_ffn_g': 3.176,
     'conv_b': 8.0,
     'a_ln_g_2': 2.889,
     'a_ln_b_2': 7.053}
    for name, (base, spread) in spreads.items():
        noise = np.random.default_rng([zlib.crc32(name.encode()), seed]).standard_normal(out[name].shape)
        drawn = base * np.exp(spread * noise) if base else spread * noise
        out[name] = __import__('jax').numpy.asarray(drawn.astype(out[name].dtype))
    for name, factor in factors.items():
        out[name] = (out[name] * factor).astype(out[name].dtype)
    return out
```

```python
import math
from contextlib import ExitStack

import numpy as np

import concourse.bass as bass
from concourse import mybir

F32 = mybir.dt.float32
F32R = mybir.dt.float32r
ALU = mybir.AluOpType
ACT = mybir.ActivationFunctionType
AX = mybir.AxisListType.X

P = 128
T = 512
D = 1024
KD = D // P
EPS = 1e-6
NT = T // P
FF = 2816
KF = FF // P
FF2 = 4096
SLOTS = 4
LOOK = SLOTS - 1
UT = 8
DH = 64
VG = 128
GCH = 64
TAU = 16.0
NEG = -1e30

OFF_Q, OFF_K, OFF_V = 0, 512, 1024
OFF_GQ, OFF_GK, OFF_GV, OFF_GR, OFF_GA = 1536, 1792, 2048, 2560, 3072
OFF_G0 = 3088
OFF_G1 = OFF_G0 + D

N_GLA, N_SB = 8, 32
STREAM = [("ga", 1), ("gla", N_GLA), ("sb", N_SB), ("branch", 8), ("wout", 8), ("ffin", 2 * KF), ("ffout", 3 * KD),
          ("cgv", 8), ("cgu", 8), ("cgout", 8),
          ("up00", 16), ("down00", 16), ("up01", 16), ("down01", 16),
          ("dil", 36), ("dilout", 4),
          ("up10", 16), ("down10", 16), ("up11", 16), ("down11", 16)]
U0 = {}
NU = 0
for _name, _n in STREAM:
    U0[_name] = NU
    NU += _n

A0 = {}
NA = 0
for _name, _n in [("ga", 1), ("gla", 8), ("sb", 32), ("branch", 16), ("wout", 8), ("ffin", 2 * KF), ("ffout", 8),
                  ("cgu", 8), ("cgout", 8), ("up00", 16), ("down00", 8), ("up01", 16), ("down01", 8),
                  ("dil", 36), ("dilout", 8), ("up10", 16), ("down10", 8), ("up11", 16), ("down11", 8)]:
    A0[_name] = NA
    NA += _n

X_SPLITS = ["wout", "final1", "cgout", "down01", "dilout"]
SQUARES = ["start", "wout", "ffout", "final1", "cgout", "down01", "dilout", "down11"]
X0 = {n: KD * (i + 1) for i, n in enumerate(X_SPLITS)}
S0 = {n: KD * i for i, n in enumerate(SQUARES)}
N0 = {n: i for i, n in enumerate(SQUARES)}

R0 = {}
_n = 0
for _name, _c in [("osb", 4), ("ogla", 4), ("y", 8), ("ffin", KF), ("cgv", 4), ("ug", 8), ("up00", 16), ("up01", 16),
                  ("dilo", 4), ("up10", 16), ("up11", 16)]:
    R0[_name] = _n
    _n += _c

G_MIX, G_FFN, G_FIN, G_MIX2, G_MLP2, G_FIN2, G_BG = 0, 1, 2, 3, 5, 7, 8
C_CONV = 80
C_BA = C_CONV + 4 * KF
C_GG = C_BA + 2
NP = C_GG + 4

CO = {0: 0, 1: 512, 3: 896, 2: 1024}
CW = 1280

LOGIT = 512
ROW = DH + 2


def at(base, i=None, step=0):
    return base if i is None else i * step + base


class Chain:

    def __init__(self, eng, sem):
        self.eng, self.sem, self.n, self.i, self.step = eng, sem, 0, None, 0

    def __call__(self, ins):
        self.n += 1
        ins.then_inc(self.sem, 1)
        self.eng.wait_ge(self.sem, at(self.n, self.i, self.step))

    def loop(self, i, step):
        self.i, self.step, self.first = i, step, self.n

    def end(self, turns):
        assert self.n == self.first + self.step, (self.n - self.first, self.step)
        self.n = self.first + self.step * turns
        self.i = None


def build(nc, wst, xT, prm, cst, wup, wsT, bs, lngb, rb, onehot, fdram, out):
    es = ExitStack()
    with es:
        def sb(name, shape, dt=F32, st=es):
            return st.enter_context(nc.sbuf_tensor(name, shape, dt))

        def sem(name):
            return es.enter_context(nc.semaphore(name))

        raw = sb("raw", [P, 2, UT * P])
        whi = sb("whi", [P, SLOTS, UT * P], F32R)
        wlo = sb("wlo", [P, SLOTS, UT * P], F32R)
        h = sb("h", [P, KD, T])
        xhi = sb("xhi", [P, KD, T], F32R)
        xlo = sb("xlo", [P, KD, T], F32R)
        par = sb("par", [P, NP])
        con = sb("con", [P, 4, P])
        ident, ones = con[:, 0, :], con[:, 3, :]
        trir = sb("trir", [P, 2, P], F32R)
        rbc = sb("rbc", [P, T])
        rtmp = sb("rtmp", [P, T])
        ssum = sb("ssum", [P, T])
        sq = sb("sq", [P, 2, T])
        eps = sb("eps", [P, 1])
        rtok = sb("rtok", [P, NT])
        PS = es.enter_context(nc.psum_tensor("ps", [P, 8 * T], F32))

        def bank(b, n=1):
            return PS[:, b * T:(b + n) * T]

        with ExitStack() as m1:
            o_gla = sb("o_gla", [P, 4, T], F32, m1)
            with ExitStack() as m:
                ga = sb("ga", [16, T], F32, m)
                wu = sb("wu", [16, 2 * P], F32, m)
                smask = sb("smask", [P, T], F32, m)
                gf = sb("gf", [P, 4, T], F32, m)
                gt = sb("gt", [P, 8, T], F32, m)
                gqk = sb("gqk", [P, 4, T], F32R, m)
                gtok = sb("gtok", [P, 6, T], F32R, m)
                gatt = sb("gatt", [P, 2, T], F32, m)
                gatr = sb("gatr", [P, 4, T], F32R, m)
                gst = sb("gst", [P, 8, P], F32, m)
                gstr = sb("gstr", [P, 2, 8, P], F32R, m)
            gate = sb("gate", [P, 2 * KD, T], F32, m1)
            o_sb = sb("o_sb", [P, 4, T], F32, m1)
            with ExitStack() as m:
                sqk = sb("sqk", [P, 4, T], F32R, m)
                svf = sb("svf", [P, T], F32, m)
                svp = sb("svp", [P, 2, 2, NT, P], F32R, m)
                sl = sb("sl", [P, CW], F32, m)
                ssp = sb("ssp", [P, 2, CW], F32, m)
                sspr = sb("sspr", [P, 2, 2, CW], F32R, m)
                sgr = sb("sgr", [P, 2, T], F32, m)
            with ExitStack() as m:
                yf = sb("yf", [P, 2, T], F32, m)
                yr = sb("yr", [P, 2, KD, T], F32R, m)
        with ExitStack() as m:
            hid = sb("hid", [P, 2, KF, T], F32R, m)
            apad = sb("apad", [P, T + 2], F32, m)
            cv = sb("cv", [P, 2, T], F32, m)
            gl = sb("gl", [P, 2, T], F32, m)
            gs = sb("gs", [P, T], F32, m)
        with ExitStack() as m:
            wsr = sb("wsr", [P, 2, KD, P], F32R, m)
            wsf = sb("wsf", [P, KD, P], F32, m)
            bsb = sb("bsb", [P, KD, P], F32, m)
            lgb = sb("lgb", [P, 2, D], F32, m)
            vt = sb("vt", [P, NT, D], F32, m)
            vr = sb("vr", [P, 2, NT, D], F32R, m)
            ugr = sb("ugr", [P, 2, KD, T], F32R, m)
            st6 = sb("st6", [P, NT, 2, 6], F32, m)
            mv = sb("mv", [P, NT, 4], F32, m)
            rtm = lgb[:, :, 0:T]
            uf = vt[:, :, :].rearrange("p t (a b) -> p (t a) b", b=T)
        with ExitStack() as m:
            mh = sb("mh", [P, 2, 16, T], F32R, m)
            mr = sb("mr", [P, 2, T], F32, m)
            ms = sb("ms", [P, 2, T], F32, m)
        with ExitStack() as m:
            bias = sb("bias", [P, 8, LOGIT], F32, m)
            oA = sb("oA", [P, NT, 8, ROW], F32, m)
            oB = sb("oB", [P, NT, 8, ROW], F32, m)
            oP = sb("oP", [P, NT, 8, ROW], F32, m)
            dqk = sb("dqk", [P, 3, 4, T], F32R, m)
            dvf = sb("dvf", [P, T], F32, m)
            dvt = sb("dvt", [P, 3, 2, T], F32R, m)
            dl = sb("dl", [P, 2, LOGIT], F32, m)
            dp = sb("dp", [P, 2, LOGIT], F32, m)
            dpt = sb("dpt", [P, 2, 2, LOGIT], F32R, m)
            mtmp = sb("mtmp", [P, 2, T], F32, m)
            fsb = dp[0:8, :, :].rearrange("p a b -> p (a b)")
            cAB = sb("cAB", [P, NT, 8, 4], F32, m)
            ohs = sb("ohs", [33, 24 + 4 * 256], F32, m)
            orr = dqk[:, :, :, :].rearrange("p a b c -> p (a b) c")

        def merged(t):
            return dl[:, t, :] if t < 2 else dp[:, t - 2, :]

        def hl(tile, k):
            return tile[:, 0, k, :], tile[:, 1, k, :]

        s_raw = [sem("raw0_loaded"), sem("raw1_loaded")]
        s_hi = sem("unit_hi_done")
        s_split = sem("unit_split_done")
        s_unit = sem("unit_multiplied")
        s_par = sem("params_loaded")
        s_h0 = sem("h_loaded")
        s_con = sem("constants_made")
        s_free = sem("acc_bank_free")
        s_xhi = sem("x_hi_done")
        s_x = sem("x_split_done")
        s_sqd = sem("square_done")
        s_ss = sem("square_summed")
        s_nmm = sem("mean_square_multiplied")
        s_nsq = sem("rms_done")
        s_rb = sem("inverse_rms_done")
        s_r = sem("operand_split_done")
        s_dch = sem("vector_chain")
        s_ach = sem("scalar_chain")
        s_pch = sem("pool_chain")
        s_gat = sem("gla_scores_copied")
        s_gpe = sem("gla_multiplied")
        s_gdv = sem("gla_vector_done")
        s_gac = sem("gla_scalar_done")
        s_gpo = sem("gla_masked")
        s_spe = sem("sb_multiplied")
        s_sdv = sem("sb_vector_done")
        s_sac = sem("sb_scalar_done")
        s_spo = sem("sb_masked")
        s_sig = sem("gate_sigmoid_done")
        s_cv = sem("conv_done")
        s_ge = sem("gelu_done")
        s_cpe = sem("chunk_gating_multiplied")
        s_cdv = sem("chunk_gating_vector_done")
        s_cac = sem("chunk_gating_gelu_done")
        s_cpo = sem("chunk_gating_masked")
        s_cld = sem("chunk_gating_params_loaded")
        s_ms = sem("relu_squared")
        s_dld = sem("bias_inputs_loaded")
        s_fst = sem("bias_rows_stored")
        s_bld = sem("bias_loaded")
        s_dpe = sem("dilated_multiplied")
        s_dtr = sem("dilated_transposed")
        s_dpv = sem("dilated_values_multiplied")
        s_ddv = sem("dilated_vector_done")
        s_dlg = sem("dilated_logits_done")
        s_dac = sem("dilated_exp_done")
        s_dhi = sem("dilated_probs_hi_done")
        s_dsp = sem("dilated_probs_split")
        s_perm = sem("dilated_rows_permuted")
        s_out = sem("out_stored")
        s_fin = sem("out_ready")

        block = es.enter_context(nc.Block())

        def sbank(x, n):
            return bank((2, 3, 4, 7)[2 * x + n % 2])[:, (n // 2) * P:(n // 2 + 1) * P]

        def mm3(pe, o, w, x, first, done, **kw):
            pe.matmul(o, w[0], x[0], start=first, stop=False, **kw)
            pe.matmul(o, w[1], x[0], start=False, stop=False, **kw)
            return pe.matmul(o, w[0], x[1], start=False, stop=done, **kw)

        @block.sync
        def _(sp):
            sp.dma_start(raw[:, 0, :], wst[0]).then_inc(s_raw[0], 16)
            sp.dma_start(raw[:, 1, :], wst[1]).then_inc(s_raw[1], 16)
            sp.wait_ge(s_split, 1)
            sp.dma_start(raw[:, 0, :], wst[2]).then_inc(s_raw[0], 16)
            with sp.Fori(0, (NU - 3) // 2, 1) as i:
                for j in range(2):
                    n = 3 + j
                    sp.wait_ge(s_split, at(n - 1, i, 2))
                    sp.dma_start(raw[:, n % 2, :], wst[2 * i + n]).then_inc(s_raw[n % 2], 16)
            for m in range(KD):
                sp.wait_ge(s_fin, m + 1)
                sp.dma_start(out[m], h[:, m, :]).then_inc(s_out, 16)
            sp.wait_ge(s_out, 16 * KD)

        @block.tensor
        def _(pe):
            def unit_ready(u, i=None, s=0):
                pe.wait_ge(s_split, at(u + 1, i, s))

            def w_tile(slot, t, n=P):
                return whi[:, slot, t * P:t * P + n], wlo[:, slot, t * P:t * P + n]

            def acc_wait(a, i=None, s=0):
                if a >= 2:
                    pe.wait_ge(s_free, at(a - 1, i, s))

            def x_tile(k):
                return xhi[:, k, :], xlo[:, k, :]

            def dense(u, a, groups, xs, i=None, us=0, as_=0):
                flat = [(g, t) for g, ts in enumerate(groups) for t in ts]
                for n, (g, (j, t, k)) in enumerate(flat):
                    if n == 0 or flat[n - 1][1][0] != j:
                        unit_ready(u + j, i, us)
                    first = n == 0 or flat[n - 1][0] != g
                    end = n + 1 == len(flat) or flat[n + 1][0] != g
                    if first:
                        acc_wait(a + g, i, as_)
                    ins = mm3(pe, bank((a + g) % 2), w_tile((u + j) % SLOTS, t), xs(k), first, end)
                    if n + 1 == len(flat) or flat[n + 1][1][0] != j:
                        ins.then_inc(s_unit, 1)

            def full(n_units):
                return [[(j, k, k) for k in range(UT)] for j in range(n_units)]

            def loop(name, turns, nu, groups, xs):
                u, a, g = U0[name], A0[name], len(groups)
                assert nu % SLOTS == 0 and g % 2 == 0
                with pe.Fori(0, turns, 1) as i:
                    dense(u, a, groups, xs, i, nu, g)

            def norm(name):
                pe.wait_ge(s_ss, S0[name] + KD)
                pe.matmul(bank(7), ones, ssum[:, :], start=True, stop=True).then_inc(s_nmm, 1)

            pe.wait_ge(s_con, 2)
            pe.wait_ge(s_par, 64)
            norm("start")
            pe.wait_ge(s_x, KD)
            dense(U0["ga"], A0["ga"], full(1), x_tile)
            for p in range(2):
                dense(U0["gla"] + 4 * p, A0["gla"] + 4 * p, full(4), x_tile)
                V = 1 + 13 * p
                pe.wait_ge(s_gdv, V)
                pe.matmul(bank(7), wu[:, p * P:(p + 1) * P], ga[:, :], start=True, stop=True).then_inc(s_gpe, 1)
                pe.wait_ge(s_gdv, V + 3)
                for n, src in enumerate((gt[:, 7, :], gf[:, 2, :], gf[:, 3, :])):
                    for t in range(NT):
                        ins = pe.transpose(bank(2 + n)[:, t * P:(t + 1) * P], src[:, t * P:(t + 1) * P], ident)
                    ins.then_inc(s_gpe, 1)
                for x in range(2):
                    r = slice(64 * x, 64 * x + 64)
                    for t in range(NT):
                        c = slice(t * P, (t + 1) * P)
                        ins = mm3(pe, bank(5 + x)[:, c], (gqk[r, 2, c], gqk[r, 3, c]), (gqk[r, 0, c], gqk[r, 1, c]),
                                  t == 0, True, skip_group_check=True)
                    ins.then_inc(s_gpe, 1)
                pe.wait_ge(s_gdv, V + 6)
                for x in range(2):
                    for n in range(7):
                        r = slice(64 * (n % 2), 64 * (n % 2) + 64)
                        c = slice((n // 2) * P, (n // 2 + 1) * P)
                        ins = mm3(pe, sbank(x, n),
                                  (gtok[r, 0, c], gtok[r, 1, c]), (gtok[r, 2 + 2 * x, c], gtok[r, 3 + 2 * x, c]),
                                  n < 2, True, skip_group_check=True)
                    ins.then_inc(s_gpe, 1)
                pe.wait_ge(s_gdv, V + 9)
                for x in range(2):
                    r = slice(64 * x, 64 * x + 64)
                    for t in range(NT):
                        c = slice(t * P, (t + 1) * P)
                        mm3(pe, bank(5 + x)[:, c], (gtok[:, 2 + 2 * x, c], gtok[:, 3 + 2 * x, c]),
                            (gatr[:, 2 * x, c], gatr[:, 2 * x + 1, c]), t == 0, True, skip_group_check=True)
                    for n in range(1, 8):
                        c = slice(n * GCH, (n + 1) * GCH)
                        ins = mm3(pe, bank(5 + x)[:, c], (gstr[r, 0, n, :], gstr[r, 1, n, :]),
                                  (gqk[r, 0, c], gqk[r, 1, c]), False, True, skip_group_check=True)
                    ins.then_inc(s_gpe, 1)
                for x in range(2):
                    pe.wait_ge(s_gdv, V + 10 + x)
                    pe.matmul(bank(2 + x), ones, gatt[:, x, :], start=True, stop=True).then_inc(s_gpe, 1)
            pe.wait_ge(s_gdv, 27)
            for p in range(4):
                u, a = U0["sb"] + 8 * p, A0["sb"] + 8 * p
                V, A = 10 * p, 5 * p

                def units(j, n=1):
                    dense(u + j, a + j, full(n), x_tile)

                def scores(x):
                    r = slice(64 * x, 64 * x + 64)
                    z = bank(2 + 3 * x, 3)
                    for c in (0, 1, 3, 2):
                        ins = mm3(pe, z[:, CO[c]:CO[c] + T - P * c], (sqk[r, 2, c * P:(c + 1) * P], sqk[r, 3, c * P:(c + 1) * P]),
                                  (sqk[r, 0, c * P:], sqk[r, 1, c * P:]), c != 3, True, skip_group_check=True)
                    ins.then_inc(s_spe, 1)

                def tails(x):
                    z = bank(2 + 3 * x, 3)
                    for c in range(NT):
                        for d in range(c, NT):
                            o = z[:, CO[c] + P * (d - c):CO[c] + T - P * c]
                            w = trir[:, 0 if d == c else 1, :]
                            for part in range(2):
                                ins = pe.matmul(o, w, sspr[:, part, x, CO[d]:CO[d] + T - P * d], start=False,
                                                stop=True, skip_group_check=True)
                    ins.then_inc(s_spe, 1)

                units(0, 4)
                if p:
                    pe.wait_ge(s_sac, A)
                pe.wait_ge(s_free, a + 3)
                for c in range(NT):
                    ins = pe.transpose(bank(5)[:, c * P:(c + 1) * P], svf[:, c * P:(c + 1) * P], ident)
                ins.then_inc(s_spe, 1)
                pe.wait_ge(s_sdv, V + 2)
                scores(0)
                units(4)
                pe.wait_ge(s_sdv, V + 3)
                scores(1)
                units(5)
                pe.wait_ge(s_sdv, V + 5)
                tails(0)
                units(6)
                pe.wait_ge(s_sdv, V + 7)
                tails(1)
                units(7)
                pe.wait_ge(s_sdv, V + 9)
                for x in range(2):
                    for c in range(NT):
                        ins = mm3(pe, bank(2)[:, c * P:], (svp[:, 0, x, c, :], svp[:, 1, x, c, :]),
                                  (sspr[:, 0, x, CO[c]:CO[c] + T - P * c], sspr[:, 1, x, CO[c]:CO[c] + T - P * c]),
                                  x == 0 and c == 0, True, skip_group_check=True)
                ins.then_inc(s_spe, 1)
            pe.wait_ge(s_r, R0["y"])
            two = [[(0, 4 * m + k, k) for k in range(4)] for m in range(2)]
            u, a = U0["branch"], A0["branch"]
            for j in range(4):
                dense(u + 2 * j, a + 4 * j, two, x_tile)
                dense(u + 2 * j + 1, a + 4 * j + 2, two, lambda k: x_tile(4 + k))
            pe.wait_ge(s_r, R0["ffin"])
            loop("wout", 2, 4, full(4), lambda k: hl(yr, k))
            norm("wout")
            pe.wait_ge(s_x, X0["wout"] + KD)
            loop("ffin", KF // 2, 4, full(4), x_tile)
            pe.wait_ge(s_r, R0["cgv"])
            down = [[(3 * m + k // UT, k % UT, k) for k in range(KF)] for m in range(4)]
            loop("ffout", 2, 12, down, lambda k: hl(hid, k))
            norm("ffout")
            norm("final1")
            pe.wait_ge(s_rb, N0["final1"] + 1)
            for t in range(NT):
                ins = pe.transpose(bank(2 + t)[:, 0:P], rbc[:, t * P:(t + 1) * P], ident)
            ins.then_inc(s_cpe, 1)
            pe.wait_ge(s_x, X0["final1"] + KD)
            pe.wait_ge(s_cdv, 1)
            for f in range(2):
                for j in range(4):
                    u = U0["cgv"] + 4 * f + j
                    unit_ready(u)
                    for kk in range(2):
                        k = 2 * j + kk
                        for t in range(NT):
                            if f and k == 0:
                                pe.wait_ge(s_cac, t + 1)
                            c = slice(t * P, (t + 1) * P)
                            ins = mm3(pe, bank(2 + t), (xhi[:, k, c], xlo[:, k, c]),
                                      (whi[:, u % SLOTS, kk * T:(kk + 1) * T], wlo[:, u % SLOTS, kk * T:(kk + 1) * T]),
                                      k == 0, k == KD - 1)
                    ins.then_inc(s_unit, 1)
            loop("cgu", 2, 4, full(4), x_tile)
            pe.wait_ge(s_r, R0["ug"])
            pe.wait_ge(s_cdv, 2)
            for g in range(KD):
                if g >= 4:
                    pe.wait_ge(s_cdv, g)
                for t in range(NT):
                    ins = mm3(pe, bank(2 + g % 4)[:, t * P:(t + 1) * P], (vr[:, 0, t, g * P:(g + 1) * P], vr[:, 1, t, g * P:(g + 1) * P]),
                              (wsr[:, 0, g, :], wsr[:, 1, g, :]), t == 0, True, skip_group_check=True)
                ins.then_inc(s_cpe, 1)
            pe.wait_ge(s_r, R0["up00"])
            loop("cgout", 2, 4, full(4), lambda k: hl(ugr, k))
            norm("cgout")

            def mlp(layer, before):
                pe.wait_ge(s_x, X0[before] + KD)
                m_t = lambda k: hl(mh, k)
                for half in range(2):
                    loop(f"up{layer}{half}", 4, 4, full(4), x_tile)
                    pe.wait_ge(s_r, R0[f"up{layer}{half}"] + 16)
                    groups = [[(2 * m + k // UT, k % UT, k) for k in range(16)] for m in range(4)]
                    loop(f"down{layer}{half}", 2, 8, groups, m_t)
                norm("down01" if layer == 0 else "down11")

            mlp(0, "cgout")
            pe.wait_ge(s_dld, 32)
            pe.wait_ge(s_ddv, 1)
            for g in range(4):
                grp = max(0, g - 1)
                ins = pe.matmul(bank(2 + g // 2)[0:8, (g % 2) * 256:(g % 2) * 256 + 256], ohs[:, 8 * grp:8 * grp + 8],
                                ohs[:, 24 + g * 256:24 + (g + 1) * 256], start=g % 2 == 0, stop=True, skip_group_check=True)
            ins.then_inc(s_dpe, 1)
            pe.wait_ge(s_x, X0["down01"] + KD)
            for p in range(4):
                D = 2 + 5 * p
                for g in range(3):
                    dense(U0["dil"] + 9 * p + 3 * g, A0["dil"] + 9 * p + 3 * g, full(3), x_tile)
                    pe.wait_ge(s_free, A0["dil"] + 9 * p + 3 * g + 3)
                    pe.wait_ge(s_ddv, D + g)
                    for t in range(NT):
                        src = dvf[:, t * P:(t + 1) * P] if g == 0 else dvf[:, t::4]
                        ins = pe.transpose(bank(7)[:, t * P:(t + 1) * P], src, ident)
                    ins.then_inc(s_dpe, 1)
                pe.wait_ge(s_ddv, D + 3)
                steps = [(x, t) for x in range(2) for t in range(NT)]

                def logits(n):
                    x, t = steps[n]
                    r = slice(64 * x, 64 * x + 64)
                    b = bank(2 + n % 2)
                    if n >= 2:
                        pe.wait_ge(s_dlg, 8 * p + n - 1)
                    c = slice(T - (t + 1) * P, T - t * P)
                    lo = (t - 1) * P if t else 0
                    o = b[:, 0:256] if t else b[:, 128:256]
                    mm3(pe, o, (dqk[r, 0, 0, c], dqk[r, 0, 1, c]), (dqk[r, 0, 2, lo:(t + 1) * P], dqk[r, 0, 3, lo:(t + 1) * P]),
                        True, True, skip_group_check=True)
                    for g in (1, 2):
                        ins = mm3(pe, b[:, 128 * (g + 1):128 * (g + 2)], (dqk[r, g, 0, 3 - t::4], dqk[r, g, 1, 3 - t::4]),
                                  (dqk[r, g, 2, t::4], dqk[r, g, 3, t::4]), False, True, skip_group_check=True)
                    ins.then_inc(s_dpe, 1)

                def values(n):
                    x, t = steps[n]
                    pe.wait_ge(s_dac, 2 * (8 * p + n + 1))
                    if 8 * p + n >= 2:
                        pe.wait_ge(s_dsp, 8 * p + n - 1)
                    tb = bank(4 + n % 2)
                    for j in range(0 if t else 1, 4):
                        ins = pe.transpose(tb[:, j * P:(j + 1) * P], dp[:, n % 2, j * P:(j + 1) * P], ident)
                    ins.then_inc(s_dtr, 1)

                def sums(n):
                    x, t = steps[n]
                    pe.wait_ge(s_dsp, 8 * p + n + 1)
                    if t == 0 and x:
                        pe.wait_ge(s_ddv, D + 4)
                    for j in range(0 if t else 1, 4):
                        g = max(0, j - 1)
                        kt = t - 1 if j == 0 else t
                        ins = mm3(pe, bank(6)[:, (2 * t + (j > 1)) * 64:(2 * t + (j > 1) + 1) * 64],
                                  (dpt[:, n % 2, 0, j * P:(j + 1) * P], dpt[:, n % 2, 1, j * P:(j + 1) * P]),
                                  (dvt[:, g, 0, kt * P + 64 * x:kt * P + 64 * x + 64], dvt[:, g, 1, kt * P + 64 * x:kt * P + 64 * x + 64]),
                                  t == 0 and j == 1, True, skip_group_check=True)
                    ins.then_inc(s_dpv, 1)

                for n in range(10):
                    if n < 8:
                        logits(n)
                    if 1 <= n < 9:
                        values(n - 1)
                    if n >= 2:
                        sums(n - 2)
            pe.wait_ge(s_ddv, 24)
            for j in range(4):
                for t in range(NT):
                    ins = pe.transpose(bank(2 + j)[:, t * P:(t + 1) * P], merged(t)[:, j * P:(j + 1) * P], ident)
                ins.then_inc(s_dpe, 1)
            pe.wait_ge(s_r, R0["up10"])
            dense(U0["dilout"], A0["dilout"], [[(j, 4 * m + k, k) for k in range(4)] for j in range(4) for m in range(2)],
                  lambda k: (orr[:, k, :], orr[:, 4 + k, :]))
            norm("dilout")
            mlp(1, "dilout")

        @block.scalar
        def _(act):
            chain = Chain(act, s_ach)

            def hi(u, i=None, s=0):
                n = u + LOOK
                if n >= NU:
                    return
                act.wait_ge(s_raw[n % 2], at(16 * (n // 2 + 1), i, 8 * s))
                if n >= SLOTS:
                    act.wait_ge(s_unit, at(n - SLOTS + 1, i, s))
                act.activation(whi[:, n % SLOTS, :], raw[:, n % 2, :], ACT.Copy).then_inc(s_hi, 1)

            def x_hi(m, xn, g, sn, i=None, s=0, mi=None):
                hm = h[:, m, :]
                if sn >= 2:
                    act.wait_ge(s_ss, at(sn - 1, i, s))
                if g is not None:
                    act.activation(xhi[:, m, :], hm, ACT.Copy, scale=par[:, 8 * g + m:8 * g + m + 1] if mi is None else
                                   par[:, bass.ds(mi + 8 * g, 1)]).then_inc(s_xhi, 1)
                elif i is not None:
                    act.wait_ge(s_h0, 16 * KD)
                act.activation(sq[:, sn % 2, :], hm, ACT.Square).then_inc(s_sqd, 1)

            def rms(name):
                act.wait_ge(s_nmm, N0[name] + 1)
                act.activation(rtmp[:, :], bank(7), ACT.Sqrt, bias=eps[:, 0:1], scale=1.0 / D).then_inc(s_nsq, 1)

            def residual(name, turns, nu, ng, g, first=0):
                u, a, sn = U0[name], A0[name], S0[first]
                step = nu // ng if nu >= ng else 1
                with act.Fori(0, turns, 1) as i:
                    for m in range(ng):
                        for j in range(m * step, (m + 1) * step):
                            hi(u + j, i, nu)
                        act.wait_ge(s_free, at(a + m + 1, i, ng))
                        x_hi(i * ng + m, None, g, sn + m, i, ng, i * ng + m)
                rms(first)

            act.dma_start(par[:, :], prm).then_inc(s_par, 16)
            act.dma_start(con[:, :, :], cst[:, 0:4 * P].rearrange("p (a b) -> p a b", a=4)).then_inc(s_par, 16)
            for m in range(KD):
                act.dma_start(h[:, m, :], xT[m]).then_inc(s_h0, 16)
            act.dma_start(wu[:, :], wup).then_inc(s_par, 16)
            act.dma_start(smask[:, :], cst[:, 4 * P:4 * P + T]).then_inc(s_par, 16)
            act.wait_ge(s_par, 64)
            act.wait_ge(s_h0, 16 * KD)
            act.wait_ge(s_con, 2)
            for m in range(KD):
                x_hi(m, None, G_MIX, m)
                if m < LOOK:
                    hi(m - LOOK)
            rms("start")
            hi(0)
            for p in range(2):
                for j in range(4):
                    hi(U0["gla"] + 4 * p + j)
                V, E = 1 + 13 * p, 12 * p
                ba = par[:, C_BA + p:C_BA + p + 1]
                act.wait_ge(s_gpe, E + 1)
                if p:
                    act.wait_ge(s_gdv, V)
                chain(act.activation(gt[:, 1, :], bank(7), ACT.Abs, bias=ba))
                chain(act.activation(gt[:, 1, :], gt[:, 1, :], ACT.Exp, scale=-1.0))
                act.activation(gt[:, 1, :], gt[:, 1, :], ACT.Ln, bias=1.0).then_inc(s_gac, 1)
                act.wait_ge(s_gdv, V + 2)
                act.activation(gt[:, 4, :], gt[:, 2, :], ACT.Exp, scale=1 / TAU)
                act.activation(gt[:, 5, :], gt[:, 2, :], ACT.Exp, scale=-1 / TAU)
                act.activation(gt[:, 6, :], gt[:, 3, :], ACT.Exp, scale=1 / TAU).then_inc(s_gac, 1)
                for x in range(2):
                    act.wait_ge(s_gpe, E + 11 + x)
                    act.activation(gt[:, x, :], bank(2 + x), ACT.Sqrt, bias=eps[:, 0:1], scale=1.0 / VG).then_inc(s_gac, 1)
            for p in range(4):
                u = U0["sb"] + 8 * p
                V, E = 10 * p, 6 * p
                for j in range(4):
                    hi(u + j)

                def softplus(x):
                    act.wait_ge(s_spe, E + 2 + x)
                    if p or x:
                        act.wait_ge(s_sdv, V + 4 if x else V)
                    z = bank(2 + 3 * x, 3)[:, 0:CW]
                    chain(act.activation(sl[:, :], z, ACT.Abs))
                    chain(act.activation(sl[:, :], sl[:, :], ACT.Exp, scale=-1.0))
                    act.activation(sl[:, :], sl[:, :], ACT.Ln, bias=1.0).then_inc(s_sac, 1)

                def weights(x):
                    act.wait_ge(s_spe, E + 4 + x)
                    act.activation(ssp[:, x, :], bank(2 + 3 * x, 3)[:, 0:CW], ACT.Exp).then_inc(s_sac, 1)

                softplus(0)
                hi(u + 4)
                softplus(1)
                hi(u + 5)
                weights(0)
                hi(u + 6)
                weights(1)
                hi(u + 7)
                act.wait_ge(s_free, A0["sb"] + 8 * p + 8)
                act.activation(sgr[:, 1, :], sgr[:, 0, :], ACT.Exp, scale=-1.0).then_inc(s_sac, 1)
            act.wait_ge(s_free, A0["branch"])
            for j in range(4):
                for b in range(2):
                    hi(U0["branch"] + 2 * j + b)
                    for m in range(2):
                        f = 2 * j + m
                        act.activation(gate[:, KD * b + f, :], gate[:, KD * b + f, :], ACT.Sigmoid,
                                       bias=par[:, 8 * (G_BG + b) + f:8 * (G_BG + b) + f + 1]).then_inc(s_sig, 1)
            residual("wout", 2, 4, 4, G_FFN, "wout")
            with act.Fori(0, KF // 2, 1) as i:
                for m in range(2):
                    hi(U0["ffin"] + 2 * m, i, 4)
                    hi(U0["ffin"] + 2 * m + 1, i, 4)
                    act.wait_ge(s_cv, at(m + 1, i, 2))
                    act.activation(gl[:, m, :], cv[:, m, :], ACT.Gelu_apprx_tanh).then_inc(s_ge, 1)
            residual("ffout", 2, 12, 4, None, "ffout")
            act.dma_start(wsf[:, :, :], wsT).then_inc(s_cld, 16)
            act.dma_start(bsb[:, :, :], bs.partition_broadcast(P)).then_inc(s_cld, 16)
            act.dma_start(lgb[:, :, :], lngb.partition_broadcast(P)).then_inc(s_cld, 16)
            for m in range(KD):
                act.wait_ge(s_rb, N0["ffout"] + 1)
                act.wait_ge(s_cv, KF + m + 1)
                x_hi(m, None, G_MIX2, S0["final1"] + m)
            rms("final1")
            act.wait_ge(s_cdv, 1)
            for f in range(2):
                for j in range(4):
                    hi(U0["cgv"] + 4 * f + j)
                act.wait_ge(s_unit, U0["cgv"] + 4 * f + 4)
                for t in range(NT):
                    act.activation(vt[:, t, f * T:(f + 1) * T], bank(2 + t), ACT.Gelu, scale=rtok[:, t:t + 1]).then_inc(s_cac, 1)
            act.wait_ge(s_cdv, 3)
            for t in range(NT):
                act.activation(mv[:, t, 2:3], mv[:, t, 1:2], ACT.Sqrt, bias=eps[:, 0:1]).then_inc(s_cac, 1)
            with act.Fori(0, 2, 1) as i:
                for m in range(4):
                    hi(U0["cgu"] + m, i, 4)
                    act.wait_ge(s_free, at(A0["cgu"] + m + 1, i, 4))
                    act.activation(uf[:, i * 4 + m, :], uf[:, i * 4 + m, :], ACT.Gelu).then_inc(s_cac, 1)
            residual("cgout", 2, 4, 4, G_MLP2, "cgout")

            def mlp(layer, g):
                for half in range(2):
                    up, dn = f"up{layer}{half}", f"down{layer}{half}"
                    k0 = 32 * layer + 16 * half
                    with act.Fori(0, 4, 1) as i:
                        for m in range(4):
                            hi(U0[up] + m, i, 4)
                            act.wait_ge(s_free, at(A0[up] + m + 1, i, 4))
                            act.activation(ms[:, m % 2, :], mr[:, m % 2, :], ACT.Square).then_inc(s_ms, 1)
                    if half == 0:
                        with act.Fori(0, 2, 1) as i:
                            for m in range(8):
                                hi(U0[dn] + m, i, 8)
                    elif layer == 0:
                        residual(dn, 2, 8, 4, g, "down01")
                    else:
                        for m in range(KD):
                            hi(U0[dn] + 2 * m)
                            hi(U0[dn] + 2 * m + 1)
                            act.wait_ge(s_free, A0[dn] + m + 1)
                            x_hi(m, None, None, S0["down11"] + m)
                        rms("down11")

            mlp(0, G_MIX2 + 1)
            act.dma_start(ohs[0:32, 0:24], rb).then_inc(s_dld, 16)
            act.dma_start(ohs[:, 24:], onehot).then_inc(s_dld, 16)
            act.wait_ge(s_ddv, 2)
            act.dma_start(fdram, fsb).then_inc(s_fst, 16)
            act.wait_ge(s_fst, 16)
            for g in range(4):
                src = bass.AP(tensor=fdram.tensor, offset=256 * g, ap=[[1, P], [1024, 8], [1, P]])
                act.dma_start(bias[:, :, g * P:(g + 1) * P], src).then_inc(s_bld, 16)
            for p in range(4):
                for j in range(9):
                    hi(U0["dil"] + 9 * p + j)
                for n in range(9):
                    if n < 8:
                        x, t = n // NT, n % NT
                        act.wait_ge(s_dlg, 8 * p + n + 1)
                        if 8 * p + n >= 2:
                            act.wait_ge(s_dtr, 8 * p + n - 1)
                        hd = 2 * p + x
                        c0 = 0 if t else 128
                        act.activation(dp[:, n % 2, c0:256], dl[:, n % 2, c0:256], ACT.Exp, bias=oA[:, t, hd, DH + 1:DH + 2],
                                       accum_out=oA[:, t, hd, DH:DH + 1]).then_inc(s_dac, 1)
                        act.activation(dp[:, n % 2, 256:512], dl[:, n % 2, 256:512], ACT.Exp, bias=oB[:, t, hd, DH + 1:DH + 2],
                                       accum_out=oB[:, t, hd, DH:DH + 1]).then_inc(s_dac, 1)
                    if n >= 1:
                        k = n - 1
                        c0 = 0 if k % NT else 128
                        act.wait_ge(s_dtr, 8 * p + k + 1)
                        if 8 * p + k >= 2:
                            act.wait_ge(s_dpv, 8 * p + k - 1)
                        act.activation(dpt[:, k % 2, 0, c0:], bank(4 + k % 2)[:, c0:], ACT.Copy).then_inc(s_dhi, 1)
            act.wait_ge(s_ddv, 22)
            for r in range(4):
                for t in range(NT):
                    act.dma_start(oP[3 - r:P:4, t, :, :], oB[96 - 32 * t:P - 32 * t, r, :, :]).then_inc(s_perm, 16)
            act.wait_ge(s_ddv, 23)
            act.activation(cAB[:, :, :, 1:3], cAB[:, :, :, 1:3], ACT.Exp).then_inc(s_dac, 1)
            u, a = U0["dilout"], A0["dilout"]
            for m in range(KD):
                if m % 2 == 0:
                    hi(u + m // 2)
                act.wait_ge(s_free, a + m + 1)
                x_hi(m, None, G_MLP2 + 1, S0["dilout"] + m)
            rms("dilout")
            mlp(1, None)

        @block.vector
        def _(dve):
            chain = Chain(dve, s_dch)

            def lo(u, i=None, s=0):
                n = u + LOOK
                if n >= NU:
                    return
                dve.wait_ge(s_hi, at(n + 1, i, s))
                dve.tensor_tensor(wlo[:, n % SLOTS, :], raw[:, n % 2, :], whi[:, n % SLOTS, :].bitcast(F32),
                                  ALU.subtract).then_inc(s_split, 1)

            def x_lo(m, xn, g, i=None, s=0, mi=None):
                dve.wait_ge(s_xhi, at(xn + 1, i, s))
                gain = par[:, 8 * g + m:8 * g + m + 1] if mi is None else par[:, bass.ds(mi + 8 * g, 1)]
                dve.scalar_tensor_tensor(xlo[:, m, :], h[:, m, :], gain, xhi[:, m, :].bitcast(F32), ALU.mult,
                                         ALU.subtract).then_inc(s_x, 1)

            def inverse_rms(name):
                dve.wait_ge(s_nsq, N0[name] + 1)
                dve.reciprocal(rbc[:, :], rtmp[:, :]).then_inc(s_rb, 1)
                dve.wait_ge(s_rb, N0[name] + 1)

            def split(hi_, lo_, src, sem_=None):
                chain(dve.tensor_copy(hi_, src))
                ins = dve.tensor_tensor(lo_, src, hi_.bitcast(F32), ALU.subtract)
                if sem_ is None:
                    chain(ins)
                else:
                    ins.then_inc(sem_, 1)

            def residual(name, turns, nu, ng, g):
                u, a = U0[name], A0[name]
                step = nu // ng
                with dve.Fori(0, turns, 1) as i:
                    for m in range(ng):
                        for j in range(m * step, (m + 1) * step):
                            lo(u + j, i, nu)
                        dve.wait_ge(s_unit, at(u + (m + 1) * step, i, nu))
                        hm = h[:, i * ng + m, :]
                        dve.tensor_tensor(hm, hm, bank((a + m) % 2), ALU.add).then_inc(s_free, 1)
                        if g is not None:
                            x_lo(i * ng + m, X0[name] + m, g, i, ng, i * ng + m)

            def rows(u, a, dst, mul=rbc, op0=None, i=None, us=0):
                dve.wait_ge(s_unit, at(u + 1, i, us))
                dve.tensor_tensor(dst, bank(a % 2), mul[:, :], ALU.mult).then_inc(s_free, 1)

            dve.wait_ge(s_par, 64)
            dve.tensor_copy(trir[:, :, :], con[:, 1:3, :]).then_inc(s_con, 1)
            dve.wait_ge(s_h0, 16 * KD)
            for m in range(KD):
                x_lo(m, m, G_MIX)
                if m < LOOK:
                    lo(m - LOOK)
            inverse_rms("start")
            lo(0)
            rows(U0["ga"], A0["ga"], gt[:, 0, :])
            dve.wait_ge(s_free, 1)
            dve.tensor_copy(ga[:, :], gt[0:16, 0, :]).then_inc(s_gdv, 1)
            for p in range(2):
                V, E = 1 + 13 * p, 12 * p
                for j in range(4):
                    u = U0["gla"] + 4 * p + j
                    lo(u)
                    rows(u, A0["gla"] + 4 * p + j, gf[:, j, :])
                ba = par[:, C_BA + p:C_BA + p + 1]
                dve.wait_ge(s_gac, 4 * p + 1)
                chain(dve.tensor_scalar(gt[:, 0, :], bank(7), ba, 0.0, ALU.add, ALU.min))
                chain(dve.tensor_tensor(gt[:, 0, :], gt[:, 0, :], gt[:, 1, :], ALU.subtract))
                cum = gt[:, 2, :]
                dve.tensor_tensor_scan(cum, smask[:, :], gt[:, 0, :], 0.0, ALU.mult, ALU.add).then_inc(s_gdv, 1)
                dve.wait_ge(s_gdv, V + 1)
                c3 = cum.rearrange("p (n c) -> p n c", c=GCH)
                lastc = c3[:, :, GCH - 1:GCH].to_broadcast([P, 8, GCH])
                dve.tensor_tensor(gt[:, 3, :].rearrange("p (n c) -> p n c", c=GCH), lastc, c3, ALU.subtract).then_inc(s_gdv, 1)
                dve.wait_ge(s_gac, 4 * p + 2)
                dve.wait_ge(s_free, A0["gla"] + 4 * p + 4)
                chain(dve.scalar_tensor_tensor(gt[:, 0, :], gf[:, 0, :], DH ** -0.5, gt[:, 4, :], ALU.mult, ALU.mult))
                split(gqk[:, 0, :], gqk[:, 1, :], gt[:, 0, :])
                chain(dve.tensor_tensor(gt[:, 1, :], gf[:, 1, :], gt[:, 5, :], ALU.mult))
                split(gqk[:, 2, :], gqk[:, 3, :], gt[:, 1, :])
                dve.tensor_tensor(gt[:, 7, :], gf[:, 1, :], gt[:, 6, :], ALU.mult).then_inc(s_gdv, 1)
                for n in range(3):
                    dve.wait_ge(s_gpe, E + 2 + n)
                    split(gtok[:, 2 * n, :], gtok[:, 2 * n + 1, :], bank(2 + n), s_gdv)
                for x in range(2):
                    dve.wait_ge(s_gpe, E + 5 + x)
                    dve.tensor_copy(gatt[:, x, :], bank(5 + x)).then_inc(s_gat, 1)
                for x in range(2):
                    r = slice(64 * x, 64 * x + 64)
                    dve.wait_ge(s_gpe, E + 7 + x)
                    for n in range(1, 8):
                        ds = sbank(x, n - 1)[r, :]
                        if n == 1:
                            chain(dve.tensor_copy(gst[r, 1, :], ds))
                        else:
                            chain(dve.scalar_tensor_tensor(gst[r, n, :], gst[r, n - 1, :], gt[r, 4, n * GCH - 1:n * GCH], ds,
                                                           ALU.mult, ALU.add))
                split(gstr[:, 0, 1:8, :], gstr[:, 1, 1:8, :], gst[:, 1:8, :], s_gdv)
                for x in range(2):
                    dve.wait_ge(s_gpo, 2 * p + x + 1)
                    split(gatr[:, 2 * x, :], gatr[:, 2 * x + 1, :], gatt[:, x, :], s_gdv)
                for x in range(2):
                    dve.wait_ge(s_gpe, E + 9 + x)
                    o = o_gla[:, 2 * p + x, :]
                    chain(dve.tensor_copy(o, bank(5 + x)))
                    dve.tensor_tensor(gatt[:, x, :], o, o, ALU.mult).then_inc(s_gdv, 1)
                for x in range(2):
                    dve.wait_ge(s_gac, 4 * p + 3 + x)
                    o = o_gla[:, 2 * p + x, :]
                    chain(dve.reciprocal(gt[:, x, :], gt[:, x, :]))
                    gg = par[:, C_GG + 2 * p + x:C_GG + 2 * p + x + 1]
                    dve.scalar_tensor_tensor(o, o, gg, gt[:, x, :], ALU.mult, ALU.mult).then_inc(s_gdv, 1)
            chain(dve.memset(svp[:, :, :, :, :].bitcast(F32), 0.0))
            for p in range(4):
                u, a = U0["sb"] + 8 * p, A0["sb"] + 8 * p
                V, E, A = 10 * p, 6 * p, 5 * p

                def gates(j):
                    lo(u + j)
                    f = 4 * p + j - 3
                    rows(u + j, a + j, gate[:, f, :])

                for j in range(2):
                    lo(u + j)
                    dve.wait_ge(s_unit, u + j + 1)
                    dst = ssp[:, j, 0:T]
                    dve.scalar_tensor_tensor(dst, bank((a + j) % 2), DH ** -0.5 if j == 0 else 1.0, rbc[:, :], ALU.mult,
                                             ALU.mult).then_inc(s_free, 1)
                    dve.wait_ge(s_free, a + j + 1)
                    split(sqk[:, 2 * j, :], sqk[:, 2 * j + 1, :], dst, s_sdv)
                lo(u + 2)
                rows(u + 2, a + 2, svf[:, :])
                gates(3)
                dve.wait_ge(s_spe, E + 1)
                vv = bank(5).rearrange("p (c d) -> p c d", d=P)
                for x in range(2):
                    d = slice(64 * x, 64 * x + 64)
                    chain(dve.tensor_copy(svp[:, 0, x, :, d], vv[:, :, d]))
                    ins = dve.tensor_tensor(svp[:, 1, x, :, d], vv[:, :, d], svp[:, 0, x, :, d].bitcast(F32), ALU.subtract)
                    if x:
                        ins.then_inc(s_sdv, 1)
                    else:
                        chain(ins)

                def softplus(x):
                    dve.wait_ge(s_sac, A + 1 + x)
                    dve.scalar_tensor_tensor(ssp[:, x, :], bank(2 + 3 * x, 3)[:, 0:CW], 0.0, sl[:, :], ALU.max,
                                             ALU.add).then_inc(s_sdv, 1)
                    dve.wait_ge(s_spo, 4 * p + 1 + x)
                    split(sspr[:, 0, x, :], sspr[:, 1, x, :], ssp[:, x, :], s_sdv)

                softplus(0)
                gates(4)
                softplus(1)
                gates(5)
                dve.wait_ge(s_spo, 4 * p + 3)
                split(sspr[:, 0, 0, :], sspr[:, 1, 0, :], ssp[:, 0, :], s_sdv)
                gates(6)
                dve.wait_ge(s_spo, 4 * p + 4)
                split(sspr[:, 0, 1, :], sspr[:, 1, 1, :], ssp[:, 1, :], s_sdv)
                lo(u + 7)
                rows(u + 7, a + 7, sgr[:, 0, :])
                dve.wait_ge(s_sac, A + 5)
                chain(dve.tensor_scalar(sgr[:, 1, :], sgr[:, 1, :], 1.0, None, ALU.add))
                chain(dve.reciprocal(sgr[:, 1, :], sgr[:, 1, :]))
                chain(dve.tensor_tensor(sgr[:, 1, :], sgr[:, 1, :], sgr[:, 0, :], ALU.mult))
                chain(dve.tensor_tensor(o_gla[:, p, :], o_gla[:, p, :], sgr[:, 1, :], ALU.mult))
                dve.wait_ge(s_spe, E + 6)
                dve.tensor_copy(o_sb[:, p, :], bank(2)).then_inc(s_sdv, 1)
            dve.wait_ge(s_sdv, 40)
            dve.wait_ge(s_unit, U0["branch"])
            for k in range(8):
                src = o_sb[:, k, :] if k < 4 else o_gla[:, k - 4, :]
                split(xhi[:, k, :], xlo[:, k, :], src, s_r)
            for j in range(4):
                for b in range(2):
                    u = U0["branch"] + 2 * j + b
                    lo(u)
                    dve.wait_ge(s_unit, u + 1)
                    for m in range(2):
                        f, a = 2 * j + m, A0["branch"] + 4 * j + 2 * b + m
                        dve.wait_ge(s_sig, 4 * j + 2 * b + m + 1)
                        g = gate[:, KD * b + f, :]
                        dve.tensor_tensor(g, g, bank(a % 2), ALU.mult).then_inc(s_free, 1)
                        if b:
                            dve.wait_ge(s_free, a + 1)
                            chain(dve.tensor_tensor(yf[:, m, :], gate[:, f, :], g, ALU.add))
                            split(yr[:, 0, f, :], yr[:, 1, f, :], yf[:, m, :], s_r)
            residual("wout", 2, 4, 4, G_FFN)
            inverse_rms("wout")
            chain(dve.memset(apad[:, 0:2], 0.0))
            with dve.Fori(0, KF // 2, 1) as i:
                chain.loop(i, 2 * 4)
                for m in range(2):
                    u, a = U0["ffin"] + 2 * m, A0["ffin"] + 2 * m
                    tap = lambda k: par[:, bass.ds(i * 8 + (C_CONV + 4 * m + k), 1)]
                    lo(u, i, 4)
                    rows(u, a, apad[:, 2:], i=i, us=4)
                    dve.wait_ge(s_free, at(a + 1, i, 4))
                    t = cv[:, m, :]
                    chain(dve.tensor_scalar(t, apad[:, 2:], tap(2), tap(3), ALU.mult, ALU.add))
                    chain(dve.scalar_tensor_tensor(t, apad[:, 1:T + 1], tap(1), t, ALU.mult, ALU.add))
                    dve.scalar_tensor_tensor(t, apad[:, 0:T], tap(0), t, ALU.mult, ALU.add).then_inc(s_cv, 1)
                    lo(u + 1, i, 4)
                    rows(u + 1, a + 1, gs[:, :], i=i, us=4)
                    dve.wait_ge(s_ge, at(m + 1, i, 2))
                    dve.wait_ge(s_free, at(a + 2, i, 4))
                    chain(dve.tensor_tensor(gl[:, m, :], gl[:, m, :], gs[:, :], ALU.mult))
                    k = i * 2 + m
                    split(hid[:, 0, k, :], hid[:, 1, k, :], gl[:, m, :], s_r)
                chain.end(KF // 2)
            residual("ffout", 2, 12, 4, None)
            inverse_rms("ffout")
            dve.wait_ge(s_sqd, S0["final1"])
            for m in range(KD):
                dve.scalar_tensor_tensor(h[:, m, :], h[:, m, :], par[:, 8 * G_FIN + m:8 * G_FIN + m + 1], rbc[:, :],
                                         ALU.mult, ALU.mult).then_inc(s_cv, 1)
                if m:
                    dve.wait_ge(s_cv, KF + m)
                    x_lo(m - 1, X0["final1"] + m - 1, G_MIX2)
            dve.wait_ge(s_cv, KF + KD)
            x_lo(KD - 1, X0["final1"] + KD - 1, G_MIX2)
            inverse_rms("final1")
            dve.wait_ge(s_cpe, 1)
            for t in range(NT):
                ins = dve.tensor_copy(rtok[:, t:t + 1], bank(2 + t)[:, 0:1])
            ins.then_inc(s_cdv, 1)
            dve.wait_ge(s_cpo, 1)
            split(wsr[:, 0, :, :], wsr[:, 1, :, :], wsf[:, :, :], s_cdv)
            dve.wait_ge(s_cld, 48)
            for j in range(8):
                lo(U0["cgv"] + j)
                if j == 4 or j == 7:
                    pass
            for t in range(NT):
                for f in range(2):
                    dve.wait_ge(s_cac, NT * f + t + 1)
                    ins = dve.bn_stats(st6[:, t, f, :], vt[:, t, f * T:(f + 1) * T])
                    chain(ins)
                ins = dve.bn_aggr(mv[:, t, 0:2], st6[:, t, :, :].rearrange("p a b -> p (a b)"))
                if t < NT - 1:
                    chain(ins)
                else:
                    ins.then_inc(s_cdv, 1)
            for t in range(NT):
                dve.wait_ge(s_cac, 8 + t + 1)
                v = vt[:, t, :]
                chain(dve.reciprocal(mv[:, t, 3:4], mv[:, t, 2:3]))
                chain(dve.tensor_scalar(v, v, mv[:, t, 0:1], mv[:, t, 3:4], ALU.subtract, ALU.mult))
                chain(dve.tensor_tensor(v, v, lgb[:, 0, :], ALU.mult))
                chain(dve.tensor_tensor(v, v, lgb[:, 1, :], ALU.add))
                split(vr[:, 0, t, :], vr[:, 1, t, :], v, s_r)
            dve.wait_ge(s_r, R0["ug"])
            with dve.Fori(0, 2, 1) as i:
                for m in range(4):
                    lo(U0["cgu"] + m, i, 4)
                    rows(U0["cgu"] + m, A0["cgu"] + m, uf[:, i * 4 + m, :], i=i, us=4)
            for g in range(KD):
                dve.wait_ge(s_cpe, 2 + g)
                dve.wait_ge(s_cac, 12 + g + 1)
                b4 = bank(2 + g % 4).rearrange("p (t c) -> p t c", c=P)
                m4 = rtm[:, g % 2, :].rearrange("p (t c) -> p t c", c=P)
                row = bsb[:, g:g + 1, :].to_broadcast([P, NT, P])
                dve.tensor_tensor(m4, b4, row, ALU.add).then_inc(s_cdv, 1)
                dve.wait_ge(s_cdv, 4 + g)
                chain(dve.tensor_tensor(uf[:, g, :], uf[:, g, :], rtm[:, g % 2, :], ALU.mult))
                split(ugr[:, 0, g, :], ugr[:, 1, g, :], uf[:, g, :], s_r)
            residual("cgout", 2, 4, 4, G_MLP2)
            inverse_rms("cgout")

            def mlp(layer, g):
                for half in range(2):
                    up, dn = f"up{layer}{half}", f"down{layer}{half}"
                    k0 = 32 * layer + 16 * half
                    with dve.Fori(0, 4, 1) as i:
                        chain.loop(i, 4)
                        for m in range(4):
                            lo(U0[up] + m, i, 4)
                            dve.wait_ge(s_unit, at(U0[up] + m + 1, i, 4))
                            dve.scalar_tensor_tensor(mr[:, m % 2, :], bank((A0[up] + m) % 2), 0.0, rbc[:, :], ALU.max,
                                                     ALU.mult).then_inc(s_free, 1)
                            dve.wait_ge(s_ms, at(k0 + m + 1, i, 4))
                            k = i * 4 + m
                            split(mh[:, 0, k, :], mh[:, 1, k, :], ms[:, m % 2, :], s_r)
                        chain.end(4)
                    if half == 0:
                        residual(dn, 2, 8, 4, None)
                    elif layer == 0:
                        residual_x(dn, g, "down01")
                    else:
                        for m in range(KD):
                            lo(U0[dn] + 2 * m)
                            lo(U0[dn] + 2 * m + 1)
                            dve.wait_ge(s_unit, U0[dn] + 2 * m + 2)
                            hm = h[:, m, :]
                            dve.tensor_tensor(hm, hm, bank((A0[dn] + m) % 2), ALU.add).then_inc(s_free, 1)
                inverse_rms("down01" if layer == 0 else "down11")

            def residual_x(dn, g, name):
                residual(dn, 2, 8, 4, g)

            mlp(0, G_MIX2 + 1)
            dve.wait_ge(s_dld, 32)
            dve.memset(ohs[32:33, 0:24], NEG).then_inc(s_ddv, 1)
            dve.wait_ge(s_dpe, 1)
            dve.tensor_copy(fsb[:, :], bank(2, 2)[0:8, :]).then_inc(s_ddv, 1)
            for p in range(4):
                for g in range(3):
                    for j in range(3):
                        u, a = U0["dil"] + 9 * p + 3 * g + j, A0["dil"] + 9 * p + 3 * g + j
                        lo(u)
                        if j < 2:
                            dve.wait_ge(s_unit, u + 1)
                            dst = mtmp[:, j, :]
                            back = dst if j else dst[:, ::-1]
                            dve.scalar_tensor_tensor(back, bank(a % 2), DH ** -0.5 if j == 0 else 1.0, rbc[:, :], ALU.mult,
                                                     ALU.mult).then_inc(s_free, 1)
                            dve.wait_ge(s_free, a + 1)
                            split(dqk[:, g, 2 * j, :], dqk[:, g, 2 * j + 1, :], dst)
                        else:
                            rows(u, a, dvf[:, :])
                    dve.wait_ge(s_dpe, 1 + 11 * p + g + 1)
                    split(dvt[:, g, 0, :], dvt[:, g, 1, :], bank(7), s_ddv)
                if p == 0:
                    dve.wait_ge(s_bld, 64)
                for n in range(10):
                    if n < 8:
                        x, t = n // NT, n % NT
                        hd = 2 * p + x
                        c0 = 0 if t else 128
                        dve.wait_ge(s_dpe, 1 + 11 * p + 3 + n + 1)
                        if 8 * p + n >= 2:
                            dve.wait_ge(s_dac, 2 * (8 * p + n - 1))
                        chain(dve.tensor_tensor(dl[:, n % 2, c0:], bank(2 + n % 2)[:, c0:], bias[:, hd, c0:], ALU.add))
                        chain(dve.tensor_reduce(oA[:, t, hd, DH + 1:DH + 2], dl[:, n % 2, c0:256], AX, ALU.max, negate=True))
                        dve.tensor_reduce(oB[:, t, hd, DH + 1:DH + 2], dl[:, n % 2, 256:], AX, ALU.max, negate=True).then_inc(s_dlg, 1)
                    if 1 <= n < 9:
                        k = n - 1
                        c0 = 0 if k % NT else 128
                        dve.wait_ge(s_dhi, 8 * p + k + 1)
                        dve.tensor_tensor(dpt[:, k % 2, 1, c0:], bank(4 + k % 2)[:, c0:], dpt[:, k % 2, 0, c0:].bitcast(F32),
                                          ALU.subtract).then_inc(s_dsp, 1)
                    if n == 5 or n == 9:
                        x = n // 9
                        dve.wait_ge(s_dpv, 8 * p + 4 * x + 4)
                        o3 = bank(6).rearrange("p (t s d) -> p t s d", s=2, d=DH)
                        chain(dve.tensor_copy(oA[:, :, 2 * p + x, 0:DH], o3[:, :, 0, :]))
                        dve.tensor_copy(oB[:, :, 2 * p + x, 0:DH], o3[:, :, 1, :]).then_inc(s_ddv, 1)
            dve.wait_ge(s_perm, 256)
            nA, nB = oA[:, :, :, DH + 1:DH + 2], oP[:, :, :, DH + 1:DH + 2]
            chain(dve.tensor_tensor(cAB[:, :, :, 0:1], nA, nB, ALU.min))
            chain(dve.tensor_tensor(cAB[:, :, :, 1:2], cAB[:, :, :, 0:1], nA, ALU.subtract))
            dve.tensor_tensor(cAB[:, :, :, 2:3], cAB[:, :, :, 0:1], nB, ALU.subtract).then_inc(s_ddv, 1)
            dve.wait_ge(s_dac, 65)
            R = DH + 1
            for k, o in ((1, oA), (2, oP)):
                for t in range(NT):
                    chain(dve.tensor_tensor(o[:, t, :, 0:R], o[:, t, :, 0:R], cAB[:, t, :, k:k + 1].to_broadcast([P, 8, R]), ALU.mult))
            for t in range(NT):
                chain(dve.tensor_tensor(oA[:, t, :, 0:R], oA[:, t, :, 0:R], oP[:, t, :, 0:R], ALU.add))
            chain(dve.reciprocal(cAB[:, :, :, 3:4], oA[:, :, :, DH:DH + 1]))
            for t in range(NT):
                ins = dve.tensor_tensor(merged(t).rearrange("p (h d) -> p h d", d=DH), oA[:, t, :, 0:DH],
                                        cAB[:, t, :, 3:4].to_broadcast([P, 8, DH]), ALU.mult)
                if t < NT - 1:
                    chain(ins)
                else:
                    ins.then_inc(s_ddv, 1)
            for j in range(4):
                dve.wait_ge(s_dpe, 1 + 44 + j + 1)
                b3 = bank(2 + j).rearrange("p (t q) -> p t q", q=P)[:, :, ::-1]
                split(orr[:, j, :].rearrange("p (t q) -> p t q", q=P), orr[:, 4 + j, :].rearrange("p (t q) -> p t q", q=P), b3, s_r)
            for m in range(KD):
                u, a = U0["dilout"] + m // 2, A0["dilout"] + m
                if m % 2 == 0:
                    lo(u)
                    dve.wait_ge(s_unit, u + 1)
                dve.tensor_tensor(h[:, m, :], h[:, m, :], bank(a % 2), ALU.add).then_inc(s_free, 1)
                x_lo(m, X0["dilout"] + m, G_MLP2 + 1)
            inverse_rms("dilout")
            mlp(1, None)
            for m in range(KD):
                dve.scalar_tensor_tensor(h[:, m, :], h[:, m, :], par[:, 8 * G_FIN2 + m:8 * G_FIN2 + m + 1], rbc[:, :],
                                         ALU.mult, ALU.mult).then_inc(s_fin, 1)

        @block.gpsimd
        def _(pool):
            chain = Chain(pool, s_pch)

            def sum_squares(name):
                for m in range(KD):
                    n = S0[name] + m
                    pool.wait_ge(s_sqd, n + 1)
                    if m == 0:
                        ins = pool.tensor_copy(ssum[:, :], sq[:, 0, :])
                    else:
                        pool.wait_ge(s_ss, n)
                        ins = pool.tensor_tensor(ssum[:, :], ssum[:, :], sq[:, n % 2, :], ALU.add)
                    ins.then_inc(s_ss, 1)

            pool.memset(eps[:, :], EPS).then_inc(s_con, 1)
            sum_squares("start")
            for p in range(2):
                for x in range(2):
                    pool.wait_ge(s_gat, 2 * p + x + 1)
                    a3 = gatt[:, x, :].rearrange("p (t c) -> p t c", c=P)
                    chain(pool.affine_select(out=a3, in_=a3, pattern=[[0, NT], [1, P]], compare_op=ALU.is_ge, fill=0.0,
                                             base=0, channel_multiplier=-1))
                    pool.memset(a3[0:GCH, :, GCH:P], 0.0).then_inc(s_gpo, 1)
            for p in range(4):
                for n in range(4):
                    x = n % 2
                    if n < 2:
                        pool.wait_ge(s_sdv, 10 * p + 4 + 2 * x)
                    else:
                        pool.wait_ge(s_sac, 5 * p + 3 + x)
                    for c in range(NT):
                        d = ssp[:, x, CO[c]:CO[c] + P]
                        ins = pool.affine_select(out=d, in_=d, pattern=[[1, P]], compare_op=ALU.is_gt, fill=0.0, base=0,
                                                 channel_multiplier=-1)
                    ins.then_inc(s_spo, 1)
            sum_squares("wout")
            sum_squares("ffout")
            pool.wait_ge(s_cld, 48)
            pool.affine_select(out=wsf[:, :, :], in_=wsf[:, :, :], pattern=[[0, KD], [1, P]], compare_op=ALU.is_ge, fill=0.0,
                               base=0, channel_multiplier=-1).then_inc(s_cpo, 1)
            sum_squares("final1")
            sum_squares("cgout")
            sum_squares("down01")
            sum_squares("dilout")
            sum_squares("down11")


def bucket(distance):
    n, exact = 32, 16
    nf = np.maximum(distance, 1).astype(np.float32)
    large = exact + (np.log(nf / np.float32(exact)) / np.float32(math.log(2048 / exact)) * np.float32(n - exact)).astype(np.int32)
    return np.where(distance < exact, distance, np.minimum(large, n - 1))


def one_hot():
    col = np.arange(256)
    out = np.zeros((33, 4, 256), np.float32)
    for g in range(4):
        rel = (P if g == 0 else 0) + P - 1 - col
        ok = (rel >= 0) & (rel <= P)
        if g == 3:
            ok &= rel % 4 == 0
        row = np.where(ok, bucket(np.clip(rel, 0, P) * (1 if g < 2 else 4)), 32)
        out[row, g, col] = 1.0
    return out.reshape(33, 1024)


def constants():
    i = np.arange(P)
    keep = np.tile((np.arange(T) % GCH != 0).astype(np.float32), (P, 1))
    tri = -(i[:, None] >= i[None, :]).astype(np.float32)
    one = np.ones((P, P), np.float32)
    return np.concatenate([np.eye(P, dtype=np.float32), tri, -one, one, keep], 1)


def units(w, k_tiles=UT):
    K, M = w.shape
    n = -(-K // (P * k_tiles))
    if K < n * P * k_tiles:
        w = np.concatenate([w, np.zeros((n * P * k_tiles - K, M), w.dtype)], 0)
    return w.reshape(n, k_tiles, P, M // P, P).transpose(3, 0, 2, 1, 4).reshape(n * M // P, P, k_tiles * P)


def wide_units(w):
    return w.reshape(4, P, -1, 2, P).transpose(2, 1, 3, 0, 4).reshape(-1, P, UT * P)


def stream(a):
    w = a["w_in"][0]
    out = [units(w[:, OFF_GA:OFF_GA + P])]
    for p in range(2):
        out += [units(w[:, OFF_GQ + P * p:OFF_GQ + P * (p + 1)]), units(w[:, OFF_GK + P * p:OFF_GK + P * (p + 1)]),
                units(w[:, OFF_GV + 2 * P * p:OFF_GV + 2 * P * (p + 1)])]
    for p in range(4):
        out += [units(w[:, o + P * p:o + P * (p + 1)]) for o in (OFF_Q, OFF_K, OFF_V)]
        out += [units(w[:, OFF_G0 + 4 * P * p:OFF_G0 + 4 * P * (p + 1)]), units(w[:, OFF_GR + P * p:OFF_GR + P * (p + 1)])]
    both = np.stack([wide_units(a["w_branch_sb"][0]), wide_units(a["w_branch_gla"][0])], 1)
    out += [both.reshape(-1, P, UT * P), units(a["w_out"][0])]
    f = a["w_ffn_in"][0]
    out += [np.stack([units(f[:, :FF]), units(f[:, FF:])], 1).reshape(-1, P, UT * P), units(a["w_ffn_out"][0])]
    w = a["a_w_in_2"][0]
    v = w[:, D:].reshape(4, 2, P, 2, T).transpose(3, 0, 2, 1, 4).reshape(8, P, UT * P)
    out += [v, units(w[:, :D]), units(a["a_w_out_2"][0])]

    def mlp(n):
        up, down = a["w_up_2"][n], a["w_down_2"][n]
        return [x for s in (0, FF2 // 2) for x in (units(up[:, s:s + FF2 // 2]), units(down[s:s + FF2 // 2]))]

    out += mlp(0)
    w = a["b_w_qkv_2"][0]
    for p in range(4):
        for g in range(3):
            out += [units(w[:, 1536 * c + 512 * g + P * p:1536 * c + 512 * g + P * (p + 1)]) for c in range(3)]
    out += [wide_units(a["b_w_out_2"][0])] + mlp(1)
    out = np.concatenate(out, 0)
    assert out.shape[0] == NU
    return out


def columns(v):
    return v.reshape(-1, P).T


def params(a):
    g2 = a["mix_norm_g_2"], a["mlp_norm_g_2"]
    rows = [a["norm_mix_g"][0], a["norm_ffn_g"][0], a["norm_final_g"], g2[0][0], g2[0][1], g2[1][0], g2[1][1],
            a["final_norm_g_2"], a["b_gate"][0, 0], a["b_gate"][0, 1]]
    conv = np.concatenate([a["conv_w"][0], a["conv_b"]], 0).reshape(4, KF, P).transpose(2, 1, 0).reshape(P, 4 * KF)
    return np.concatenate([columns(r) for r in rows] + [conv, columns(a["b_alpha"][0]), columns(a["gla_norm_g"][0])], 1)


def kernel(**inputs):
    import concourse.bacc as bacc
    from concourse.bass_utils import run_bass_kernel_spmd

    a = {k: np.asarray(v) for k, v in inputs.items()}
    arrays = {
        "wst": stream(a),
        "xT": a["x"][0].T.reshape(KD, P, T),
        "prm": params(a),
        "cst": constants(),
        "wup": a["w_alpha_up"][0],
        "wsT": a["a_w_s_2"][0].transpose(2, 0, 1),
        "bs": a["a_b_s_2"][0],
        "lngb": np.stack([a["a_ln_g_2"][0], a["a_ln_b_2"][0]]),
        "rb": a["rel_bias_2"],
        "onehot": one_hot(),
    }
    arrays = {k: np.ascontiguousarray(v) for k, v in arrays.items()}
    nc = bacc.Bacc("TRN2", target_bir_lowering=False, num_devices=1)
    args = [nc.dram_tensor(n, v.shape, mybir.dt.from_np(v.dtype), kind="ExternalInput").ap() for n, v in arrays.items()]
    fdram = nc.dram_tensor("bias_rows", (8, 1024), F32, kind="Internal").ap()
    out = nc.dram_tensor("out", (KD, P, T), F32, kind="ExternalOutput").ap()
    build(nc, *args, fdram, out)
    r = run_bass_kernel_spmd(nc, [arrays], core_ids=[0])
    got = r.results[0]["out"]
    return np.ascontiguousarray(got.reshape(D, T).T).reshape(1, T, D)
```

```python
import math
from contextlib import ExitStack

import numpy as np

import concourse.bass as bass
from concourse import mybir

F32 = mybir.dt.float32
F32R = mybir.dt.float32r
ALU = mybir.AluOpType
ACT = mybir.ActivationFunctionType
AX = mybir.AxisListType.X

P = 128
T = 512
D = 1024
KD = D // P
EPS = 1e-6
NT = T // P
FF = 2816
KF = FF // P
FF2 = 4096
SLOTS = 4
LOOK = SLOTS - 1
UT = 8
DH = 64
VG = 128
GCH = 64
TAU = 16.0
NEG = -1e30

OFF_Q, OFF_K, OFF_V = 0, 512, 1024
OFF_GQ, OFF_GK, OFF_GV, OFF_GR, OFF_GA = 1536, 1792, 2048, 2560, 3072
OFF_G0 = 3088
OFF_G1 = OFF_G0 + D

GLA_PLAN = [("decay", 0), ("q", 0), ("cumulate", 0), ("k", 0), ("va", 0), ("scale", 0), ("vb", 0), ("gate", 0),
            ("turn", 0), ("gate", 1), ("states", 0), ("gate", 2), ("q", 1), ("outputs", 0), ("k", 1), ("norms", 0),
            ("decay", 1), ("va", 1), ("cumulate", 1), ("vb", 1), ("scale", 1), ("gate", 3), ("turn", 1),
            ("gate", 4), ("states", 1), ("gate", 5), ("gate", 6), ("outputs", 1), ("gate", 7), ("norms", 1)]
GLA_UNITS = [e for e in GLA_PLAN if e[0] in ("q", "k", "va", "vb", "gate")]
N_GLA, N_SB = len(GLA_UNITS), 24
SB_R, SB_G, SB_Q, SB_V, SB_PAIR = 3, 4, 6, 8, 6
STREAM = [("ga", 1), ("gla", N_GLA), ("sb", N_SB), ("branch", 8), ("wout", 8), ("ffin", 2 * KF), ("ffout", 3 * KD),
          ("cgv", 8), ("cgu", 8), ("cgout", 8),
          ("up00", 16), ("down00", 16), ("up01", 16), ("down01", 16),
          ("dil", 36), ("dilout", 4),
          ("up10", 16), ("down10", 16), ("up11", 16), ("down11", 16)]
U0 = {}
NU = 0
for _name, _n in STREAM:
    U0[_name] = NU
    NU += _n

A0 = {}
NA = 0
for _name, _n in [("ga", 1), ("gla", N_GLA), ("sb", N_SB), ("branch", 16), ("wout", 8), ("ffin", 2 * KF), ("ffout", 8),
                  ("cgu", 8), ("cgout", 8), ("up00", 16), ("down00", 8), ("up01", 16), ("down01", 8),
                  ("dil", 36), ("dilout", 16), ("up10", 16), ("down10", 8), ("up11", 16), ("down11", 8)]:
    A0[_name] = NA
    NA += _n

X_SPLITS = ["wout", "final1", "cgout", "down01", "dilout"]
SQUARES = ["start", "wout", "ffout", "final1", "cgout", "down01", "dilout", "down11"]
X0 = {n: KD * (i + 1) for i, n in enumerate(X_SPLITS)}
S0 = {n: KD * i for i, n in enumerate(SQUARES)}
N0 = {n: i for i, n in enumerate(SQUARES)}

R0 = {}
_n = 0
for _name, _c in [("ogla", 4), ("osb", 4), ("y", 8), ("ffin", KF), ("cgv", 4), ("ug", 8), ("up00", 16), ("up01", 16),
                  ("dilo", 4), ("up10", 16), ("up11", 16)]:
    R0[_name] = _n
    _n += _c

G_MIX, G_FFN, G_FIN, G_MIX2, G_MLP2, G_FIN2, G_BG = 0, 1, 2, 3, 5, 7, 8
C_CONV = 80
C_BA = C_CONV + 4 * KF
C_GG = C_BA + 2
NP = C_GG + 4

CO = {0: 0, 1: 512, 3: 896, 2: 1024}
CW = 1280

LOGIT = 512
DEN, NMAX, ROW = 2 * DH, 2 * DH + 2, 2 * DH + 4

TICKS, LAG_T, LAG_V = 4, 2, 4
STEPS = 64
STEP_AT = {}
for _p in range(4):
    for _s in range(8):
        STEP_AT[TICKS * (9 * _p + 3) + 3 * _s] = 16 * _p + _s
        STEP_AT[TICKS * (9 * _p + 9) + (3 * _s // 2 if _p < 3 else _s)] = 16 * _p + 8 + _s
for _s in range(LAG_V):
    STEP_AT[TICKS * 36 + 8 + _s] = STEPS + _s
LAST_TICK = TICKS * 36 + 8 + LAG_V
PERMUTE_AT, MERGE_AT = 52, 53
TRANSPOSE_AT, SPLIT_AT, OUT_AT = 56, (56, 57, 58), 59


OUT_UNITS = (57, 63, 66)


def step_of(n):
    return n // 16, n // 8 % 2, n // 4 % 2, n % 4


def at(base, i=None, step=0):
    return base if i is None else i * step + base


class Chain:

    def __init__(self, eng, sem):
        self.eng, self.sem, self.n, self.i, self.step = eng, sem, 0, None, 0

    def __call__(self, ins):
        self.n += 1
        ins.then_inc(self.sem, 1)
        self.eng.wait_ge(self.sem, at(self.n, self.i, self.step))

    def loop(self, i, step):
        self.i, self.step, self.first = i, step, self.n

    def end(self, turns):
        assert self.n == self.first + self.step, (self.n - self.first, self.step)
        self.n = self.first + self.step * turns
        self.i = None


def build(nc, wst, xT, prm, cst, wup, wsT, bs, lngb, rb, onehot, fdram, out):
    es = ExitStack()
    with es:
        def sb(name, shape, dt=F32, st=es):
            return st.enter_context(nc.sbuf_tensor(name, shape, dt))

        def sem(name):
            return es.enter_context(nc.semaphore(name))

        raw = sb("raw", [P, 2, UT * P])
        whi = sb("whi", [P, SLOTS, UT * P], F32R)
        wlo = sb("wlo", [P, SLOTS, UT * P], F32R)
        h = sb("h", [P, KD, T])
        xhi = sb("xhi", [P, KD, T], F32R)
        xlo = sb("xlo", [P, KD, T], F32R)
        par = sb("par", [P, NP])
        con = sb("con", [P, 4, P])
        ident, ones = con[:, 0, :], con[:, 3, :]
        trir = sb("trir", [P, 2, P], F32R)
        rbc = sb("rbc", [P, T])
        rtmp = sb("rtmp", [P, T])
        ssum = sb("ssum", [P, T])
        sq = sb("sq", [P, 2, T])
        eps = sb("eps", [P, 1])
        rtok = sb("rtok", [P, NT])
        PS = es.enter_context(nc.psum_tensor("ps", [P, 8 * T], F32))

        def bank(b, n=1):
            return PS[:, b * T:(b + n) * T]

        with ExitStack() as m1:
            o_gla = sb("o_gla", [P, 4, T], F32, m1)
            gate_a = sb("gate_a", [P, KD, T], F32, m1)
            with ExitStack() as m:
                ga = sb("ga", [16, T], F32, m)
                wu = sb("wu", [16, 2 * P], F32, m)
                smask = sb("smask", [P, T], F32, m)
                gf = sb("gf", [P, 4, T], F32, m)
                gt = sb("gt", [P, 8, T], F32, m)
                gqk = sb("gqk", [P, 4, T], F32R, m)
                gtok = sb("gtok", [P, 6, T], F32R, m)
                gatt = sb("gatt", [P, 2, T], F32, m)
                gatr = sb("gatr", [P, 4, T], F32R, m)
                gst = sb("gst", [P, 8, P], F32, m)
                gstr = sb("gstr", [P, 2, 8, P], F32R, m)
            gate_b = sb("gate_b", [P, KD, T], F32, m1)
            o_sb = sb("o_sb", [P, 4, T], F32, m1)
            with ExitStack() as m:
                sqk = sb("sqk", [P, 4, T], F32R, m)
                svf = sb("svf", [P, T], F32, m)
                svp = sb("svp", [P, 2, 2, NT, P], F32R, m)
                sl = sb("sl", [P, CW], F32, m)
                ssp = sb("ssp", [P, 2, CW], F32, m)
                sspr = sb("sspr", [P, 2, 2, CW], F32R, m)
                sgr = sb("sgr", [P, 2, T], F32, m)
            with ExitStack() as m:
                yf = sb("yf", [P, 2, T], F32, m)
                yr = sb("yr", [P, 2, KD, T], F32R, m)
        with ExitStack() as m:
            hid = sb("hid", [P, 2, KF, T], F32R, m)
            apad = sb("apad", [P, T + 2], F32, m)
            cv = sb("cv", [P, 2, T], F32, m)
            gl = sb("gl", [P, 2, T], F32, m)
            gs = sb("gs", [P, T], F32, m)
        with ExitStack() as m:
            wsr = sb("wsr", [P, 2, KD, P], F32R, m)
            wsf = sb("wsf", [P, KD, P], F32, m)
            bsb = sb("bsb", [P, KD, P], F32, m)
            lgb = sb("lgb", [P, 2, D], F32, m)
            vt = sb("vt", [P, NT, D], F32, m)
            vr = sb("vr", [P, 2, NT, D], F32R, m)
            ugr = sb("ugr", [P, 2, KD, T], F32R, m)
            st6 = sb("st6", [P, NT, 2, 6], F32, m)
            mv = sb("mv", [P, NT, 4], F32, m)
            rtm = lgb[:, :, 0:T]
            uf = vt[:, :, :].rearrange("p t (a b) -> p (t a) b", b=T)
        with ExitStack() as m:
            mh = sb("mh", [P, 2, 16, T], F32R, m)
            mr = sb("mr", [P, 2, T], F32, m)
            ms = sb("ms", [P, 2, T], F32, m)
        with ExitStack() as m:
            oA = sb("oA", [P, NT, 4, ROW], F32, m)
            oB = sb("oB", [P, NT, 4, ROW], F32, m)
            oP = sb("oP", [P, NT, 4, ROW], F32, m)
            dqk = sb("dqk", [P, 3, 4, T], F32R, m)
            dvt = sb("dvt", [P, 3, 2, T], F32R, m)
            mtmp = sb("mtmp", [P, 2, T], F32, m)
            dvf = sb("dvf", [P, T], F32, m)
            dl = sb("dl", [P, 4, 256], F32, m)
            cAB = sb("cAB", [P, 4, NT, 4, 2], F32, m)
            sb("behind_mlp", [P, 36 * T - 3 * NT * 4 * ROW - 23 * T - NT * 32], F32, m)
            bias = sb("bias", [P, 8, LOGIT], F32, m)
            ohs = sb("ohs", [33, 24 + 4 * 256], F32, m)
            dp = sb("dp", [P, 4, 256], F32, m)
            dpt = sb("dpt", [P, 4, 2, 256], F32R, m)
            fsb = dp[0:8, :, :].rearrange("p a b -> p (a b)")
            orr = [dqk[:, 0, 0:2, :], dqk[:, 0, 2:4, :], None, dqk[:, 1, 0:2, :]]

        def gate(f):
            return gate_a[:, f, :] if f < KD else gate_b[:, f - KD, :]

        def out_pair(j):
            return (xhi[:, 0, :], xlo[:, 0, :]) if j == 2 else (orr[j][:, 0, :], orr[j][:, 1, :])

        def weigh(eng, p):
            return [eng.tensor_tensor(o, o, cAB[:, k, :, p, :].unsqueeze(3).to_broadcast([P, NT, 2, DH]), ALU.mult)
                    for k, o in ((k, tile[:, :, p, 0:DEN].rearrange("p t (x d) -> p t x d", d=DH)) for k, tile in ((1, oA), (2, oP)))]

        def hl(tile, k):
            return tile[:, 0, k, :], tile[:, 1, k, :]

        s_raw = [sem("raw0_loaded"), sem("raw1_loaded")]
        s_hi = sem("unit_hi_done")
        s_split = sem("unit_split_done")
        s_unit = sem("unit_multiplied")
        s_par = sem("params_loaded")
        s_h0 = sem("h_loaded")
        s_con = sem("constants_made")
        s_free = sem("acc_bank_free")
        s_xhi = sem("x_hi_done")
        s_x = sem("x_split_done")
        s_sqd = sem("square_done")
        s_ss = sem("square_summed")
        s_nmm = sem("mean_square_multiplied")
        s_nsq = sem("rms_done")
        s_rb = sem("inverse_rms_done")
        s_r = sem("operand_split_done")
        s_dch = sem("vector_chain")
        s_ach = sem("scalar_chain")
        s_pch = sem("pool_chain")
        s_gat = sem("gla_scores_copied")
        s_gpe = sem("gla_multiplied")
        s_gdv = sem("gla_vector_done")
        s_gac = sem("gla_scalar_done")
        s_gpo = sem("gla_masked")
        s_sqk = sem("sb_qk_split")
        s_spe = sem("sb_multiplied")
        s_sdv = sem("sb_vector_done")
        s_sac = sem("sb_scalar_done")
        s_spo = sem("sb_masked")
        s_sig = sem("gate_sigmoid_done")
        s_cv = sem("conv_done")
        s_ge = sem("gelu_done")
        s_cpe = sem("chunk_gating_multiplied")
        s_cdv = sem("chunk_gating_vector_done")
        s_cac = sem("chunk_gating_gelu_done")
        s_cpo = sem("chunk_gating_masked")
        s_cld = sem("chunk_gating_params_loaded")
        s_ms = sem("relu_squared")
        s_dld = sem("bias_inputs_loaded")
        s_fst = sem("bias_rows_stored")
        s_bld = sem("bias_loaded")
        s_bmm = sem("bias_rows_multiplied")
        s_bdv = sem("bias_rows_copied")
        s_dqk = sem("dilated_qk_split")
        s_dtv = sem("dilated_v_transposed")
        s_dvs = sem("dilated_v_split")
        s_dlo = sem("dilated_logits_multiplied")
        s_dof = sem("dilated_outputs_copied")
        s_min = sem("dilated_maxima_compared")
        s_mex = sem("merge_factors_done")
        s_fac = sem("first_merge_factors_ready")
        s_pmr = sem("first_pairs_merged")
        s_mrg = sem("dilated_merged")
        s_dop = sem("dilated_projection_part")
        s_otr = sem("dilated_outputs_transposed")
        s_dtr = sem("dilated_transposed")
        s_dpv = sem("dilated_values_multiplied")
        s_dlg = sem("dilated_logits_done")
        s_dac = sem("dilated_exp_done")
        s_dhi = sem("dilated_probs_hi_done")
        s_dsp = sem("dilated_probs_split")
        s_perm = sem("dilated_rows_permuted")
        s_out = sem("out_stored")
        s_fin = sem("out_ready")

        block = es.enter_context(nc.Block())

        def sbank(x, n):
            return bank((2, 3, 4, 7)[2 * x + n % 2])[:, (n // 2) * P:(n // 2 + 1) * P]

        def mm3(pe, o, w, x, first, done, **kw):
            pe.matmul(o, w[0], x[0], start=first, stop=False, **kw)
            pe.matmul(o, w[1], x[0], start=False, stop=False, **kw)
            return pe.matmul(o, w[0], x[1], start=False, stop=done, **kw)

        @block.sync
        def _(sp):
            sp.dma_start(raw[:, 0, :], wst[0]).then_inc(s_raw[0], 16)
            sp.dma_start(raw[:, 1, :], wst[1]).then_inc(s_raw[1], 16)
            sp.wait_ge(s_split, 1)
            sp.dma_start(raw[:, 0, :], wst[2]).then_inc(s_raw[0], 16)
            with sp.Fori(0, (NU - 3) // 2, 1) as i:
                for j in range(2):
                    n = 3 + j
                    sp.wait_ge(s_split, at(n - 1, i, 2))
                    sp.dma_start(raw[:, n % 2, :], wst[2 * i + n]).then_inc(s_raw[n % 2], 16)
            for m in range(KD):
                sp.wait_ge(s_fin, m + 1)
                sp.dma_start(out[m], h[:, m, :]).then_inc(s_out, 16)
            sp.wait_ge(s_out, 16 * KD)

        @block.tensor
        def _(pe):
            def unit_ready(u, i=None, s=0):
                pe.wait_ge(s_split, at(u + 1, i, s))

            def w_tile(slot, t, n=P):
                return whi[:, slot, t * P:t * P + n], wlo[:, slot, t * P:t * P + n]

            def acc_wait(a, i=None, s=0):
                if a >= 2:
                    pe.wait_ge(s_free, at(a - 1, i, s))

            def x_tile(k):
                return xhi[:, k, :], xlo[:, k, :]

            def dense(u, a, groups, xs, i=None, us=0, as_=0, tick=None):
                flat = [(g, t) for g, ts in enumerate(groups) for t in ts]
                for n, (g, (j, t, k)) in enumerate(flat):
                    if n == 0 or flat[n - 1][1][0] != j:
                        unit_ready(u + j, i, us)
                    first = n == 0 or flat[n - 1][0] != g
                    end = n + 1 == len(flat) or flat[n + 1][0] != g
                    if first:
                        acc_wait(a + g, i, as_)
                    ins = mm3(pe, bank((a + g) % 2), w_tile((u + j) % SLOTS, t), xs(k), first, end)
                    if n + 1 == len(flat) or flat[n + 1][1][0] != j:
                        ins.then_inc(s_unit, 1)
                    if tick and n % 2:
                        tick(n // 2)

            def full(n_units):
                return [[(j, k, k) for k in range(UT)] for j in range(n_units)]

            def loop(name, turns, nu, groups, xs):
                u, a, g = U0[name], A0[name], len(groups)
                assert nu % SLOTS == 0 and g % 2 == 0
                with pe.Fori(0, turns, 1) as i:
                    dense(u, a, groups, xs, i, nu, g)

            def norm(name):
                pe.wait_ge(s_ss, S0[name] + KD)
                pe.matmul(bank(7), ones, ssum[:, :], start=True, stop=True).then_inc(s_nmm, 1)

            pe.wait_ge(s_con, 2)
            pe.wait_ge(s_par, 64)
            norm("start")
            pe.wait_ge(s_x, KD)
            dense(U0["ga"], A0["ga"], full(1), x_tile)
            def decay(p):
                pe.wait_ge(s_gdv, 14 * p - (6 if p else -1))
                pe.matmul(bank(7), wu[:, p * P:(p + 1) * P], ga[:, :], start=True, stop=True).then_inc(s_gpe, 1)

            def turn(p):
                pe.wait_ge(s_free, A0["gla"] + GLA_UNITS.index(("vb", p)) + 1)
                pe.wait_ge(s_gdv, 1 + 13 * p + 3)
                for n, src in enumerate((gt[:, 7, :], gf[:, 2, :], gf[:, 3, :])):
                    for t in range(NT):
                        ins = pe.transpose(bank(2 + n)[:, t * P:(t + 1) * P], src[:, t * P:(t + 1) * P], ident)
                    ins.then_inc(s_gpe, 1)
                for x in range(2):
                    r = slice(64 * x, 64 * x + 64)
                    for t in range(NT):
                        c = slice(t * P, (t + 1) * P)
                        ins = mm3(pe, bank(5 + x)[:, c], (gqk[r, 2, c], gqk[r, 3, c]), (gqk[r, 0, c], gqk[r, 1, c]),
                                  t == 0, True, skip_group_check=True)
                    ins.then_inc(s_gpe, 1)

            def states(p):
                pe.wait_ge(s_gdv, 1 + 13 * p + 6)
                for x in range(2):
                    for n in range(7):
                        r = slice(64 * (n % 2), 64 * (n % 2) + 64)
                        c = slice((n // 2) * P, (n // 2 + 1) * P)
                        ins = mm3(pe, sbank(x, n),
                                  (gtok[r, 0, c], gtok[r, 1, c]), (gtok[r, 2 + 2 * x, c], gtok[r, 3 + 2 * x, c]),
                                  n < 2, True, skip_group_check=True)
                    ins.then_inc(s_gpe, 1)

            def outputs(p):
                pe.wait_ge(s_gdv, 1 + 13 * p + 9)
                for x in range(2):
                    r = slice(64 * x, 64 * x + 64)
                    for t in range(NT):
                        c = slice(t * P, (t + 1) * P)
                        mm3(pe, bank(5 + x)[:, c], (gtok[:, 2 + 2 * x, c], gtok[:, 3 + 2 * x, c]),
                            (gatr[:, 2 * x, c], gatr[:, 2 * x + 1, c]), t == 0, True, skip_group_check=True)
                    for n in range(1, 8):
                        c = slice(n * GCH, (n + 1) * GCH)
                        ins = mm3(pe, bank(5 + x)[:, c], (gstr[r, 0, n, :], gstr[r, 1, n, :]),
                                  (gqk[r, 0, c], gqk[r, 1, c]), False, True, skip_group_check=True)
                    ins.then_inc(s_gpe, 1)

            def norms(p):
                for x in range(2):
                    pe.wait_ge(s_gdv, 1 + 13 * p + 10 + x)
                    pe.matmul(bank(2 + x), ones, gatt[:, x, :], start=True, stop=True).then_inc(s_gpe, 1)

            for what, p in GLA_PLAN:
                if (what, p) in GLA_UNITS:
                    n = GLA_UNITS.index((what, p))
                    dense(U0["gla"] + n, A0["gla"] + n, full(1), x_tile)
                elif what == "decay":
                    decay(p)
                elif what == "turn":
                    turn(p)
                elif what == "states":
                    states(p)
                elif what == "outputs":
                    outputs(p)
                elif what == "norms":
                    norms(p)
            def branch(n, count):
                if n == 1:
                    pe.wait_ge(s_r, R0["osb"])
                for j in range(n - 1, n - 1 + count):
                    dense(U0["branch"] + j, A0["branch"] + 2 * j, [[(0, 4 * m + k, k) for k in range(4)] for m in range(2)],
                          lambda k: x_tile(4 + k if j < 4 else k))

            pe.wait_ge(s_gdv, 27)
            for p in range(4):
                u, a = U0["sb"] + SB_PAIR * p, A0["sb"] + SB_PAIR * p
                V, A = 8 * p, 5 * p

                def units(j, n=1):
                    dense(u + j, a + j, full(n), x_tile)

                def scores(x):
                    r = slice(64 * x, 64 * x + 64)
                    z = bank(2 + 3 * x, 3)
                    for c in (0, 1, 3, 2):
                        ins = mm3(pe, z[:, CO[c]:CO[c] + T - P * c], (sqk[r, 2, c * P:(c + 1) * P], sqk[r, 3, c * P:(c + 1) * P]),
                                  (sqk[r, 0, c * P:], sqk[r, 1, c * P:]), c != 3, True, skip_group_check=True)
                    ins.then_inc(s_spe, 1)

                def tails(x):
                    z = bank(2 + 3 * x, 3)
                    for c in range(NT):
                        for d in range(c, NT):
                            o = z[:, CO[c] + P * (d - c):CO[c] + T - P * c]
                            w = trir[:, 0 if d == c else 1, :]
                            for part in range(2):
                                ins = pe.matmul(o, w, sspr[:, part, x, CO[d]:CO[d] + T - P * d], start=False,
                                                stop=True, skip_group_check=True)
                    ins.then_inc(s_spe, 1)

                if p == 0:
                    units(0, 3)
                else:
                    pe.wait_ge(s_sac, A)
                pe.wait_ge(s_free, a + 3)
                for c in range(NT):
                    ins = pe.transpose(bank(5)[:, c * P:(c + 1) * P], svf[:, c * P:(c + 1) * P], ident)
                ins.then_inc(s_spe, 1)
                pe.wait_ge(s_sqk, 2 * p + 2)
                if p:
                    pe.wait_ge(s_sdv, V)
                scores(0)
                units(SB_R)
                pe.wait_ge(s_sdv, V + 1)
                scores(1)
                units(SB_G)
                pe.wait_ge(s_sdv, V + 3)
                tails(0)
                units(SB_G + 1)
                pe.wait_ge(s_sdv, V + 5)
                tails(1)
                if p < 3:
                    units(SB_Q, 2)
                else:
                    branch(1, 2)
                pe.wait_ge(s_sdv, V + 7)
                for x in range(2):
                    for c in range(NT):
                        ins = mm3(pe, bank(2)[:, c * P:], (svp[:, 0, x, c, :], svp[:, 1, x, c, :]),
                                  (sspr[:, 0, x, CO[c]:CO[c] + T - P * c], sspr[:, 1, x, CO[c]:CO[c] + T - P * c]),
                                  x == 0 and c == 0, True, skip_group_check=True)
                ins.then_inc(s_spe, 1)
                if p < 3:
                    units(SB_V)
            branch(3, 2)
            pe.wait_ge(s_r, R0["y"])
            branch(5, 4)
            pe.wait_ge(s_r, R0["ffin"])
            loop("wout", 2, 4, full(4), lambda k: hl(yr, k))
            norm("wout")
            pe.wait_ge(s_x, X0["wout"] + KD)
            loop("ffin", KF // 2, 4, full(4), x_tile)
            pe.wait_ge(s_r, R0["cgv"])
            down = [[(3 * m + k // UT, k % UT, k) for k in range(KF)] for m in range(4)]
            loop("ffout", 2, 12, down, lambda k: hl(hid, k))
            norm("ffout")
            norm("final1")
            pe.wait_ge(s_rb, N0["final1"] + 1)
            for t in range(NT):
                ins = pe.transpose(bank(2 + t)[:, 0:P], rbc[:, t * P:(t + 1) * P], ident)
            ins.then_inc(s_cpe, 1)
            pe.wait_ge(s_x, X0["final1"] + KD)
            pe.wait_ge(s_cdv, 1)
            for f in range(2):
                for j in range(4):
                    u = U0["cgv"] + 4 * f + j
                    unit_ready(u)
                    for kk in range(2):
                        k = 2 * j + kk
                        for t in range(NT):
                            if f and k == 0:
                                pe.wait_ge(s_cac, t + 1)
                            c = slice(t * P, (t + 1) * P)
                            ins = mm3(pe, bank(2 + t), (xhi[:, k, c], xlo[:, k, c]),
                                      (whi[:, u % SLOTS, kk * T:(kk + 1) * T], wlo[:, u % SLOTS, kk * T:(kk + 1) * T]),
                                      k == 0, k == KD - 1)
                    ins.then_inc(s_unit, 1)
            loop("cgu", 2, 4, full(4), x_tile)
            pe.wait_ge(s_r, R0["ug"])
            pe.wait_ge(s_cdv, 2)
            for g in range(KD):
                if g >= 4:
                    pe.wait_ge(s_cdv, g)
                for t in range(NT):
                    ins = mm3(pe, bank(2 + g % 4)[:, t * P:(t + 1) * P], (vr[:, 0, t, g * P:(g + 1) * P], vr[:, 1, t, g * P:(g + 1) * P]),
                              (wsr[:, 0, g, :], wsr[:, 1, g, :]), t == 0, True, skip_group_check=True)
                ins.then_inc(s_cpe, 1)
            pe.wait_ge(s_r, R0["up00"])
            loop("cgout", 2, 4, full(4), lambda k: hl(ugr, k))
            norm("cgout")

            def bias_rows():
                pe.wait_ge(s_dld, 32)
                pe.wait_ge(s_bdv, 1)
                for g in range(4):
                    grp = max(0, g - 1)
                    ins = pe.matmul(bank(2 + g // 2)[0:8, (g % 2) * 256:(g % 2) * 256 + 256], ohs[:, 8 * grp:8 * grp + 8],
                                    ohs[:, 24 + g * 256:24 + (g + 1) * 256], start=g % 2 == 0, stop=True, skip_group_check=True)
                ins.then_inc(s_bmm, 1)

            def mlp(layer, before):
                pe.wait_ge(s_x, X0[before] + KD)
                m_t = lambda k: hl(mh, k)
                for half in range(2):
                    loop(f"up{layer}{half}", 4, 4, full(4), x_tile)
                    if layer == 0 and half == 0:
                        bias_rows()
                    pe.wait_ge(s_r, R0[f"up{layer}{half}"] + 16)
                    groups = [[(2 * m + k // UT, k % UT, k) for k in range(16)] for m in range(4)]
                    loop(f"down{layer}{half}", 2, 8, groups, m_t)
                norm("down01" if layer == 0 else "down11")

            mlp(0, "cgout")
            pe.wait_ge(s_x, X0["down01"] + KD)

            def logits(n):
                p, part, x, t = step_of(n)
                r = slice(64 * x, 64 * x + 64)
                b = bank(2 + n % 2)
                if n % 8 == 0:
                    pe.wait_ge(s_dqk, 2 * (3 * p + (3 if part else 1)))
                if n >= 2:
                    pe.wait_ge(s_dlg, n - 1)
                if part == 0:
                    c = slice(T - (t + 1) * P, T - t * P)
                    k0 = (t - 1) * P if t else 0
                    ins = mm3(pe, b[:, 0:256] if t else b[:, 128:256], (dqk[r, 0, 0, c], dqk[r, 0, 1, c]),
                              (dqk[r, 0, 2, k0:(t + 1) * P], dqk[r, 0, 3, k0:(t + 1) * P]), True, True, skip_group_check=True)
                else:
                    for g in (1, 2):
                        ins = mm3(pe, b[:, 128 * (g - 1):128 * g], (dqk[r, g, 0, 3 - t::4], dqk[r, g, 1, 3 - t::4]),
                                  (dqk[r, g, 2, t::4], dqk[r, g, 3, t::4]), g == 1, True, skip_group_check=True)
                ins.then_inc(s_dlo, 1)

            def turned(n):
                p, part, x, t = step_of(n)
                pe.wait_ge(s_dac, n + 1)
                if n >= 2:
                    pe.wait_ge(s_dsp, n - 1)
                for j in range(0 if part or t else 1, 2):
                    ins = pe.transpose(bank(4 + n % 2)[:, j * P:(j + 1) * P], dp[:, n % 4, j * P:(j + 1) * P], ident)
                ins.then_inc(s_dtr, 1)

            def sums(n):
                p, part, x, t = step_of(n)
                pe.wait_ge(s_dsp, n + 1)
                if n % 8 == 0:
                    pe.wait_ge(s_dvs, 3 * p + (3 if part else 1))
                if t == 0 and n:
                    pe.wait_ge(s_dof, n // 4)
                first = t == 0
                for j in range(0 if part or t else 1, 2):
                    g = j + 1 if part else 0
                    kt = t - 1 + j if part == 0 else t
                    v = slice(kt * P + 64 * x, kt * P + 64 * x + 64)
                    ins = mm3(pe, bank(6)[:, t * 64:(t + 1) * 64],
                              (dpt[:, n % 4, 0, j * P:(j + 1) * P], dpt[:, n % 4, 1, j * P:(j + 1) * P]),
                              (dvt[:, g, 0, v], dvt[:, g, 1, v]), first, True, skip_group_check=True)
                    first = False
                ins.then_inc(s_dpv, 1)

            def outputs_turned(j, b):
                for t in range(NT):
                    ins = pe.transpose(bank(b)[:, t * P:(t + 1) * P], oA[:, t, j, 0:DEN], ident)
                ins.then_inc(s_otr, 1)

            def attend(k, q):
                if k and k % 3 == 0 and q == 1:
                    v = k // 3 - 1
                    pe.wait_ge(s_free, A0["dil"] + k)
                    if v:
                        pe.wait_ge(s_dvs, v)
                    for t in range(NT):
                        src = dvf[:, t * P:(t + 1) * P] if v % 3 == 0 else dvf[:, t::4]
                        ins = pe.transpose(bank(7)[:, t * P:(t + 1) * P], src, ident)
                    ins.then_inc(s_dtv, 1)
                n = STEP_AT.get(TICKS * k + q)
                if n is None:
                    return
                if LAG_T <= n < STEPS + LAG_T:
                    turned(n - LAG_T)
                if n >= LAG_V:
                    sums(n - LAG_V)
                if n < STEPS:
                    logits(n)
                if OUT_AT <= n < OUT_AT + KD:
                    m = n - OUT_AT
                    pe.wait_ge(s_r, R0["dilo"] + 3)
                    for k in range(3):
                        u, f = U0["dilout"] + (3 * m + k) // UT, (3 * m + k) % UT
                        if k == 0 or f == 0:
                            unit_ready(u)
                        if k == 0:
                            acc_wait(A0["dilout"] + m)
                        ins = mm3(pe, bank(m % 2), w_tile(u % SLOTS, f), out_pair(k), k == 0, k == 2)
                        if f == UT - 1:
                            ins.then_inc(s_unit, 1)
                    if m < KD - 1:
                        ins.then_inc(s_dop, 1)
                if n == TRANSPOSE_AT:
                    pe.wait_ge(s_pmr, 3)
                    pe.wait_ge(s_free, A0["dil"] + 36)
                    for j in range(2):
                        outputs_turned(j, j)
                if n == TRANSPOSE_AT + 1:
                    pe.wait_ge(s_dvs, 12)
                    outputs_turned(2, 7)

            for k in range(36):
                dense(U0["dil"] + k, A0["dil"] + k, full(1), x_tile, tick=lambda q: attend(k, q))
            for tick in range(TICKS * 36, LAST_TICK):
                attend(tick // TICKS, tick % TICKS)
            pe.wait_ge(s_mrg, 1)
            outputs_turned(3, 2)
            pe.wait_ge(s_r, R0["up10"])
            u = U0["dilout"] + 3
            unit_ready(u)
            for m in range(KD):
                acc_wait(A0["dilout"] + KD + m)
                ins = mm3(pe, bank(m % 2), w_tile(u % SLOTS, m), out_pair(3), True, True)
                ins.then_inc(s_dop if m < KD - 1 else s_unit, 1)
            norm("dilout")
            mlp(1, "dilout")

        @block.scalar
        def _(act):
            chain = Chain(act, s_ach)

            def hi(u, i=None, s=0):
                n = u + LOOK
                if n >= NU:
                    return
                act.wait_ge(s_raw[n % 2], at(16 * (n // 2 + 1), i, 8 * s))
                if n >= SLOTS:
                    act.wait_ge(s_unit, at(n - SLOTS + 1, i, s))
                act.activation(whi[:, n % SLOTS, :], raw[:, n % 2, :], ACT.Copy).then_inc(s_hi, 1)

            def x_hi(m, xn, g, sn, i=None, s=0, mi=None):
                hm = h[:, m, :]
                if sn >= 2:
                    act.wait_ge(s_ss, at(sn - 1, i, s))
                if g is not None:
                    act.activation(xhi[:, m, :], hm, ACT.Copy, scale=par[:, 8 * g + m:8 * g + m + 1] if mi is None else
                                   par[:, bass.ds(mi + 8 * g, 1)]).then_inc(s_xhi, 1)
                elif i is not None:
                    act.wait_ge(s_h0, 16 * KD)
                act.activation(sq[:, sn % 2, :], hm, ACT.Square).then_inc(s_sqd, 1)

            def rms(name):
                act.wait_ge(s_nmm, N0[name] + 1)
                act.activation(rtmp[:, :], bank(7), ACT.Sqrt, bias=eps[:, 0:1], scale=1.0 / D).then_inc(s_nsq, 1)

            def residual(name, turns, nu, ng, g, first=0):
                u, a, sn = U0[name], A0[name], S0[first]
                step = nu // ng if nu >= ng else 1
                with act.Fori(0, turns, 1) as i:
                    for m in range(ng):
                        for j in range(m * step, (m + 1) * step):
                            hi(u + j, i, nu)
                        act.wait_ge(s_free, at(a + m + 1, i, ng))
                        x_hi(i * ng + m, None, g, sn + m, i, ng, i * ng + m)
                rms(first)

            act.dma_start(par[:, :], prm).then_inc(s_par, 16)
            act.dma_start(con[:, :, :], cst[:, 0:4 * P].rearrange("p (a b) -> p a b", a=4)).then_inc(s_par, 16)
            for m in range(KD):
                act.dma_start(h[:, m, :], xT[m]).then_inc(s_h0, 16)
            act.dma_start(wu[:, :], wup).then_inc(s_par, 16)
            act.dma_start(smask[:, :], cst[:, 4 * P:4 * P + T]).then_inc(s_par, 16)
            act.wait_ge(s_par, 64)
            act.wait_ge(s_h0, 16 * KD)
            act.wait_ge(s_con, 2)
            for m in range(KD):
                x_hi(m, None, G_MIX, m)
                if m < LOOK:
                    hi(m - LOOK)
            rms("start")
            hi(0)
            for what, p in GLA_PLAN:
                V, E = 1 + 13 * p, 12 * p
                if (what, p) in GLA_UNITS:
                    hi(U0["gla"] + GLA_UNITS.index((what, p)))
                elif what == "decay":
                    ba = par[:, C_BA + p:C_BA + p + 1]
                    act.wait_ge(s_gpe, E + 1)
                    if p:
                        act.wait_ge(s_gdv, V)
                    chain(act.activation(gt[:, 1, :], bank(7), ACT.Abs, bias=ba))
                    chain(act.activation(gt[:, 1, :], gt[:, 1, :], ACT.Exp, scale=-1.0))
                    act.activation(gt[:, 1, :], gt[:, 1, :], ACT.Ln, bias=1.0).then_inc(s_gac, 1)
                elif what == "cumulate":
                    act.wait_ge(s_gdv, V + 2)
                    act.activation(gt[:, 4, :], gt[:, 2, :], ACT.Exp, scale=1 / TAU)
                    act.activation(gt[:, 5, :], gt[:, 2, :], ACT.Exp, scale=-1 / TAU)
                    act.activation(gt[:, 6, :], gt[:, 3, :], ACT.Exp, scale=1 / TAU).then_inc(s_gac, 1)
                elif what == "norms":
                    for x in range(2):
                        act.wait_ge(s_gpe, E + 11 + x)
                        act.activation(gt[:, x, :], bank(2 + x), ACT.Sqrt, bias=eps[:, 0:1], scale=1.0 / VG).then_inc(s_gac, 1)
            for j in range(3):
                hi(U0["sb"] + j)
            for p in range(4):
                u = U0["sb"] + SB_PAIR * p
                V, E = 8 * p, 6 * p

                def softplus(x):
                    act.wait_ge(s_spe, E + 2 + x)
                    if p or x:
                        act.wait_ge(s_sdv, V + 2 if x else V - 4)
                    z = bank(2 + 3 * x, 3)[:, 0:CW]
                    chain(act.activation(sl[:, :], z, ACT.Abs))
                    chain(act.activation(sl[:, :], sl[:, :], ACT.Exp, scale=-1.0))
                    act.activation(sl[:, :], sl[:, :], ACT.Ln, bias=1.0).then_inc(s_sac, 1)

                def weights(x):
                    act.wait_ge(s_spe, E + 4 + x)
                    act.activation(ssp[:, x, :], bank(2 + 3 * x, 3)[:, 0:CW], ACT.Exp).then_inc(s_sac, 1)

                hi(u + SB_R)
                softplus(0)
                hi(u + SB_G)
                softplus(1)
                act.wait_ge(s_free, A0["sb"] + SB_PAIR * p + SB_R + 1)
                act.activation(sgr[:, 1, :], sgr[:, 0, :], ACT.Exp, scale=-1.0).then_inc(s_sac, 1)
                hi(u + SB_G + 1)
                weights(0)
                if p < 3:
                    hi(u + SB_Q)
                    weights(1)
                    hi(u + SB_Q + 1)
                    hi(u + SB_V)
                else:
                    hi(U0["branch"])
                    weights(1)
            act.wait_ge(s_free, A0["branch"])
            for j in range(KD):
                if j:
                    hi(U0["branch"] + j)
                for m in range(2):
                    f = 2 * j + m
                    g, b = (gate(KD + f), 1) if j < 4 else (gate(f - KD), 0)
                    act.activation(g, g, ACT.Sigmoid,
                                   bias=par[:, 8 * (G_BG + b) + f % KD:8 * (G_BG + b) + f % KD + 1]).then_inc(s_sig, 1)
            residual("wout", 2, 4, 4, G_FFN, "wout")
            with act.Fori(0, KF // 2, 1) as i:
                for m in range(2):
                    hi(U0["ffin"] + 2 * m, i, 4)
                    hi(U0["ffin"] + 2 * m + 1, i, 4)
                    act.wait_ge(s_cv, at(m + 1, i, 2))
                    act.activation(gl[:, m, :], cv[:, m, :], ACT.Gelu_apprx_tanh).then_inc(s_ge, 1)
            residual("ffout", 2, 12, 4, None, "ffout")
            act.dma_start(wsf[:, :, :], wsT).then_inc(s_cld, 16)
            act.dma_start(bsb[:, :, :], bs.partition_broadcast(P)).then_inc(s_cld, 16)
            act.dma_start(lgb[:, :, :], lngb.partition_broadcast(P)).then_inc(s_cld, 16)
            for m in range(KD):
                act.wait_ge(s_rb, N0["ffout"] + 1)
                act.wait_ge(s_cv, KF + m + 1)
                x_hi(m, None, G_MIX2, S0["final1"] + m)
            rms("final1")
            act.wait_ge(s_cdv, 1)
            for f in range(2):
                for j in range(4):
                    hi(U0["cgv"] + 4 * f + j)
                act.wait_ge(s_unit, U0["cgv"] + 4 * f + 4)
                for t in range(NT):
                    act.activation(vt[:, t, f * T:(f + 1) * T], bank(2 + t), ACT.Gelu, scale=rtok[:, t:t + 1]).then_inc(s_cac, 1)
            act.wait_ge(s_cdv, 3)
            for t in range(NT):
                act.activation(mv[:, t, 2:3], mv[:, t, 1:2], ACT.Sqrt, bias=eps[:, 0:1]).then_inc(s_cac, 1)
            with act.Fori(0, 2, 1) as i:
                for m in range(4):
                    hi(U0["cgu"] + m, i, 4)
                    act.wait_ge(s_free, at(A0["cgu"] + m + 1, i, 4))
                    act.activation(uf[:, i * 4 + m, :], uf[:, i * 4 + m, :], ACT.Gelu).then_inc(s_cac, 1)
            residual("cgout", 2, 4, 4, G_MLP2, "cgout")

            def mlp(layer, g):
                for half in range(2):
                    up, dn = f"up{layer}{half}", f"down{layer}{half}"
                    k0 = 32 * layer + 16 * half
                    with act.Fori(0, 4, 1) as i:
                        for m in range(4):
                            hi(U0[up] + m, i, 4)
                            act.wait_ge(s_free, at(A0[up] + m + 1, i, 4))
                            act.activation(ms[:, m % 2, :], mr[:, m % 2, :], ACT.Square).then_inc(s_ms, 1)
                    if half == 0:
                        if layer == 0:
                            act.wait_ge(s_bdv, 2)
                            act.dma_start(fdram, fsb).then_inc(s_fst, 16)
                        with act.Fori(0, 2, 1) as i:
                            for m in range(8):
                                hi(U0[dn] + m, i, 8)
                        if layer == 0:
                            act.wait_ge(s_fst, 16)
                            for g in range(4):
                                src = bass.AP(tensor=fdram.tensor, offset=256 * g, ap=[[1, P], [1024, 8], [1, P]])
                                act.dma_start(bias[:, :, g * P:(g + 1) * P], src).then_inc(s_bld, 16)
                    elif layer == 0:
                        residual(dn, 2, 8, 4, g, "down01")
                    else:
                        for m in range(KD):
                            hi(U0[dn] + 2 * m)
                            hi(U0[dn] + 2 * m + 1)
                            act.wait_ge(s_free, A0[dn] + m + 1)
                            x_hi(m, None, None, S0["down11"] + m)
                        rms("down11")

            act.dma_start(ohs[0:32, 0:24], rb).then_inc(s_dld, 16)
            act.dma_start(ohs[:, 24:], onehot).then_inc(s_dld, 16)
            mlp(0, G_MIX2 + 1)

            def permute(p0, p1):
                act.wait_ge(s_dof, 4 * p1)
                for t in range(NT):
                    act.dma_start(oP[:, t, p0:p1, :], oB[96 - 32 * t:P - 32 * t, :, p0:p1, :]).then_inc(s_perm, 16)

            def factors(x, p0, p1):
                act.wait_ge(s_min, x + 1)
                for k in (1, 2):
                    ins = act.activation(cAB[:, k, :, p0:p1, :], cAB[:, k, :, p0:p1, :], ACT.Exp)
                ins.then_inc(s_mex, 1)

            def attend(k, q):
                n = STEP_AT.get(TICKS * k + q)
                if n is None:
                    return
                if LAG_T <= n < STEPS + LAG_T:
                    m = n - LAG_T
                    c0 = 0 if m % 4 or m // 8 % 2 else 128
                    act.wait_ge(s_dtr, m + 1)
                    if m >= 4:
                        act.wait_ge(s_dpv, m - 3)
                    act.activation(dpt[:, m % 4, 0, c0:], bank(4 + m % 2)[:, c0:256], ACT.Copy).then_inc(s_dhi, 1)
                if n < STEPS:
                    p, part, x, t = step_of(n)
                    o, tt = (oB, 3 - t) if part else (oA, t)
                    c0 = 0 if t or part else 128
                    act.wait_ge(s_dlg, n + 1)
                    if n >= 4:
                        act.wait_ge(s_dtr, n - 3)
                    act.activation(dp[:, n % 4, c0:], dl[:, n % 4, c0:], ACT.Exp, bias=o[:, tt, p, NMAX + x:NMAX + x + 1],
                                   accum_out=o[:, tt, p, DEN + x:DEN + x + 1]).then_inc(s_dac, 1)
                if n == PERMUTE_AT:
                    permute(0, 3)
                if n in OUT_UNITS:
                    hi(U0["dilout"] + OUT_UNITS.index(n))
                if n == MERGE_AT:
                    factors(0, 0, 3)

            for k in range(36):
                hi(U0["dil"] + k)
                for q in range(TICKS):
                    attend(k, q)
            for tick in range(TICKS * 36, LAST_TICK):
                attend(tick // TICKS, tick % TICKS)
            permute(3, 4)
            factors(1, 3, 4)
            for m in range(KD):
                if m == 1:
                    hi(U0["dilout"] + 3)
                act.wait_ge(s_free, A0["dilout"] + KD + m + 1)
                x_hi(m, None, G_MLP2 + 1, S0["dilout"] + m)
            rms("dilout")
            mlp(1, None)

        @block.vector
        def _(dve):
            chain = Chain(dve, s_dch)

            def lo(u, i=None, s=0):
                n = u + LOOK
                if n >= NU:
                    return
                dve.wait_ge(s_hi, at(n + 1, i, s))
                dve.tensor_tensor(wlo[:, n % SLOTS, :], raw[:, n % 2, :], whi[:, n % SLOTS, :].bitcast(F32),
                                  ALU.subtract).then_inc(s_split, 1)

            def x_lo(m, xn, g, i=None, s=0, mi=None):
                dve.wait_ge(s_xhi, at(xn + 1, i, s))
                gain = par[:, 8 * g + m:8 * g + m + 1] if mi is None else par[:, bass.ds(mi + 8 * g, 1)]
                dve.scalar_tensor_tensor(xlo[:, m, :], h[:, m, :], gain, xhi[:, m, :].bitcast(F32), ALU.mult,
                                         ALU.subtract).then_inc(s_x, 1)

            def inverse_rms(name):
                dve.wait_ge(s_nsq, N0[name] + 1)
                dve.reciprocal(rbc[:, :], rtmp[:, :]).then_inc(s_rb, 1)
                dve.wait_ge(s_rb, N0[name] + 1)

            def split(hi_, lo_, src, sem_=None):
                chain(dve.tensor_copy(hi_, src))
                ins = dve.tensor_tensor(lo_, src, hi_.bitcast(F32), ALU.subtract)
                if sem_ is None:
                    chain(ins)
                else:
                    ins.then_inc(sem_, 1)

            def residual(name, turns, nu, ng, g):
                u, a = U0[name], A0[name]
                step = nu // ng
                with dve.Fori(0, turns, 1) as i:
                    for m in range(ng):
                        for j in range(m * step, (m + 1) * step):
                            lo(u + j, i, nu)
                        dve.wait_ge(s_unit, at(u + (m + 1) * step, i, nu))
                        hm = h[:, i * ng + m, :]
                        dve.tensor_tensor(hm, hm, bank((a + m) % 2), ALU.add).then_inc(s_free, 1)
                        if g is not None:
                            x_lo(i * ng + m, X0[name] + m, g, i, ng, i * ng + m)

            def rows(u, a, dst, mul=rbc, op0=None, i=None, us=0):
                dve.wait_ge(s_unit, at(u + 1, i, us))
                dve.tensor_tensor(dst, bank(a % 2), mul[:, :], ALU.mult).then_inc(s_free, 1)

            dve.wait_ge(s_par, 64)
            dve.tensor_copy(trir[:, :, :], con[:, 1:3, :]).then_inc(s_con, 1)
            dve.wait_ge(s_h0, 16 * KD)
            for m in range(KD):
                x_lo(m, m, G_MIX)
                if m < LOOK:
                    lo(m - LOOK)
            inverse_rms("start")
            lo(0)
            rows(U0["ga"], A0["ga"], gt[:, 0, :])
            dve.wait_ge(s_free, 1)
            dve.tensor_copy(ga[:, :], gt[0:16, 0, :]).then_inc(s_gdv, 1)
            for what, p in GLA_PLAN:
                V, E = 1 + 13 * p, 12 * p
                if (what, p) in GLA_UNITS:
                    n = GLA_UNITS.index((what, p))
                    lo(U0["gla"] + n)
                    rows(U0["gla"] + n, A0["gla"] + n, gate(p) if what == "gate" else gf[:, ("q", "k", "va", "vb").index(what), :])
                elif what == "cumulate":
                    ba = par[:, C_BA + p:C_BA + p + 1]
                    dve.wait_ge(s_gac, 4 * p + 1)
                    chain(dve.tensor_scalar(gt[:, 0, :], bank(7), ba, 0.0, ALU.add, ALU.min))
                    chain(dve.tensor_tensor(gt[:, 0, :], gt[:, 0, :], gt[:, 1, :], ALU.subtract))
                    cum = gt[:, 2, :]
                    dve.tensor_tensor_scan(cum, smask[:, :], gt[:, 0, :], 0.0, ALU.mult, ALU.add).then_inc(s_gdv, 1)
                    dve.wait_ge(s_gdv, V + 1)
                    c3 = cum.rearrange("p (n c) -> p n c", c=GCH)
                    lastc = c3[:, :, GCH - 1:GCH].to_broadcast([P, 8, GCH])
                    dve.tensor_tensor(gt[:, 3, :].rearrange("p (n c) -> p n c", c=GCH), lastc, c3, ALU.subtract).then_inc(s_gdv, 1)
                elif what == "scale":
                    dve.wait_ge(s_gac, 4 * p + 2)
                    dve.wait_ge(s_free, A0["gla"] + GLA_UNITS.index(("k", p)) + 1)
                    chain(dve.scalar_tensor_tensor(gt[:, 0, :], gf[:, 0, :], DH ** -0.5, gt[:, 4, :], ALU.mult, ALU.mult))
                    split(gqk[:, 0, :], gqk[:, 1, :], gt[:, 0, :])
                    chain(dve.tensor_tensor(gt[:, 1, :], gf[:, 1, :], gt[:, 5, :], ALU.mult))
                    split(gqk[:, 2, :], gqk[:, 3, :], gt[:, 1, :])
                    dve.tensor_tensor(gt[:, 7, :], gf[:, 1, :], gt[:, 6, :], ALU.mult).then_inc(s_gdv, 1)
                elif what == "turn":
                    for n in range(3):
                        dve.wait_ge(s_gpe, E + 2 + n)
                        split(gtok[:, 2 * n, :], gtok[:, 2 * n + 1, :], bank(2 + n), s_gdv)
                    for x in range(2):
                        dve.wait_ge(s_gpe, E + 5 + x)
                        dve.tensor_copy(gatt[:, x, :], bank(5 + x)).then_inc(s_gat, 1)
                elif what == "states":
                    for x in range(2):
                        r = slice(64 * x, 64 * x + 64)
                        dve.wait_ge(s_gpe, E + 7 + x)
                        for n in range(1, 8):
                            ds = sbank(x, n - 1)[r, :]
                            if n == 1:
                                chain(dve.tensor_copy(gst[r, 1, :], ds))
                            else:
                                chain(dve.scalar_tensor_tensor(gst[r, n, :], gst[r, n - 1, :], gt[r, 4, n * GCH - 1:n * GCH], ds,
                                                               ALU.mult, ALU.add))
                    split(gstr[:, 0, 1:8, :], gstr[:, 1, 1:8, :], gst[:, 1:8, :], s_gdv)
                    for x in range(2):
                        dve.wait_ge(s_gpo, 2 * p + x + 1)
                        split(gatr[:, 2 * x, :], gatr[:, 2 * x + 1, :], gatt[:, x, :], s_gdv)
                elif what == "outputs":
                    for x in range(2):
                        dve.wait_ge(s_gpe, E + 9 + x)
                        o = o_gla[:, 2 * p + x, :]
                        chain(dve.tensor_copy(o, bank(5 + x)))
                        dve.tensor_tensor(gatt[:, x, :], o, o, ALU.mult).then_inc(s_gdv, 1)
                elif what == "norms":
                    for x in range(2):
                        dve.wait_ge(s_gac, 4 * p + 3 + x)
                        o = o_gla[:, 2 * p + x, :]
                        chain(dve.reciprocal(gt[:, x, :], gt[:, x, :]))
                        gg = par[:, C_GG + 2 * p + x:C_GG + 2 * p + x + 1]
                        dve.scalar_tensor_tensor(o, o, gg, gt[:, x, :], ALU.mult, ALU.mult).then_inc(s_gdv, 1)
            chain(dve.memset(svp[:, :, :, :, :].bitcast(F32), 0.0))

            def qk(u, a, p):
                for j in range(2):
                    lo(u + j)
                    dve.wait_ge(s_unit, u + j + 1)
                    if p and j == 0:
                        dve.wait_ge(s_sac, 5 * p - 3)
                    dst = sl[:, j * T:(j + 1) * T]
                    dve.scalar_tensor_tensor(dst, bank((a + j) % 2), DH ** -0.5 if j == 0 else 1.0, rbc[:, :], ALU.mult,
                                             ALU.mult).then_inc(s_free, 1)
                    dve.wait_ge(s_free, a + j + 1)
                    split(sqk[:, 2 * j, :], sqk[:, 2 * j + 1, :], dst, s_sqk)

            qk(U0["sb"], A0["sb"], 0)
            lo(U0["sb"] + 2)
            rows(U0["sb"] + 2, A0["sb"] + 2, svf[:, :])
            for p in range(4):
                u, a = U0["sb"] + SB_PAIR * p, A0["sb"] + SB_PAIR * p
                E, A = 6 * p, 5 * p

                def evacuated(j, dst):
                    lo(u + j)
                    rows(u + j, a + j, dst)

                dve.wait_ge(s_spe, E + 1)
                vv = bank(5).rearrange("p (c d) -> p c d", d=P)
                for x in range(2):
                    d = slice(64 * x, 64 * x + 64)
                    chain(dve.tensor_copy(svp[:, 0, x, :, d], vv[:, :, d]))
                    ins = dve.tensor_tensor(svp[:, 1, x, :, d], vv[:, :, d], svp[:, 0, x, :, d].bitcast(F32), ALU.subtract)
                    if x:
                        ins.then_inc(s_sdv, 1)
                    else:
                        chain(ins)

                def softplus(x):
                    dve.wait_ge(s_sac, A + 1 + x)
                    dve.scalar_tensor_tensor(ssp[:, x, :], bank(2 + 3 * x, 3)[:, 0:CW], 0.0, sl[:, :], ALU.max,
                                             ALU.add).then_inc(s_sdv, 1)
                    dve.wait_ge(s_spo, 4 * p + 1 + x)
                    split(sspr[:, 0, x, :], sspr[:, 1, x, :], ssp[:, x, :], s_sdv)

                def weights(x):
                    dve.wait_ge(s_spo, 4 * p + 3 + x)
                    split(sspr[:, 0, x, :], sspr[:, 1, x, :], ssp[:, x, :], s_sdv)

                def output():
                    dve.wait_ge(s_spe, E + 6)
                    dve.tensor_copy(o_sb[:, p, :], bank(2)).then_inc(s_sdv, 1)

                lo(u + SB_R)
                softplus(0)
                rows(u + SB_R, a + SB_R, sgr[:, 0, :])
                lo(u + SB_G)
                softplus(1)
                rows(u + SB_G, a + SB_G, gate(KD + 2 * p))
                dve.wait_ge(s_sac, A + 3)
                chain(dve.tensor_scalar(sgr[:, 1, :], sgr[:, 1, :], 1.0, None, ALU.add))
                chain(dve.reciprocal(sgr[:, 1, :], sgr[:, 1, :]))
                chain(dve.tensor_tensor(sgr[:, 1, :], sgr[:, 1, :], sgr[:, 0, :], ALU.mult))
                chain(dve.tensor_tensor(o_gla[:, p, :], o_gla[:, p, :], sgr[:, 1, :], ALU.mult))
                lo(u + SB_G + 1)
                weights(0)
                rows(u + SB_G + 1, a + SB_G + 1, gate(KD + 2 * p + 1))
                if p < 3:
                    weights(1)
                    qk(u + SB_Q, a + SB_Q, p + 1)
                    lo(u + SB_V)
                    output()
                    rows(u + SB_V, a + SB_V, svf[:, :])
                else:
                    for k in range(4):
                        split(xhi[:, 4 + k, :], xlo[:, 4 + k, :], o_gla[:, k, :], s_r)
                    lo(U0["branch"])
                    weights(1)
            for j in range(KD):
                u = U0["branch"] + j
                if j:
                    lo(u)
                dve.wait_ge(s_unit, u + 1)
                for m in range(2):
                    f, a = 2 * j + m, A0["branch"] + 2 * j + m
                    dve.wait_ge(s_sig, f + 1)
                    g = gate((f + KD) % (2 * KD))
                    dve.tensor_tensor(g, g, bank(a % 2), ALU.mult).then_inc(s_free, 1)
                    if j >= 4:
                        dve.wait_ge(s_free, a + 1)
                        chain(dve.tensor_tensor(yf[:, m, :], gate(f), g, ALU.add))
                        split(yr[:, 0, f - KD, :], yr[:, 1, f - KD, :], yf[:, m, :], s_r)
                if j == 1:
                    output()
                    dve.wait_ge(s_sdv, 32)
                    for k in range(4):
                        split(xhi[:, k, :], xlo[:, k, :], o_sb[:, k, :], s_r)
            residual("wout", 2, 4, 4, G_FFN)
            inverse_rms("wout")
            chain(dve.memset(apad[:, 0:2], 0.0))
            with dve.Fori(0, KF // 2, 1) as i:
                chain.loop(i, 2 * 4)
                for m in range(2):
                    u, a = U0["ffin"] + 2 * m, A0["ffin"] + 2 * m
                    tap = lambda k: par[:, bass.ds(i * 8 + (C_CONV + 4 * m + k), 1)]
                    lo(u, i, 4)
                    rows(u, a, apad[:, 2:], i=i, us=4)
                    dve.wait_ge(s_free, at(a + 1, i, 4))
                    t = cv[:, m, :]
                    chain(dve.tensor_scalar(t, apad[:, 2:], tap(2), tap(3), ALU.mult, ALU.add))
                    chain(dve.scalar_tensor_tensor(t, apad[:, 1:T + 1], tap(1), t, ALU.mult, ALU.add))
                    dve.scalar_tensor_tensor(t, apad[:, 0:T], tap(0), t, ALU.mult, ALU.add).then_inc(s_cv, 1)
                    lo(u + 1, i, 4)
                    rows(u + 1, a + 1, gs[:, :], i=i, us=4)
                    dve.wait_ge(s_ge, at(m + 1, i, 2))
                    dve.wait_ge(s_free, at(a + 2, i, 4))
                    chain(dve.tensor_tensor(gl[:, m, :], gl[:, m, :], gs[:, :], ALU.mult))
                    k = i * 2 + m
                    split(hid[:, 0, k, :], hid[:, 1, k, :], gl[:, m, :], s_r)
                chain.end(KF // 2)
            residual("ffout", 2, 12, 4, None)
            inverse_rms("ffout")
            dve.wait_ge(s_sqd, S0["final1"])
            for m in range(KD):
                dve.scalar_tensor_tensor(h[:, m, :], h[:, m, :], par[:, 8 * G_FIN + m:8 * G_FIN + m + 1], rbc[:, :],
                                         ALU.mult, ALU.mult).then_inc(s_cv, 1)
                if m:
                    dve.wait_ge(s_cv, KF + m)
                    x_lo(m - 1, X0["final1"] + m - 1, G_MIX2)
            dve.wait_ge(s_cv, KF + KD)
            x_lo(KD - 1, X0["final1"] + KD - 1, G_MIX2)
            inverse_rms("final1")
            dve.wait_ge(s_cpe, 1)
            for t in range(NT):
                ins = dve.tensor_copy(rtok[:, t:t + 1], bank(2 + t)[:, 0:1])
            ins.then_inc(s_cdv, 1)
            dve.wait_ge(s_cpo, 1)
            split(wsr[:, 0, :, :], wsr[:, 1, :, :], wsf[:, :, :], s_cdv)
            dve.wait_ge(s_cld, 48)
            for j in range(8):
                lo(U0["cgv"] + j)
                if j == 4 or j == 7:
                    pass
            for t in range(NT):
                for f in range(2):
                    dve.wait_ge(s_cac, NT * f + t + 1)
                    ins = dve.bn_stats(st6[:, t, f, :], vt[:, t, f * T:(f + 1) * T])
                    chain(ins)
                ins = dve.bn_aggr(mv[:, t, 0:2], st6[:, t, :, :].rearrange("p a b -> p (a b)"))
                if t < NT - 1:
                    chain(ins)
                else:
                    ins.then_inc(s_cdv, 1)
            for t in range(NT):
                dve.wait_ge(s_cac, 8 + t + 1)
                v = vt[:, t, :]
                chain(dve.reciprocal(mv[:, t, 3:4], mv[:, t, 2:3]))
                chain(dve.tensor_scalar(v, v, mv[:, t, 0:1], mv[:, t, 3:4], ALU.subtract, ALU.mult))
                chain(dve.tensor_tensor(v, v, lgb[:, 0, :], ALU.mult))
                chain(dve.tensor_tensor(v, v, lgb[:, 1, :], ALU.add))
                split(vr[:, 0, t, :], vr[:, 1, t, :], v, s_r)
            dve.wait_ge(s_r, R0["ug"])
            with dve.Fori(0, 2, 1) as i:
                for m in range(4):
                    lo(U0["cgu"] + m, i, 4)
                    rows(U0["cgu"] + m, A0["cgu"] + m, uf[:, i * 4 + m, :], i=i, us=4)
            for g in range(KD):
                dve.wait_ge(s_cpe, 2 + g)
                dve.wait_ge(s_cac, 12 + g + 1)
                b4 = bank(2 + g % 4).rearrange("p (t c) -> p t c", c=P)
                m4 = rtm[:, g % 2, :].rearrange("p (t c) -> p t c", c=P)
                row = bsb[:, g:g + 1, :].to_broadcast([P, NT, P])
                dve.tensor_tensor(m4, b4, row, ALU.add).then_inc(s_cdv, 1)
                dve.wait_ge(s_cdv, 4 + g)
                chain(dve.tensor_tensor(uf[:, g, :], uf[:, g, :], rtm[:, g % 2, :], ALU.mult))
                split(ugr[:, 0, g, :], ugr[:, 1, g, :], uf[:, g, :], s_r)
            residual("cgout", 2, 4, 4, G_MLP2)
            inverse_rms("cgout")

            def mlp(layer, g):
                for half in range(2):
                    up, dn = f"up{layer}{half}", f"down{layer}{half}"
                    k0 = 32 * layer + 16 * half
                    with dve.Fori(0, 4, 1) as i:
                        chain.loop(i, 4)
                        for m in range(4):
                            lo(U0[up] + m, i, 4)
                            dve.wait_ge(s_unit, at(U0[up] + m + 1, i, 4))
                            dve.scalar_tensor_tensor(mr[:, m % 2, :], bank((A0[up] + m) % 2), 0.0, rbc[:, :], ALU.max,
                                                     ALU.mult).then_inc(s_free, 1)
                            dve.wait_ge(s_ms, at(k0 + m + 1, i, 4))
                            k = i * 4 + m
                            split(mh[:, 0, k, :], mh[:, 1, k, :], ms[:, m % 2, :], s_r)
                        chain.end(4)
                    if half == 0:
                        if layer == 0:
                            dve.wait_ge(s_bmm, 1)
                            dve.tensor_copy(fsb[:, :], bank(2, 2)[0:8, :]).then_inc(s_bdv, 1)
                        residual(dn, 2, 8, 4, None)
                    elif layer == 0:
                        residual_x(dn, g, "down01")
                    else:
                        for m in range(KD):
                            lo(U0[dn] + 2 * m)
                            lo(U0[dn] + 2 * m + 1)
                            dve.wait_ge(s_unit, U0[dn] + 2 * m + 2)
                            hm = h[:, m, :]
                            dve.tensor_tensor(hm, hm, bank((A0[dn] + m) % 2), ALU.add).then_inc(s_free, 1)
                inverse_rms("down01" if layer == 0 else "down11")

            def residual_x(dn, g, name):
                residual(dn, 2, 8, 4, g)

            dve.memset(ohs[32:33, 0:24], NEG).then_inc(s_bdv, 1)
            mlp(0, G_MIX2 + 1)
            def out_of_bank(k):
                p, g, j = k // 9, k // 3 % 3, k % 3
                u, a = U0["dil"] + k, A0["dil"] + k
                if j == 2:
                    rows(u, a, dvf[:, :])
                    return
                dve.wait_ge(s_unit, u + 1)
                dst = mtmp[:, j, :]
                back = dst if j else dst[:, ::-1]
                dve.scalar_tensor_tensor(back, bank(a % 2), DH ** -0.5 if j == 0 else 1.0, rbc[:, :], ALU.mult,
                                         ALU.mult).then_inc(s_free, 1)
                dve.wait_ge(s_free, a + 1)
                if p and j == 0:
                    dve.wait_ge(s_dlo, 16 * p - (0 if g else 8))
                split(dqk[:, g, 2 * j, :], dqk[:, g, 2 * j + 1, :], dst, s_dqk)

            def merge(x, p0, p1):
                ps = slice(p0, p1)
                dve.wait_ge(s_perm, 64 * (x + 1))

                def c(k):
                    return cAB[:, k, :, ps, :]

                nA, nB = oA[:, :, ps, NMAX:ROW], oP[:, :, ps, NMAX:ROW]
                dA, dB = oA[:, :, ps, DEN:NMAX], oP[:, :, ps, DEN:NMAX]
                chain(dve.tensor_tensor(c(0), nA, nB, ALU.min))
                chain(dve.tensor_tensor(c(1), c(0), nA, ALU.subtract))
                dve.tensor_tensor(c(2), c(0), nB, ALU.subtract).then_inc(s_min, 1)
                dve.wait_ge(s_mex, x + 1)
                chain(dve.tensor_tensor(dA, dA, c(1), ALU.mult))
                chain(dve.tensor_tensor(dB, dB, c(2), ALU.mult))
                chain(dve.tensor_tensor(dA, dA, dB, ALU.add))
                chain(dve.reciprocal(c(3), dA))
                chain(dve.tensor_tensor(c(1), c(1), c(3), ALU.mult))
                ins = dve.tensor_tensor(c(2), c(2), c(3), ALU.mult)
                if x == 0:
                    ins.then_inc(s_fac, 1)
                    return
                chain(ins)
                a, b = weigh(dve, p0)
                chain(b)
                ins = dve.tensor_tensor(oA[:, :, p0, 0:DEN], oA[:, :, p0, 0:DEN], oP[:, :, p0, 0:DEN], ALU.add)
                ins.then_inc(s_mrg, 1)

            def add_part(m, part):
                if m < KD - 1:
                    dve.wait_ge(s_dop, (KD - 1) * part + m + 1)
                else:
                    dve.wait_ge(s_unit, U0["dilout"] + 3 + part)
                if part and m == 0:
                    dve.wait_ge(s_free, A0["dilout"] + KD)
                dve.tensor_tensor(h[:, m, :], h[:, m, :], bank(m % 2), ALU.add).then_inc(s_free, 1)

            def outputs_split(j, b):
                dve.wait_ge(s_otr, j + 1)
                b3 = bank(b).rearrange("p (t q) -> p t q", q=P)[:, :, ::-1]
                o_hi, o_lo = (o.rearrange("p (t q) -> p t q", q=P) for o in out_pair(j))
                split(o_hi, o_lo, b3, s_r)

            def attend(k, q):
                if k and k % 3 == 0 and q == 2:
                    v = k // 3 - 1
                    dve.wait_ge(s_dtv, v + 1)
                    if v >= 3:
                        dve.wait_ge(s_dpv, 16 * (v // 3) - (0 if v % 3 else 8))
                    split(dvt[:, v % 3, 0, :], dvt[:, v % 3, 1, :], bank(7), s_dvs)
                n = STEP_AT.get(TICKS * k + q)
                if n is None:
                    return
                if n < STEPS:
                    p, part, x, t = step_of(n)
                    o, tt = (oB, 3 - t) if part else (oA, t)
                    c0 = 0 if t or part else 128
                    b0 = 256 * part
                    dve.wait_ge(s_dlo, n + 1)
                    if n >= 4:
                        dve.wait_ge(s_dac, n - 3)
                    chain(dve.tensor_tensor(dl[:, n % 4, c0:], bank(2 + n % 2)[:, c0:256], bias[:, 2 * p + x, b0 + c0:b0 + 256], ALU.add))
                    dve.tensor_reduce(o[:, tt, p, NMAX + x:NMAX + x + 1], dl[:, n % 4, c0:], AX, ALU.max, negate=True).then_inc(s_dlg, 1)
                if LAG_T <= n < STEPS + LAG_T:
                    m = n - LAG_T
                    c0 = 0 if m % 4 or m // 8 % 2 else 128
                    dve.wait_ge(s_dhi, m + 1)
                    dve.tensor_tensor(dpt[:, m % 4, 1, c0:], bank(4 + m % 2)[:, c0:256], dpt[:, m % 4, 0, c0:].bitcast(F32),
                                      ALU.subtract).then_inc(s_dsp, 1)
                if n >= LAG_V and n % 4 == 3:
                    m = n - LAG_V
                    p, part, x, t = step_of(m)
                    dve.wait_ge(s_dpv, m + 1)
                    o3 = bank(6)[:, 0:256].rearrange("p (t d) -> p t d", d=DH)
                    o = oB[:, ::-1] if part else oA
                    dve.tensor_copy(o[:, :, p, x * DH:(x + 1) * DH], o3).then_inc(s_dof, 1)
                if n in OUT_UNITS:
                    lo(U0["dilout"] + OUT_UNITS.index(n))
                if OUT_AT < n <= OUT_AT + KD:
                    add_part(n - OUT_AT - 1, 0)
                if n == MERGE_AT:
                    merge(0, 0, 3)
                if n in SPLIT_AT:
                    j = SPLIT_AT.index(n)
                    outputs_split(j, (0, 1, 7)[j])

            dve.wait_ge(s_bld, 64)
            for k in range(37):
                for q in range(TICKS):
                    if q == 0 and k:
                        out_of_bank(k - 1)
                    if q == 1 and k < 36:
                        lo(U0["dil"] + k)
                    attend(k, q)
            for tick in range(TICKS * 37, LAST_TICK):
                attend(tick // TICKS, tick % TICKS)
            merge(1, 3, 4)
            outputs_split(3, 2)
            add_part(0, 1)
            for m in range(KD):
                if m < KD - 1:
                    add_part(m + 1, 1)
                x_lo(m, X0["dilout"] + m, G_MLP2 + 1)
            lo(U0["dilout"] + 3)
            inverse_rms("dilout")
            mlp(1, None)
            for m in range(KD):
                dve.scalar_tensor_tensor(h[:, m, :], h[:, m, :], par[:, 8 * G_FIN2 + m:8 * G_FIN2 + m + 1], rbc[:, :],
                                         ALU.mult, ALU.mult).then_inc(s_fin, 1)

        @block.gpsimd
        def _(pool):
            chain = Chain(pool, s_pch)

            def sum_squares(name):
                for m in range(KD):
                    n = S0[name] + m
                    pool.wait_ge(s_sqd, n + 1)
                    if m == 0:
                        ins = pool.tensor_copy(ssum[:, :], sq[:, 0, :])
                    else:
                        pool.wait_ge(s_ss, n)
                        ins = pool.tensor_tensor(ssum[:, :], ssum[:, :], sq[:, n % 2, :], ALU.add)
                    ins.then_inc(s_ss, 1)

            pool.memset(eps[:, :], EPS).then_inc(s_con, 1)
            sum_squares("start")
            for p in range(2):
                for x in range(2):
                    pool.wait_ge(s_gat, 2 * p + x + 1)
                    a3 = gatt[:, x, :].rearrange("p (t c) -> p t c", c=P)
                    chain(pool.affine_select(out=a3, in_=a3, pattern=[[0, NT], [1, P]], compare_op=ALU.is_ge, fill=0.0,
                                             base=0, channel_multiplier=-1))
                    pool.memset(a3[0:GCH, :, GCH:P], 0.0).then_inc(s_gpo, 1)
            for p in range(4):
                for n in range(4):
                    x = n % 2
                    if n < 2:
                        pool.wait_ge(s_sdv, 8 * p + 2 + 2 * x)
                    else:
                        pool.wait_ge(s_sac, 5 * p + 4 + x)
                    for c in range(NT):
                        d = ssp[:, x, CO[c]:CO[c] + P]
                        ins = pool.affine_select(out=d, in_=d, pattern=[[1, P]], compare_op=ALU.is_gt, fill=0.0, base=0,
                                                 channel_multiplier=-1)
                    ins.then_inc(s_spo, 1)
            sum_squares("wout")
            sum_squares("ffout")
            pool.wait_ge(s_cld, 48)
            pool.affine_select(out=wsf[:, :, :], in_=wsf[:, :, :], pattern=[[0, KD], [1, P]], compare_op=ALU.is_ge, fill=0.0,
                               base=0, channel_multiplier=-1).then_inc(s_cpo, 1)
            sum_squares("final1")
            sum_squares("cgout")
            sum_squares("down01")
            pool.wait_ge(s_fac, 1)
            for p in range(3):
                a, b = weigh(pool, p)
                chain(b)
                o = oA[:, :, p, 0:DEN]
                pool.tensor_tensor(o, o, oP[:, :, p, 0:DEN], ALU.add).then_inc(s_pmr, 1)
            sum_squares("dilout")
            sum_squares("down11")


def bucket(distance):
    n, exact = 32, 16
    nf = np.maximum(distance, 1).astype(np.float32)
    large = exact + (np.log(nf / np.float32(exact)) / np.float32(math.log(2048 / exact)) * np.float32(n - exact)).astype(np.int32)
    return np.where(distance < exact, distance, np.minimum(large, n - 1))


def one_hot():
    col = np.arange(256)
    out = np.zeros((33, 4, 256), np.float32)
    for g in range(4):
        rel = (P if g == 0 else 0) + P - 1 - col
        ok = (rel >= 0) & (rel <= P)
        if g == 3:
            ok &= rel % 4 == 0
        row = np.where(ok, bucket(np.clip(rel, 0, P) * (1 if g < 2 else 4)), 32)
        out[row, g, col] = 1.0
    return out.reshape(33, 1024)


def constants():
    i = np.arange(P)
    keep = np.tile((np.arange(T) % GCH != 0).astype(np.float32), (P, 1))
    tri = -(i[:, None] >= i[None, :]).astype(np.float32)
    one = np.ones((P, P), np.float32)
    return np.concatenate([np.eye(P, dtype=np.float32), tri, -one, one, keep], 1)


def units(w, k_tiles=UT):
    K, M = w.shape
    n = -(-K // (P * k_tiles))
    if K < n * P * k_tiles:
        w = np.concatenate([w, np.zeros((n * P * k_tiles - K, M), w.dtype)], 0)
    return w.reshape(n, k_tiles, P, M // P, P).transpose(3, 0, 2, 1, 4).reshape(n * M // P, P, k_tiles * P)


def wide_units(w):
    return w.reshape(4, P, -1, 2, P).transpose(2, 1, 3, 0, 4).reshape(-1, P, UT * P)


def stream(a):
    w = a["w_in"][0]
    out = [units(w[:, OFF_GA:OFF_GA + P])]
    first = {"q": lambda p: OFF_GQ + P * p, "k": lambda p: OFF_GK + P * p, "va": lambda p: OFF_GV + 2 * P * p,
             "vb": lambda p: OFF_GV + 2 * P * p + P, "gate": lambda f: OFF_G0 + P * f}
    cols = [first[what](p) for what, p in GLA_UNITS] + [o for o in (OFF_Q, OFF_K, OFF_V)]
    for p in range(4):
        cols += [OFF_GR + P * p, OFF_G1 + 2 * P * p, OFF_G1 + 2 * P * p + P]
        cols += [o + P * (p + 1) for o in (OFF_Q, OFF_K, OFF_V)] if p < 3 else []
    out += [units(w[:, c:c + P]) for c in cols]
    out += [wide_units(a["w_branch_gla"][0]), wide_units(a["w_branch_sb"][0]), units(a["w_out"][0])]
    f = a["w_ffn_in"][0]
    out += [np.stack([units(f[:, :FF]), units(f[:, FF:])], 1).reshape(-1, P, UT * P), units(a["w_ffn_out"][0])]
    w = a["a_w_in_2"][0]
    v = w[:, D:].reshape(4, 2, P, 2, T).transpose(3, 0, 2, 1, 4).reshape(8, P, UT * P)
    out += [v, units(w[:, :D]), units(a["a_w_out_2"][0])]

    def mlp(n):
        up, down = a["w_up_2"][n], a["w_down_2"][n]
        return [x for s in (0, FF2 // 2) for x in (units(up[:, s:s + FF2 // 2]), units(down[s:s + FF2 // 2]))]

    out += mlp(0)
    w = a["b_w_qkv_2"][0]
    for p in range(4):
        for g in range(3):
            out += [units(w[:, 1536 * c + 512 * g + P * p:1536 * c + 512 * g + P * (p + 1)]) for c in range(3)]
    t = wide_units(a["b_w_out_2"][0]).reshape(4, P, 2, 4, P).transpose(0, 2, 3, 1, 4).reshape(KD, 4, P, P)
    t = np.concatenate([t[:, :3].reshape(-1, P, P), t[:, 3]], 0)
    out += [t.reshape(4, UT, P, P).transpose(0, 2, 1, 3).reshape(4, P, UT * P)] + mlp(1)
    out = np.concatenate(out, 0)
    assert out.shape[0] == NU
    return out


def columns(v):
    return v.reshape(-1, P).T


def params(a):
    g2 = a["mix_norm_g_2"], a["mlp_norm_g_2"]
    rows = [a["norm_mix_g"][0], a["norm_ffn_g"][0], a["norm_final_g"], g2[0][0], g2[0][1], g2[1][0], g2[1][1],
            a["final_norm_g_2"], a["b_gate"][0, 0], a["b_gate"][0, 1]]
    conv = np.concatenate([a["conv_w"][0], a["conv_b"]], 0).reshape(4, KF, P).transpose(2, 1, 0).reshape(P, 4 * KF)
    return np.concatenate([columns(r) for r in rows] + [conv, columns(a["b_alpha"][0]), columns(a["gla_norm_g"][0])], 1)


def kernel(**inputs):
    import concourse.bacc as bacc
    from concourse.bass_utils import run_bass_kernel_spmd

    a = {k: np.asarray(v) for k, v in inputs.items()}
    arrays = {
        "wst": stream(a),
        "xT": a["x"][0].T.reshape(KD, P, T),
        "prm": params(a),
        "cst": constants(),
        "wup": a["w_alpha_up"][0],
        "wsT": a["a_w_s_2"][0].transpose(2, 0, 1),
        "bs": a["a_b_s_2"][0],
        "lngb": np.stack([a["a_ln_g_2"][0], a["a_ln_b_2"][0]]),
        "rb": a["rel_bias_2"],
        "onehot": one_hot(),
    }
    arrays = {k: np.ascontiguousarray(v) for k, v in arrays.items()}
    nc = bacc.Bacc("TRN2", target_bir_lowering=False, num_devices=1)
    args = [nc.dram_tensor(n, v.shape, mybir.dt.from_np(v.dtype), kind="ExternalInput").ap() for n, v in arrays.items()]
    fdram = nc.dram_tensor("bias_rows", (8, 1024), F32, kind="Internal").ap()
    out = nc.dram_tensor("out", (KD, P, T), F32, kind="ExternalOutput").ap()
    build(nc, *args, fdram, out)
    r = run_bass_kernel_spmd(nc, [arrays], core_ids=[0])
    got = r.results[0]["out"]
    return np.ascontiguousarray(got.reshape(D, T).T).reshape(1, T, D)
```

```python
import math
from contextlib import ExitStack

import numpy as np

import concourse.bass as bass
from concourse import mybir

F32 = mybir.dt.float32
F32R = mybir.dt.float32r
ALU = mybir.AluOpType
ACT = mybir.ActivationFunctionType
AX = mybir.AxisListType.X

P = 128
T = 512
D = 1024
KD = D // P
EPS = 1e-6
NT = T // P
FF = 2816
KF = FF // P
FF2 = 4096
SLOTS = 4
LOOK = SLOTS - 1
UT = 8
DH = 64
VG = 128
GCH = 64
TAU = 16.0
NEG = -1e30

OFF_Q, OFF_K, OFF_V = 0, 512, 1024
OFF_GQ, OFF_GK, OFF_GV, OFF_GR, OFF_GA = 1536, 1792, 2048, 2560, 3072
OFF_G0 = 3088
OFF_G1 = OFF_G0 + D

GLA_PLAN = [("q", 0), ("decay", 0), ("k", 0), ("cumulate", 0), ("va", 0), ("scale", 0), ("vb", 0), ("gate", 0),
            ("turn", 0), ("gate", 1), ("states", 0), ("gate", 2), ("q", 1), ("decay", 1), ("k", 1), ("outputs", 0),
            ("norms", 0), ("cumulate", 1), ("normed", 0), ("va", 1), ("scale", 1), ("vb", 1), ("normed", 1),
            ("gate", 3), ("turn", 1), ("gate", 4), ("states", 1), ("gate", 5), ("gate", 6), ("outputs", 1),
            ("norms", 1), ("gate", 7)]
GLA_UNITS = [e for e in GLA_PLAN if e[0] in ("q", "k", "va", "vb", "gate")]
N_GLA, N_SB = len(GLA_UNITS), 24
SB_R, SB_G, SB_Q, SB_V, SB_PAIR = 3, 4, 6, 8, 6
STREAM = [("ga", 1), ("gla", N_GLA), ("sb", N_SB), ("branch", 8), ("wout", 8), ("ffin", 2 * KF), ("ffout", 3 * KD),
          ("cgv", 8), ("cgu", 8), ("cgout", 8),
          ("up00", 16), ("down00", 16), ("up01", 16), ("down01", 16),
          ("dil", 36), ("dilout", 4),
          ("up10", 16), ("down10", 16), ("up11", 16), ("down11", 16)]
U0 = {}
NU = 0
for _name, _n in STREAM:
    U0[_name] = NU
    NU += _n

A0 = {}
NA = 0
for _name, _n in [("ga", 1), ("gla", N_GLA), ("sb", N_SB), ("branch", 16), ("wout", 8), ("ffin", 2 * KF), ("ffout", 8),
                  ("cgu", 8), ("cgout", 8), ("up00", 16), ("down00", 8), ("up01", 16), ("down01", 8),
                  ("dil", 36), ("dilout", 16), ("up10", 16), ("down10", 8), ("up11", 16), ("down11", 8)]:
    A0[_name] = NA
    NA += _n

X_SPLITS = ["wout", "final1", "cgout", "down01", "dilout"]
SQUARES = ["start", "wout", "ffout", "final1", "cgout", "down01", "dilout", "down11"]
X0 = {n: KD * (i + 1) for i, n in enumerate(X_SPLITS)}
S0 = {n: KD * i for i, n in enumerate(SQUARES)}
N0 = {n: i for i, n in enumerate(SQUARES)}

R0 = {}
_n = 0
for _name, _c in [("ogla", 4), ("osb", 4), ("y", 8), ("ffin", KF), ("v", 4), ("ug", 8), ("up00", 16), ("up01", 16),
                  ("dilo", 4), ("up10", 16), ("up11", 16)]:
    R0[_name] = _n
    _n += _c

G_MIX, G_FFN, G_FIN, G_MIX2, G_MLP2, G_FIN2, G_BG = 0, 1, 2, 3, 5, 7, 8
C_CONV = 80
C_BA = C_CONV + 4 * KF
C_GG = C_BA + 2
NP = C_GG + 4

BRANCH_BANKS = (0, 1, 3, 4)
CG_BANKS = (2, 3, 4, 5), (6, 7, 2, 3)

CO = {0: 0, 1: 512, 3: 896, 2: 1024}
CW = 1280

LOGIT = 512
DEN, NMAX, ROW = 2 * DH, 2 * DH + 2, 2 * DH + 4

TICKS, LAG_T, LAG_V = 4, 2, 4
STEPS = 64
STEP_AT = {}
for _p in range(4):
    for _s in range(8):
        STEP_AT[TICKS * (9 * _p + 3) + 3 * _s] = 16 * _p + _s
        STEP_AT[TICKS * (9 * _p + 9) + (3 * _s // 2 if _p < 3 else _s)] = 16 * _p + 8 + _s
PERMUTE_AT, MERGE_AT = 52, 53
TRANSPOSE_AT, SPLIT_AT, OUT_AT = 56, (57, 58, 59), 61


for _s in range(STEPS, OUT_AT + KD + 1):
    STEP_AT[TICKS * 36 + 8 + _s - STEPS] = _s
LAST_TICK = TICKS * 36 + 8 + OUT_AT + KD + 1 - STEPS
OUT_UNITS = (60, OUT_AT + 4, OUT_AT + 7)


def step_of(n):
    return n // 16, n // 8 % 2, n // 4 % 2, n % 4


def at(base, i=None, step=0):
    return base if i is None else i * step + base


class Chain:

    def __init__(self, eng, sem):
        self.eng, self.sem, self.n, self.i, self.step = eng, sem, 0, None, 0

    def __call__(self, ins):
        self.n += 1
        ins.then_inc(self.sem, 1)
        self.eng.wait_ge(self.sem, at(self.n, self.i, self.step))

    def loop(self, i, step):
        self.i, self.step, self.first = i, step, self.n

    def end(self, turns):
        assert self.n == self.first + self.step, (self.n - self.first, self.step)
        self.n = self.first + self.step * turns
        self.i = None


def build(nc, wst, xT, prm, cst, wup, wsT, bs, lngb, rb, onehot, fdram, out):
    es = ExitStack()
    with es:
        def sb(name, shape, dt=F32, st=es):
            return st.enter_context(nc.sbuf_tensor(name, shape, dt))

        def sem(name):
            return es.enter_context(nc.semaphore(name))

        raw = sb("raw", [P, 2, UT * P])
        whi = sb("whi", [P, SLOTS, UT * P], F32R)
        wlo = sb("wlo", [P, SLOTS, UT * P], F32R)
        h = sb("h", [P, KD, T])
        xhi = sb("xhi", [P, KD, T], F32R)
        xlo = sb("xlo", [P, KD, T], F32R)
        par = sb("par", [P, NP])
        con = sb("con", [P, 4, P])
        ident, ones = con[:, 0, :], con[:, 3, :]
        trir = sb("trir", [P, 2, P], F32R)
        rbc = sb("rbc", [P, T])
        rtmp = sb("rtmp", [P, T])
        ssum = sb("ssum", [P, T])
        sq = sb("sq", [P, 2, T])
        eps = sb("eps", [P, 1])
        rtok = sb("rtok", [P, NT])
        PS = es.enter_context(nc.psum_tensor("ps", [P, 8 * T], F32))

        def bank(b, n=1):
            return PS[:, b * T:(b + n) * T]

        with ExitStack() as m1:
            o_gla = sb("o_gla", [P, 4, T], F32, m1)
            gate_a = sb("gate_a", [P, KD, T], F32, m1)
            with ExitStack() as m:
                ga = sb("ga", [16, T], F32, m)
                wu = sb("wu", [16, 2 * P], F32, m)
                smask = sb("smask", [P, T], F32, m)
                gf = sb("gf", [P, 4, T], F32, m)
                gst = sb("gst", [P, 8, P], F32, m)
                gatt = sb("gatt", [P, 2, T], F32, m)
                gt = sb("gt", [P, 8, T], F32, m)
                gqk = sb("gqk", [P, 4, T], F32R, m)
                gtok = sb("gtok", [P, 6, T], F32R, m)
                gatr = sb("gatr", [P, 4, T], F32R, m)
                gstr = sb("gstr", [P, 2, 8, P], F32R, m)
            gate_b = sb("gate_b", [P, KD, T], F32, m1)
            o_sb = sb("o_sb", [P, 4, T], F32, m1)
            with ExitStack() as m:
                sqk = sb("sqk", [P, 4, T], F32R, m)
                svf = sb("svf", [P, T], F32, m)
                svp = sb("svp", [P, 2, 2, NT, P], F32R, m)
                sl = sb("sl", [P, CW], F32, m)
                ssp = sb("ssp", [P, 2, CW], F32, m)
                sspr = sb("sspr", [P, 2, 2, CW], F32R, m)
                sgr = sb("sgr", [P, 2, T], F32, m)
            with ExitStack() as m:
                yf = sb("yf", [P, 2, T], F32, m)
                yr = sb("yr", [P, 2, KD, T], F32R, m)
        with ExitStack() as m:
            hid = sb("hid", [P, 2, KF, T], F32R, m)
            apad = sb("apad", [P, T + 2], F32, m)
            cv = sb("cv", [P, 2, T], F32, m)
            gl = sb("gl", [P, 2, T], F32, m)
            gs = sb("gs", [P, T], F32, m)
        with ExitStack() as m:
            wsr = sb("wsr", [P, 2, KD, P], F32R, m)
            wsf = sb("wsf", [P, KD, P], F32, m)
            bsb = sb("bsb", [P, KD, P], F32, m)
            lgb = sb("lgb", [P, 2, D], F32, m)
            vt = sb("vt", [P, NT, D], F32, m)
            vr = sb("vr", [P, 2, NT, D], F32R, m)
            ugh = sb("ugh", [P, KD, T], F32R, m)
            with ExitStack() as m2:
                uf = sb("uf", [P, KD, T], F32, m2)
            ugl = sb("ugl", [P, KD, T], F32R, m)
            st6 = sb("st6", [P, NT, 2, 6], F32, m)
            mv = sb("mv", [P, NT, 4], F32, m)
            rtm = lgb[:, :, 0:T]
        with ExitStack() as m:
            mh = sb("mh", [P, 2, 16, T], F32R, m)
            mr = sb("mr", [P, 2, T], F32, m)
            ms = sb("ms", [P, 2, T], F32, m)
        with ExitStack() as m:
            oA = sb("oA", [P, NT, 4, ROW], F32, m)
            oB = sb("oB", [P, NT, 4, ROW], F32, m)
            oP = sb("oP", [P, NT, 4, ROW], F32, m)
            dqk = sb("dqk", [P, 3, 4, T], F32R, m)
            dvt = sb("dvt", [P, 3, 2, T], F32R, m)
            mtmp = sb("mtmp", [P, 2, T], F32, m)
            dvf = sb("dvf", [P, T], F32, m)
            dl = sb("dl", [P, 4, 256], F32, m)
            cAB = sb("cAB", [P, 4, NT, 4, 2], F32, m)
            sb("behind_mlp", [P, 36 * T - 3 * NT * 4 * ROW - 23 * T - NT * 32], F32, m)
            bias = sb("bias", [P, 8, LOGIT], F32, m)
            ohs = sb("ohs", [33, 24 + 4 * 256], F32, m)
            dp = sb("dp", [P, 4, 256], F32, m)
            dpt = sb("dpt", [P, 4, 2, 256], F32R, m)
            fsb = dp[0:8, :, :].rearrange("p a b -> p (a b)")
            orr = [dqk[:, 0, 0:2, :], dqk[:, 0, 2:4, :], None, dqk[:, 1, 0:2, :]]

        def gate(f):
            return gate_a[:, f, :] if f < KD else gate_b[:, f - KD, :]

        def ogla_pair(k):
            return (sqk[:, 2 * k, :], sqk[:, 2 * k + 1, :]) if k < 2 else (xhi[:, 4 + k, :], xlo[:, 4 + k, :])

        def out_pair(j):
            return (xhi[:, 0, :], xlo[:, 0, :]) if j == 2 else (orr[j][:, 0, :], orr[j][:, 1, :])

        def weigh(eng, p):
            return [eng.tensor_tensor(o, o, cAB[:, k, :, p, :].unsqueeze(3).to_broadcast([P, NT, 2, DH]), ALU.mult)
                    for k, o in ((k, tile[:, :, p, 0:DEN].rearrange("p t (x d) -> p t x d", d=DH)) for k, tile in ((1, oA), (2, oP)))]

        def hl(tile, k):
            return tile[:, 0, k, :], tile[:, 1, k, :]

        s_raw = [sem("raw0_loaded"), sem("raw1_loaded")]
        s_hi = sem("unit_hi_done")
        s_split = sem("unit_split_done")
        s_unit = sem("unit_multiplied")
        s_par = sem("params_loaded")
        s_h0 = [sem(f"h{m}_loaded") for m in range(KD)]
        s_pin = sem("decay_inputs_loaded")
        s_con = sem("constants_made")
        s_free = sem("acc_bank_free")
        s_xhi = sem("x_hi_done")
        s_x = sem("x_split_done")
        s_sqd = sem("square_done")
        s_ss = sem("square_summed")
        s_nmm = sem("mean_square_multiplied")
        s_nsq = sem("rms_done")
        s_rb = sem("inverse_rms_done")
        s_r = sem("operand_split_done")
        s_dch = sem("vector_chain")
        s_ach = sem("scalar_chain")
        s_pch = sem("pool_chain")
        s_gat = sem("gla_scores_copied")
        s_gdm = sem("decay_multiplied")
        s_gdc = sem("decay_vector_done")
        s_gad = sem("decay_scalar_done")
        s_gdn = sem("gla_outputs_normed")
        s_yad = sem("branches_added")
        s_lnd = sem("v_normalized")
        s_lng = sem("v_gain_applied")
        s_svz = sem("sb_values_zeroed")
        s_gpe = sem("gla_multiplied")
        s_gdv = sem("gla_vector_done")
        s_gac = sem("gla_scalar_done")
        s_gpo = sem("gla_masked")
        s_sqk = sem("sb_qk_split")
        s_spe = sem("sb_multiplied")
        s_sdv = sem("sb_vector_done")
        s_sac = sem("sb_scalar_done")
        s_spo = sem("sb_masked")
        s_sig = sem("gate_sigmoid_done")
        s_cv = sem("conv_done")
        s_ge = sem("gelu_done")
        s_cpe = sem("chunk_gating_multiplied")
        s_cdv = sem("chunk_gating_vector_done")
        s_cac = sem("chunk_gating_gelu_done")
        s_cpo = sem("chunk_gating_masked")
        s_cld = sem("chunk_gating_params_loaded")
        s_ms = sem("relu_squared")
        s_dld = sem("bias_inputs_loaded")
        s_fst = sem("bias_rows_stored")
        s_bld = sem("bias_loaded")
        s_bmm = sem("bias_rows_multiplied")
        s_bdv = sem("bias_rows_copied")
        s_dqk = sem("dilated_qk_split")
        s_dtv = sem("dilated_v_transposed")
        s_dvs = sem("dilated_v_split")
        s_dlo = sem("dilated_logits_multiplied")
        s_dof = sem("dilated_outputs_copied")
        s_min = sem("dilated_maxima_compared")
        s_mex = sem("merge_factors_done")
        s_fac = sem("first_merge_factors_ready")
        s_pmr = sem("first_pairs_merged")
        s_mrg = sem("dilated_merged")
        s_dop = sem("dilated_projection_part")
        s_otr = sem("dilated_outputs_transposed")
        s_dtr = sem("dilated_transposed")
        s_dpv = sem("dilated_values_multiplied")
        s_dlg = sem("dilated_logits_done")
        s_dac = sem("dilated_exp_done")
        s_dhi = sem("dilated_probs_hi_done")
        s_dsp = sem("dilated_probs_split")
        s_perm = sem("dilated_rows_permuted")
        s_out = sem("out_stored")
        s_fin = sem("out_ready")

        block = es.enter_context(nc.Block())

        def sbank(x, n):
            return bank((2, 3, 4, 7)[2 * x + n % 2])[:, (n // 2) * P:(n // 2 + 1) * P]

        def mm3(pe, o, w, x, first, done, **kw):
            pe.matmul(o, w[0], x[0], start=first, stop=False, **kw)
            pe.matmul(o, w[1], x[0], start=False, stop=False, **kw)
            return pe.matmul(o, w[0], x[1], start=False, stop=done, **kw)

        @block.sync
        def _(sp):
            sp.dma_start(raw[:, 0, :], wst[0]).then_inc(s_raw[0], 16)
            sp.dma_start(raw[:, 1, :], wst[1]).then_inc(s_raw[1], 16)
            sp.wait_ge(s_split, 1)
            sp.dma_start(raw[:, 0, :], wst[2]).then_inc(s_raw[0], 16)
            with sp.Fori(0, (NU - 3) // 2, 1) as i:
                for j in range(2):
                    n = 3 + j
                    sp.wait_ge(s_split, at(n - 1, i, 2))
                    sp.dma_start(raw[:, n % 2, :], wst[2 * i + n]).then_inc(s_raw[n % 2], 16)
            for m in range(KD):
                sp.wait_ge(s_fin, m + 1)
                sp.dma_start(out[m], h[:, m, :]).then_inc(s_out, 16)
            sp.wait_ge(s_out, 16 * KD)

        @block.tensor
        def _(pe):
            def unit_ready(u, i=None, s=0):
                pe.wait_ge(s_split, at(u + 1, i, s))

            def w_tile(slot, t, n=P):
                return whi[:, slot, t * P:t * P + n], wlo[:, slot, t * P:t * P + n]

            def acc_wait(a, i=None, s=0):
                if a >= 2:
                    pe.wait_ge(s_free, at(a - 1, i, s))

            def x_tile(k):
                return xhi[:, k, :], xlo[:, k, :]

            def dense(u, a, groups, xs, i=None, us=0, as_=0, tick=None, banks=(0, 1)):
                flat = [(g, t) for g, ts in enumerate(groups) for t in ts]
                for n, (g, (j, t, k)) in enumerate(flat):
                    if n == 0 or flat[n - 1][1][0] != j:
                        unit_ready(u + j, i, us)
                    first = n == 0 or flat[n - 1][0] != g
                    end = n + 1 == len(flat) or flat[n + 1][0] != g
                    if first:
                        acc_wait(a + g - (len(banks) - 2), i, as_)
                    ins = mm3(pe, bank(banks[(a + g) % len(banks)]), w_tile((u + j) % SLOTS, t), xs(k), first, end)
                    if n + 1 == len(flat) or flat[n + 1][1][0] != j:
                        ins.then_inc(s_unit, 1)
                    if tick and n % 2:
                        tick(n // 2)

            def full(n_units):
                return [[(j, k, k) for k in range(UT)] for j in range(n_units)]

            def fresh(xs, made, count):
                def tile(k):
                    pe.wait_ge(made, count + k + 1)
                    return xs(k)
                return tile

            def loop(name, turns, nu, groups, xs, made, count, before=None):
                u, a, g = U0[name], A0[name], len(groups)
                assert nu % SLOTS == 0 and g % 2 == 0
                dense(u, a, groups[:1], fresh(xs, made, count))
                if before:
                    norm(before)
                dense(u, a + 1, groups[1:], xs)
                with pe.Fori(1, turns, 1) as i:
                    dense(u, a, groups, xs, i, nu, g)

            def norm(name):
                pe.wait_ge(s_ss, S0[name] + KD)
                pe.matmul(bank(7), ones, ssum[:, :], start=True, stop=True).then_inc(s_nmm, 1)

            pe.wait_ge(s_con, 2)
            pe.wait_ge(s_par, 32)
            dense(U0["ga"], A0["ga"], full(1), fresh(x_tile, s_x, 0))
            norm("start")
            def decay(p):
                if p == 0:
                    pe.wait_ge(s_pin, 32)
                pe.wait_ge(s_gdv, 5 if p else 1)
                pe.matmul(bank(7), wu[:, p * P:(p + 1) * P], ga[:, :], start=True, stop=True).then_inc(s_gdm, 1)

            def turn(p):
                pe.wait_ge(s_free, A0["gla"] + GLA_UNITS.index(("vb", p)) + 1)
                pe.wait_ge(s_gdc, 3 * p + 3)
                if p:
                    pe.wait_ge(s_gdv, 9)
                    pe.wait_ge(s_gac, 2)
                for n, src in enumerate((gt[:, 7, :], gf[:, 2, :], gf[:, 3, :])):
                    for t in range(NT):
                        ins = pe.transpose(bank(2 + n)[:, t * P:(t + 1) * P], src[:, t * P:(t + 1) * P], ident)
                    ins.then_inc(s_gpe, 1)
                for x in range(2):
                    r = slice(64 * x, 64 * x + 64)
                    for t in range(NT):
                        c = slice(t * P, (t + 1) * P)
                        ins = mm3(pe, bank(5 + x)[:, c], (gqk[r, 2, c], gqk[r, 3, c]), (gqk[r, 0, c], gqk[r, 1, c]),
                                  t == 0, True, skip_group_check=True)
                    ins.then_inc(s_gpe, 1)

            def states(p):
                pe.wait_ge(s_gdv, 1 + 8 * p + 3)
                for x in range(2):
                    for n in range(7):
                        r = slice(64 * (n % 2), 64 * (n % 2) + 64)
                        c = slice((n // 2) * P, (n // 2 + 1) * P)
                        ins = mm3(pe, sbank(x, n),
                                  (gtok[r, 0, c], gtok[r, 1, c]), (gtok[r, 2 + 2 * x, c], gtok[r, 3 + 2 * x, c]),
                                  n < 2, True, skip_group_check=True)
                    ins.then_inc(s_gpe, 1)

            def outputs(p):
                pe.wait_ge(s_gdv, 1 + 8 * p + 6)
                for x in range(2):
                    r = slice(64 * x, 64 * x + 64)
                    for t in range(NT):
                        c = slice(t * P, (t + 1) * P)
                        mm3(pe, bank(5 + x)[:, c], (gtok[:, 2 + 2 * x, c], gtok[:, 3 + 2 * x, c]),
                            (gatr[:, 2 * x, c], gatr[:, 2 * x + 1, c]), t == 0, True, skip_group_check=True)
                    for n in range(1, 8):
                        c = slice(n * GCH, (n + 1) * GCH)
                        ins = mm3(pe, bank(5 + x)[:, c], (gstr[r, 0, n, :], gstr[r, 1, n, :]),
                                  (gqk[r, 0, c], gqk[r, 1, c]), False, True, skip_group_check=True)
                    ins.then_inc(s_gpe, 1)

            def norms(p):
                for x in range(2):
                    pe.wait_ge(s_gdv, 1 + 8 * p + 7 + x)
                    pe.matmul(bank(2 + x), ones, gatt[:, x, :], start=True, stop=True).then_inc(s_gpe, 1)

            for what, p in GLA_PLAN:
                if (what, p) in GLA_UNITS:
                    n = GLA_UNITS.index((what, p))
                    dense(U0["gla"] + n, A0["gla"] + n, full(1), x_tile)
                elif what == "decay":
                    decay(p)
                elif what == "turn":
                    turn(p)
                elif what == "states":
                    states(p)
                elif what == "outputs":
                    outputs(p)
                elif what == "norms":
                    norms(p)
            def branch(n, count):
                if n == 1:
                    pe.wait_ge(s_free, A0["branch"])
                    pe.wait_ge(s_sac, 19)
                    pe.wait_ge(s_r, R0["osb"])
                for j in range(n - 1, n - 1 + count):
                    dense(U0["branch"] + j, A0["branch"] + 2 * j, [[(0, 4 * m + k, k) for k in range(4)] for m in range(2)],
                          (lambda k: ogla_pair(k)) if j < 4 else x_tile, banks=BRANCH_BANKS)

            pe.wait_ge(s_gdv, 17)
            pe.wait_ge(s_gac, 4)
            for p in range(4):
                u, a = U0["sb"] + SB_PAIR * p, A0["sb"] + SB_PAIR * p
                V, A = 8 * p, 5 * p

                def units(j, n=1):
                    dense(u + j, a + j, full(n), x_tile)

                def scores(x):
                    r = slice(64 * x, 64 * x + 64)
                    z = bank(2 + 3 * x, 3)
                    for c in (0, 1, 3, 2):
                        ins = mm3(pe, z[:, CO[c]:CO[c] + T - P * c], (sqk[r, 2, c * P:(c + 1) * P], sqk[r, 3, c * P:(c + 1) * P]),
                                  (sqk[r, 0, c * P:], sqk[r, 1, c * P:]), c != 3, True, skip_group_check=True)
                    ins.then_inc(s_spe, 1)

                def tails(x):
                    z = bank(2 + 3 * x, 3)
                    for c in range(NT):
                        for d in range(c, NT):
                            o = z[:, CO[c] + P * (d - c):CO[c] + T - P * c]
                            w = trir[:, 0 if d == c else 1, :]
                            for part in range(2):
                                ins = pe.matmul(o, w, sspr[:, part, x, CO[d]:CO[d] + T - P * d], start=False,
                                                stop=True, skip_group_check=True)
                    ins.then_inc(s_spe, 1)

                if p == 0:
                    units(0, 3)
                else:
                    pe.wait_ge(s_sac, A)
                pe.wait_ge(s_free, a + 3)
                for c in range(NT):
                    ins = pe.transpose(bank(5)[:, c * P:(c + 1) * P], svf[:, c * P:(c + 1) * P], ident)
                ins.then_inc(s_spe, 1)
                pe.wait_ge(s_sqk, 2 * p + 2)
                if p:
                    pe.wait_ge(s_sdv, V)
                scores(0)
                units(SB_R)
                pe.wait_ge(s_sdv, V + 1)
                scores(1)
                units(SB_G)
                pe.wait_ge(s_sdv, V + 3)
                tails(0)
                units(SB_G + 1)
                pe.wait_ge(s_sdv, V + 5)
                tails(1)
                if p < 3:
                    units(SB_Q, 2)
                else:
                    branch(1, 2)
                pe.wait_ge(s_sdv, V + 7)
                for x in range(2):
                    for c in range(NT):
                        ins = mm3(pe, bank(2)[:, c * P:], (svp[:, 0, x, c, :], svp[:, 1, x, c, :]),
                                  (sspr[:, 0, x, CO[c]:CO[c] + T - P * c], sspr[:, 1, x, CO[c]:CO[c] + T - P * c]),
                                  x == 0 and c == 0, True, skip_group_check=True)
                ins.then_inc(s_spe, 1)
                if p < 3:
                    units(SB_V)
            branch(3, 2)
            pe.wait_ge(s_r, R0["y"])
            branch(5, 4)
            loop("wout", 2, 4, full(4), lambda k: hl(yr, k), s_r, R0["y"])
            loop("ffin", KF // 2, 4, full(4), x_tile, s_x, X0["wout"], "wout")
            down = [[(3 * m + k // UT, k % UT, k) for k in range(KF)] for m in range(4)]
            loop("ffout", 2, 12, down, lambda k: hl(hid, k), s_r, R0["ffin"])
            norm("ffout")
            for f in range(2):
                for j in range(4):
                    u = U0["cgv"] + 4 * f + j
                    unit_ready(u)
                    for kk in range(2):
                        k = 2 * j + kk
                        if f == 0:
                            pe.wait_ge(s_x, X0["final1"] + k + 1)
                        for t in range(NT):
                            if f and k == 0 and t == 1:
                                pe.wait_ge(s_cdv, 1)
                            if f and k == 0 and t >= 2:
                                pe.wait_ge(s_cac, t - 1)
                            c = slice(t * P, (t + 1) * P)
                            ins = mm3(pe, bank(CG_BANKS[f][t]), (xhi[:, k, c], xlo[:, k, c]),
                                      (whi[:, u % SLOTS, kk * T:(kk + 1) * T], wlo[:, u % SLOTS, kk * T:(kk + 1) * T]),
                                      k == 0, k == KD - 1)
                    ins.then_inc(s_unit, 1)
                    if f == 0 and j == 1:
                        norm("final1")
                    if f == 0 and j == 3:
                        pe.wait_ge(s_rb, N0["final1"] + 1)
                        for t in range(NT):
                            ins = pe.transpose(bank(7)[:, t * P:(t + 1) * P], rbc[:, t * P:(t + 1) * P], ident)
                        ins.then_inc(s_cpe, 1)
            dense(U0["cgu"], A0["cgu"], full(8), x_tile)
            pe.wait_ge(s_r, R0["ug"])
            pe.wait_ge(s_cdv, 2)
            for g in range(KD):
                if g >= 4:
                    pe.wait_ge(s_cdv, g)
                for t in range(NT):
                    ins = mm3(pe, bank(2 + g % 4)[:, t * P:(t + 1) * P], (vr[:, 0, t, g * P:(g + 1) * P], vr[:, 1, t, g * P:(g + 1) * P]),
                              (wsr[:, 0, g, :], wsr[:, 1, g, :]), t == 0, True, skip_group_check=True)
                ins.then_inc(s_cpe, 1)
            loop("cgout", 2, 4, full(4), lambda k: (ugh[:, k, :], ugl[:, k, :]), s_r, R0["ug"])

            def bias_rows():
                pe.wait_ge(s_dld, 32)
                pe.wait_ge(s_bdv, 1)
                for g in range(4):
                    grp = max(0, g - 1)
                    ins = pe.matmul(bank(2 + g // 2)[0:8, (g % 2) * 256:(g % 2) * 256 + 256], ohs[:, 8 * grp:8 * grp + 8],
                                    ohs[:, 24 + g * 256:24 + (g + 1) * 256], start=g % 2 == 0, stop=True, skip_group_check=True)
                ins.then_inc(s_bmm, 1)

            def mlp(layer, before):
                m_t = lambda k: hl(mh, k)
                for half in range(2):
                    loop(f"up{layer}{half}", 4, 4, full(4), x_tile, s_x, X0[before], None if half else before)
                    if layer == 0 and half == 0:
                        bias_rows()
                    groups = [[(2 * m + k // UT, k % UT, k) for k in range(16)] for m in range(4)]
                    loop(f"down{layer}{half}", 2, 8, groups, m_t, s_r, R0[f"up{layer}{half}"])

            mlp(0, "cgout")
            def logits(n):
                p, part, x, t = step_of(n)
                r = slice(64 * x, 64 * x + 64)
                b = bank(2 + n % 2)
                if n % 8 == 0:
                    pe.wait_ge(s_dqk, 2 * (3 * p + (3 if part else 1)))
                if n >= 2:
                    pe.wait_ge(s_dlg, n - 1)
                if part == 0:
                    c = slice(T - (t + 1) * P, T - t * P)
                    k0 = (t - 1) * P if t else 0
                    ins = mm3(pe, b[:, 0:256] if t else b[:, 128:256], (dqk[r, 0, 0, c], dqk[r, 0, 1, c]),
                              (dqk[r, 0, 2, k0:(t + 1) * P], dqk[r, 0, 3, k0:(t + 1) * P]), True, True, skip_group_check=True)
                else:
                    for g in (1, 2):
                        ins = mm3(pe, b[:, 128 * (g - 1):128 * g], (dqk[r, g, 0, 3 - t::4], dqk[r, g, 1, 3 - t::4]),
                                  (dqk[r, g, 2, t::4], dqk[r, g, 3, t::4]), g == 1, True, skip_group_check=True)
                ins.then_inc(s_dlo, 1)

            def turned(n):
                p, part, x, t = step_of(n)
                pe.wait_ge(s_dac, n + 1)
                if n >= 2:
                    pe.wait_ge(s_dsp, n - 1)
                for j in range(0 if part or t else 1, 2):
                    ins = pe.transpose(bank(4 + n % 2)[:, j * P:(j + 1) * P], dp[:, n % 4, j * P:(j + 1) * P], ident)
                ins.then_inc(s_dtr, 1)

            def sums(n):
                p, part, x, t = step_of(n)
                pe.wait_ge(s_dsp, n + 1)
                if n % 8 == 0:
                    pe.wait_ge(s_dvs, 3 * p + (3 if part else 1))
                if t == 0 and n:
                    pe.wait_ge(s_dof, n // 4)
                first = t == 0
                for j in range(0 if part or t else 1, 2):
                    g = j + 1 if part else 0
                    kt = t - 1 + j if part == 0 else t
                    v = slice(kt * P + 64 * x, kt * P + 64 * x + 64)
                    ins = mm3(pe, bank(6)[:, t * 64:(t + 1) * 64],
                              (dpt[:, n % 4, 0, j * P:(j + 1) * P], dpt[:, n % 4, 1, j * P:(j + 1) * P]),
                              (dvt[:, g, 0, v], dvt[:, g, 1, v]), first, True, skip_group_check=True)
                    first = False
                ins.then_inc(s_dpv, 1)

            def outputs_turned(j, b):
                for t in range(NT):
                    ins = pe.transpose(bank(b)[:, t * P:(t + 1) * P], oA[:, t, j, 0:DEN], ident)
                ins.then_inc(s_otr, 1)

            def attend(k, q):
                if k and k % 3 == 0 and q == 1:
                    v = k // 3 - 1
                    pe.wait_ge(s_free, A0["dil"] + k)
                    if v:
                        pe.wait_ge(s_dvs, v)
                    for t in range(NT):
                        src = dvf[:, t * P:(t + 1) * P] if v % 3 == 0 else dvf[:, t::4]
                        ins = pe.transpose(bank(7)[:, t * P:(t + 1) * P], src, ident)
                    ins.then_inc(s_dtv, 1)
                n = STEP_AT.get(TICKS * k + q)
                if n is None:
                    return
                if LAG_T <= n < STEPS + LAG_T:
                    turned(n - LAG_T)
                if LAG_V <= n < STEPS + LAG_V:
                    sums(n - LAG_V)
                if n < STEPS:
                    logits(n)
                if OUT_AT <= n < OUT_AT + KD:
                    m = n - OUT_AT
                    pe.wait_ge(s_r, R0["dilo"] + 3)
                    for k in range(3):
                        u, f = U0["dilout"] + (3 * m + k) // UT, (3 * m + k) % UT
                        if k == 0 or f == 0:
                            unit_ready(u)
                        if k == 0:
                            acc_wait(A0["dilout"] + m)
                        ins = mm3(pe, bank((A0["dilout"] + m) % 2), w_tile(u % SLOTS, f), out_pair(k), k == 0, k == 2)
                        if f == UT - 1:
                            ins.then_inc(s_unit, 1)
                    if m < KD - 1:
                        ins.then_inc(s_dop, 1)
                if n == TRANSPOSE_AT:
                    pe.wait_ge(s_pmr, 3)
                    pe.wait_ge(s_free, A0["dil"] + 36)
                    for j in range(2):
                        outputs_turned(j, j)
                if n == TRANSPOSE_AT + 2:
                    pe.wait_ge(s_dvs, 12)
                    outputs_turned(2, 7)

            for k in range(36):
                xs = x_tile if k else fresh(x_tile, s_x, X0["down01"])
                dense(U0["dil"] + k, A0["dil"] + k, full(1), xs, tick=lambda q: attend(k, q))
                if k == 0:
                    norm("down01")
            for tick in range(TICKS * 36, LAST_TICK):
                attend(tick // TICKS, tick % TICKS)
            pe.wait_ge(s_mrg, 1)
            outputs_turned(3, 2)
            pe.wait_ge(s_r, R0["up10"])
            u = U0["dilout"] + 3
            unit_ready(u)
            for m in range(KD):
                acc_wait(A0["dilout"] + KD + m)
                ins = mm3(pe, bank((A0["dilout"] + m) % 2), w_tile(u % SLOTS, m), out_pair(3), True, True)
                ins.then_inc(s_dop if m < KD - 1 else s_unit, 1)
            mlp(1, "dilout")
            norm("down11")

        @block.scalar
        def _(act):
            chain = Chain(act, s_ach)

            def hi(u, i=None, s=0):
                n = u + LOOK
                if n >= NU:
                    return
                act.wait_ge(s_raw[n % 2], at(16 * (n // 2 + 1), i, 8 * s))
                if n >= SLOTS:
                    act.wait_ge(s_unit, at(n - SLOTS + 1, i, s))
                act.activation(whi[:, n % SLOTS, :], raw[:, n % 2, :], ACT.Copy).then_inc(s_hi, 1)

            def x_hi(m, xn, g, sn, i=None, s=0, mi=None):
                hm = h[:, m, :]
                if sn >= 2:
                    act.wait_ge(s_ss, at(sn - 1, i, s))
                if g is not None:
                    act.activation(xhi[:, m, :], hm, ACT.Copy, scale=par[:, 8 * g + m:8 * g + m + 1] if mi is None else
                                   par[:, bass.ds(mi + 8 * g, 1)]).then_inc(s_xhi, 1)
                elif i is not None:
                    act.wait_ge(s_h0[0], 16)
                act.activation(sq[:, sn % 2, :], hm, ACT.Square).then_inc(s_sqd, 1)

            def rms(name):
                act.wait_ge(s_nmm, N0[name] + 1)
                act.activation(rtmp[:, :], bank(7), ACT.Sqrt, bias=eps[:, 0:1], scale=1.0 / D).then_inc(s_nsq, 1)

            def residual(name, turns, nu, ng, g, first=0):
                u, a, sn = U0[name], A0[name], S0[first]
                step = nu // ng if nu >= ng else 1
                with act.Fori(0, turns, 1) as i:
                    for m in range(ng):
                        for j in range(m * step, (m + 1) * step):
                            hi(u + j, i, nu)
                        act.wait_ge(s_free, at(a + m + 1, i, ng))
                        x_hi(i * ng + m, None, g, sn + m, i, ng, i * ng + m)
                rms(first)

            act.dma_start(par[:, :], prm).then_inc(s_par, 16)
            act.dma_start(con[:, :, :], cst[:, 0:4 * P].rearrange("p (a b) -> p a b", a=4)).then_inc(s_par, 16)
            for m in range(KD):
                act.dma_start(h[:, m, :], xT[m]).then_inc(s_h0[m], 16)
            act.dma_start(wu[:, :], wup).then_inc(s_pin, 16)
            act.dma_start(smask[:, :], cst[:, 4 * P:4 * P + T]).then_inc(s_pin, 16)
            act.wait_ge(s_par, 32)
            act.wait_ge(s_con, 2)
            for m in range(KD):
                act.wait_ge(s_h0[m], 16)
                x_hi(m, None, G_MIX, m)
                if m < LOOK:
                    hi(m - LOOK)
            rms("start")
            hi(0)
            for what, p in GLA_PLAN:
                if (what, p) in GLA_UNITS:
                    hi(U0["gla"] + GLA_UNITS.index((what, p)))
                elif what == "decay":
                    ba = par[:, C_BA + p:C_BA + p + 1]
                    act.wait_ge(s_gdm, p + 1)
                    if p:
                        act.wait_ge(s_gdc, 3 * p)
                    chain(act.activation(gt[:, 1, :], bank(7), ACT.Abs, bias=ba))
                    chain(act.activation(gt[:, 1, :], gt[:, 1, :], ACT.Exp, scale=-1.0))
                    act.activation(gt[:, 1, :], gt[:, 1, :], ACT.Ln, bias=1.0).then_inc(s_gad, 1)
                elif what == "cumulate":
                    act.wait_ge(s_gdc, 3 * p + 2)
                    if p:
                        act.wait_ge(s_gdv, 5)
                    act.activation(gt[:, 4, :], gt[:, 2, :], ACT.Exp, scale=1 / TAU)
                    act.activation(gt[:, 5, :], gt[:, 2, :], ACT.Exp, scale=-1 / TAU)
                    act.activation(gt[:, 6, :], gt[:, 3, :], ACT.Exp, scale=1 / TAU).then_inc(s_gad, 1)
                elif what == "norms":
                    for x in range(2):
                        act.wait_ge(s_gpe, 11 * p + 10 + x)
                        act.activation(gatt[:, x, :], bank(2 + x), ACT.Sqrt, bias=eps[:, 0:1], scale=1.0 / VG).then_inc(s_gac, 1)
            for j in range(3):
                hi(U0["sb"] + j)
            for p in range(4):
                u = U0["sb"] + SB_PAIR * p
                V, E = 8 * p, 6 * p

                def softplus(x):
                    act.wait_ge(s_spe, E + 2 + x)
                    if p or x:
                        act.wait_ge(s_sdv, V + 2 if x else V - 4)
                    z = bank(2 + 3 * x, 3)[:, 0:CW]
                    chain(act.activation(sl[:, :], z, ACT.Abs))
                    chain(act.activation(sl[:, :], sl[:, :], ACT.Exp, scale=-1.0))
                    act.activation(sl[:, :], sl[:, :], ACT.Ln, bias=1.0).then_inc(s_sac, 1)

                def weights(x):
                    act.wait_ge(s_spe, E + 4 + x)
                    act.activation(ssp[:, x, :], bank(2 + 3 * x, 3)[:, 0:CW], ACT.Exp).then_inc(s_sac, 1)

                hi(u + SB_R)
                softplus(0)
                hi(u + SB_G)
                softplus(1)
                act.wait_ge(s_free, A0["sb"] + SB_PAIR * p + SB_R + 1)
                act.activation(sgr[:, 1, :], sgr[:, 0, :], ACT.Sigmoid).then_inc(s_sac, 1)
                hi(u + SB_G + 1)
                weights(0)
                if p < 3:
                    hi(u + SB_Q)
                    weights(1)
                    hi(u + SB_Q + 1)
                    hi(u + SB_V)
                else:
                    hi(U0["branch"])
                    weights(1)
            act.wait_ge(s_free, A0["branch"])
            for j in range(KD):
                if j:
                    hi(U0["branch"] + j)
                for m in range(2):
                    f = 2 * j + m
                    g, b = (gate(KD + f), 1) if j < 4 else (gate(f - KD), 0)
                    act.activation(g, g, ACT.Sigmoid,
                                   bias=par[:, 8 * (G_BG + b) + f % KD:8 * (G_BG + b) + f % KD + 1]).then_inc(s_sig, 1)
            residual("wout", 2, 4, 4, G_FFN, "wout")
            with act.Fori(0, KF // 2, 1) as i:
                for m in range(2):
                    hi(U0["ffin"] + 2 * m, i, 4)
                    hi(U0["ffin"] + 2 * m + 1, i, 4)
                    act.wait_ge(s_cv, at(m + 1, i, 2))
                    act.activation(gl[:, m, :], cv[:, m, :], ACT.Gelu_apprx_tanh).then_inc(s_ge, 1)
            residual("ffout", 2, 12, 4, None, "ffout")
            act.dma_start(wsf[:, :, :], wsT).then_inc(s_cld, 16)
            act.dma_start(bsb[:, :, :], bs.partition_broadcast(P)).then_inc(s_cld, 16)
            act.dma_start(lgb[:, :, :], lngb.partition_broadcast(P)).then_inc(s_cld, 16)
            for m in range(KD):
                act.wait_ge(s_rb, N0["ffout"] + 1)
                act.wait_ge(s_cv, KF + m + 1)
                x_hi(m, None, G_MIX2, S0["final1"] + m)
            hi(U0["cgv"])
            rms("final1")
            for f in range(2):
                for j in range(4):
                    if f or j:
                        hi(U0["cgv"] + 4 * f + j)
                if f == 0:
                    act.wait_ge(s_cdv, 1)
                act.wait_ge(s_unit, U0["cgv"] + 4 * f + 4)
                for t in range(NT):
                    act.activation(vt[:, t, f * T:(f + 1) * T], bank(CG_BANKS[f][t]), ACT.Gelu, scale=rtok[:, t:t + 1]).then_inc(s_cac, 1)
            act.wait_ge(s_cdv, 3)
            for t in range(NT):
                act.activation(mv[:, t, 2:3], mv[:, t, 1:2], ACT.Sqrt, bias=eps[:, 0:1]).then_inc(s_cac, 1)
            for m in range(KD):
                hi(U0["cgu"] + m)
                act.wait_ge(s_free, A0["cgu"] + m + 1)
                act.activation(uf[:, m, :], uf[:, m, :], ACT.Gelu).then_inc(s_cac, 1)
            residual("cgout", 2, 4, 4, G_MLP2, "cgout")

            def mlp(layer, g):
                for half in range(2):
                    up, dn = f"up{layer}{half}", f"down{layer}{half}"
                    with act.Fori(0, 4, 1) as i:
                        for m in range(4):
                            hi(U0[up] + m, i, 4)
                            act.wait_ge(s_free, at(A0[up] + m + 1, i, 4))
                            act.activation(ms[:, m % 2, :], mr[:, m % 2, :], ACT.Square).then_inc(s_ms, 1)
                    if half == 0:
                        if layer == 0:
                            act.wait_ge(s_bdv, 2)
                            act.dma_start(fdram, fsb).then_inc(s_fst, 16)
                        with act.Fori(0, 2, 1) as i:
                            for m in range(8):
                                hi(U0[dn] + m, i, 8)
                        if layer == 0:
                            act.wait_ge(s_fst, 16)
                            for g in range(4):
                                src = bass.AP(tensor=fdram.tensor, offset=256 * g, ap=[[1, P], [1024, 8], [1, P]])
                                act.dma_start(bias[:, :, g * P:(g + 1) * P], src).then_inc(s_bld, 16)
                    elif layer == 0:
                        residual(dn, 2, 8, 4, g, "down01")
                    else:
                        for m in range(KD):
                            hi(U0[dn] + 2 * m)
                            hi(U0[dn] + 2 * m + 1)
                            act.wait_ge(s_free, A0[dn] + m + 1)
                            x_hi(m, None, None, S0["down11"] + m)
                        rms("down11")

            act.dma_start(ohs[0:32, 0:24], rb).then_inc(s_dld, 16)
            act.dma_start(ohs[:, 24:], onehot).then_inc(s_dld, 16)
            mlp(0, G_MIX2 + 1)

            def permute(p0, p1):
                act.wait_ge(s_dof, 4 * p1)
                for t in range(NT):
                    act.dma_start(oP[:, t, p0:p1, :], oB[96 - 32 * t:P - 32 * t, :, p0:p1, :]).then_inc(s_perm, 16)

            def factors(x, p0, p1):
                act.wait_ge(s_min, x + 1)
                for k in (1, 2):
                    ins = act.activation(cAB[:, k, :, p0:p1, :], cAB[:, k, :, p0:p1, :], ACT.Exp)
                ins.then_inc(s_mex, 1)

            def attend(k, q):
                n = STEP_AT.get(TICKS * k + q)
                if n is None:
                    return
                if LAG_T <= n < STEPS + LAG_T:
                    m = n - LAG_T
                    c0 = 0 if m % 4 or m // 8 % 2 else 128
                    act.wait_ge(s_dtr, m + 1)
                    if m >= 4:
                        act.wait_ge(s_dpv, m - 3)
                    act.activation(dpt[:, m % 4, 0, c0:], bank(4 + m % 2)[:, c0:256], ACT.Copy).then_inc(s_dhi, 1)
                if n < STEPS:
                    p, part, x, t = step_of(n)
                    o, tt = (oB, 3 - t) if part else (oA, t)
                    c0 = 0 if t or part else 128
                    act.wait_ge(s_dlg, n + 1)
                    if n >= 4:
                        act.wait_ge(s_dtr, n - 3)
                    act.activation(dp[:, n % 4, c0:], dl[:, n % 4, c0:], ACT.Exp, bias=o[:, tt, p, NMAX + x:NMAX + x + 1],
                                   accum_out=o[:, tt, p, DEN + x:DEN + x + 1]).then_inc(s_dac, 1)
                if n == PERMUTE_AT:
                    permute(0, 3)
                if n == STEPS + LAG_V - 1:
                    permute(3, 4)
                if n in OUT_UNITS:
                    hi(U0["dilout"] + OUT_UNITS.index(n))
                if n == MERGE_AT:
                    factors(0, 0, 3)

            for k in range(36):
                hi(U0["dil"] + k)
                for q in range(TICKS):
                    attend(k, q)
            for tick in range(TICKS * 36, LAST_TICK):
                attend(tick // TICKS, tick % TICKS)
            factors(1, 3, 4)
            for m in range(KD):
                if m == 1:
                    hi(U0["dilout"] + 3)
                act.wait_ge(s_free, A0["dilout"] + KD + m + 1)
                x_hi(m, None, G_MLP2 + 1, S0["dilout"] + m)
            rms("dilout")
            mlp(1, None)

        @block.vector
        def _(dve):
            chain = Chain(dve, s_dch)

            def lo(u, i=None, s=0):
                n = u + LOOK
                if n >= NU:
                    return
                dve.wait_ge(s_hi, at(n + 1, i, s))
                dve.tensor_tensor(wlo[:, n % SLOTS, :], raw[:, n % 2, :], whi[:, n % SLOTS, :].bitcast(F32),
                                  ALU.subtract).then_inc(s_split, 1)

            def x_lo(m, xn, g, i=None, s=0, mi=None):
                dve.wait_ge(s_xhi, at(xn + 1, i, s))
                gain = par[:, 8 * g + m:8 * g + m + 1] if mi is None else par[:, bass.ds(mi + 8 * g, 1)]
                dve.scalar_tensor_tensor(xlo[:, m, :], h[:, m, :], gain, xhi[:, m, :].bitcast(F32), ALU.mult,
                                         ALU.subtract).then_inc(s_x, 1)

            def inverse_rms(name):
                dve.wait_ge(s_nsq, N0[name] + 1)
                dve.reciprocal(rbc[:, :], rtmp[:, :]).then_inc(s_rb, 1)
                dve.wait_ge(s_rb, N0[name] + 1)

            def split(hi_, lo_, src, sem_=None):
                chain(dve.tensor_copy(hi_, src))
                ins = dve.tensor_tensor(lo_, src, hi_.bitcast(F32), ALU.subtract)
                if sem_ is None:
                    chain(ins)
                else:
                    ins.then_inc(sem_, 1)

            def residual(name, turns, nu, ng, g):
                u, a = U0[name], A0[name]
                step = nu // ng
                with dve.Fori(0, turns, 1) as i:
                    for m in range(ng):
                        for j in range(m * step, (m + 1) * step):
                            lo(u + j, i, nu)
                        dve.wait_ge(s_unit, at(u + (m + 1) * step, i, nu))
                        hm = h[:, i * ng + m, :]
                        dve.tensor_tensor(hm, hm, bank((a + m) % 2), ALU.add).then_inc(s_free, 1)
                        if g is not None:
                            x_lo(i * ng + m, X0[name] + m, g, i, ng, i * ng + m)

            def rows(u, a, dst, mul=rbc, op0=None, i=None, us=0):
                dve.wait_ge(s_unit, at(u + 1, i, us))
                dve.tensor_tensor(dst, bank(a % 2), mul[:, :], ALU.mult).then_inc(s_free, 1)

            dve.wait_ge(s_par, 32)
            dve.tensor_copy(trir[:, :, :], con[:, 1:3, :]).then_inc(s_con, 1)
            for m in range(KD):
                x_lo(m, m, G_MIX)
                if m < LOOK:
                    lo(m - LOOK)
            inverse_rms("start")
            lo(0)
            rows(U0["ga"], A0["ga"], gt[:, 0, :])
            dve.wait_ge(s_free, 1)
            dve.tensor_copy(ga[:, :], gt[0:16, 0, :]).then_inc(s_gdv, 1)
            def normed(f):
                dve.wait_ge(s_gac, f + 1)
                o = o_gla[:, f, :]
                chain(dve.reciprocal(gatt[:, f % 2, :], gatt[:, f % 2, :]))
                dve.scalar_tensor_tensor(o, o, par[:, C_GG + f:C_GG + f + 1], gatt[:, f % 2, :], ALU.mult, ALU.mult).then_inc(s_gdn, 1)

            for what, p in GLA_PLAN:
                E = 11 * p
                if (what, p) in GLA_UNITS:
                    n = GLA_UNITS.index((what, p))
                    lo(U0["gla"] + n)
                    rows(U0["gla"] + n, A0["gla"] + n, gate(p) if what == "gate" else gf[:, ("q", "k", "va", "vb").index(what), :])
                elif what == "cumulate":
                    if p == 0:
                        dve.wait_ge(s_pin, 32)
                    ba = par[:, C_BA + p:C_BA + p + 1]
                    dve.wait_ge(s_gad, 2 * p + 1)
                    chain(dve.tensor_scalar(gt[:, 0, :], bank(7), ba, 0.0, ALU.add, ALU.min))
                    chain(dve.tensor_tensor(gt[:, 0, :], gt[:, 0, :], gt[:, 1, :], ALU.subtract))
                    cum = gt[:, 2, :]
                    dve.tensor_tensor_scan(cum, smask[:, :], gt[:, 0, :], 0.0, ALU.mult, ALU.add).then_inc(s_gdc, 1)
                    dve.wait_ge(s_gdc, 3 * p + 1)
                    c3 = cum.rearrange("p (n c) -> p n c", c=GCH)
                    lastc = c3[:, :, GCH - 1:GCH].to_broadcast([P, 8, GCH])
                    dve.tensor_tensor(gt[:, 3, :].rearrange("p (n c) -> p n c", c=GCH), lastc, c3, ALU.subtract).then_inc(s_gdc, 1)
                elif what == "scale":
                    dve.wait_ge(s_gad, 2 * p + 2)
                    dve.wait_ge(s_free, A0["gla"] + GLA_UNITS.index(("k", p)) + 1)
                    chain(dve.scalar_tensor_tensor(gt[:, 0, :], gf[:, 0, :], DH ** -0.5, gt[:, 4, :], ALU.mult, ALU.mult))
                    split(gqk[:, 0, :], gqk[:, 1, :], gt[:, 0, :])
                    chain(dve.tensor_tensor(gt[:, 1, :], gf[:, 1, :], gt[:, 5, :], ALU.mult))
                    split(gqk[:, 2, :], gqk[:, 3, :], gt[:, 1, :])
                    dve.tensor_tensor(gt[:, 7, :], gf[:, 1, :], gt[:, 6, :], ALU.mult).then_inc(s_gdc, 1)
                elif what == "turn":
                    for n in range(3):
                        dve.wait_ge(s_gpe, E + 1 + n)
                        split(gtok[:, 2 * n, :], gtok[:, 2 * n + 1, :], bank(2 + n), s_gdv)
                    for x in range(2):
                        dve.wait_ge(s_gpe, E + 4 + x)
                        dve.tensor_copy(gatt[:, x, :], bank(5 + x)).then_inc(s_gat, 1)
                elif what == "states":
                    for x in range(2):
                        r = slice(64 * x, 64 * x + 64)
                        dve.wait_ge(s_gpe, E + 6 + x)
                        for n in range(1, 8):
                            ds = sbank(x, n - 1)[r, :]
                            if n == 1:
                                chain(dve.tensor_copy(gst[r, 1, :], ds))
                            else:
                                chain(dve.scalar_tensor_tensor(gst[r, n, :], gst[r, n - 1, :], gt[r, 4, n * GCH - 1:n * GCH], ds,
                                                               ALU.mult, ALU.add))
                    split(gstr[:, 0, 1:8, :], gstr[:, 1, 1:8, :], gst[:, 1:8, :], s_gdv)
                    for x in range(2):
                        dve.wait_ge(s_gpo, 2 * p + x + 1)
                        split(gatr[:, 2 * x, :], gatr[:, 2 * x + 1, :], gatt[:, x, :], s_gdv)
                elif what == "outputs":
                    for x in range(2):
                        dve.wait_ge(s_gpe, E + 8 + x)
                        o = o_gla[:, 2 * p + x, :]
                        chain(dve.tensor_copy(o, bank(5 + x)))
                        dve.tensor_tensor(gatt[:, x, :], o, o, ALU.mult).then_inc(s_gdv, 1)
                elif what == "normed":
                    normed(p)

            def qk(u, a, p):
                for j in range(2):
                    lo(u + j)
                    dve.wait_ge(s_unit, u + j + 1)
                    if p and j == 0:
                        dve.wait_ge(s_sac, 5 * p - 3)
                    dst = sl[:, j * T:(j + 1) * T]
                    dve.scalar_tensor_tensor(dst, bank((a + j) % 2), DH ** -0.5 if j == 0 else 1.0, rbc[:, :], ALU.mult,
                                             ALU.mult).then_inc(s_free, 1)
                    dve.wait_ge(s_free, a + j + 1)
                    split(sqk[:, 2 * j, :], sqk[:, 2 * j + 1, :], dst, s_sqk)

            qk(U0["sb"], A0["sb"], 0)
            lo(U0["sb"] + 2)
            rows(U0["sb"] + 2, A0["sb"] + 2, svf[:, :])
            for p in range(4):
                u, a = U0["sb"] + SB_PAIR * p, A0["sb"] + SB_PAIR * p
                E, A = 6 * p, 5 * p

                dve.wait_ge(s_spe, E + 1)
                if p == 0:
                    dve.wait_ge(s_svz, 1)
                vv = bank(5).rearrange("p (c d) -> p c d", d=P)
                for x in range(2):
                    d = slice(64 * x, 64 * x + 64)
                    chain(dve.tensor_copy(svp[:, 0, x, :, d], vv[:, :, d]))
                    ins = dve.tensor_tensor(svp[:, 1, x, :, d], vv[:, :, d], svp[:, 0, x, :, d].bitcast(F32), ALU.subtract)
                    if x:
                        ins.then_inc(s_sdv, 1)
                    else:
                        chain(ins)

                def softplus(x):
                    dve.wait_ge(s_sac, A + 1 + x)
                    dve.scalar_tensor_tensor(ssp[:, x, :], bank(2 + 3 * x, 3)[:, 0:CW], 0.0, sl[:, :], ALU.max,
                                             ALU.add).then_inc(s_sdv, 1)
                    dve.wait_ge(s_spo, 4 * p + 1 + x)
                    split(sspr[:, 0, x, :], sspr[:, 1, x, :], ssp[:, x, :], s_sdv)

                def weights(x):
                    dve.wait_ge(s_spo, 4 * p + 3 + x)
                    split(sspr[:, 0, x, :], sspr[:, 1, x, :], ssp[:, x, :], s_sdv)

                def output():
                    dve.wait_ge(s_spe, E + 6)
                    dve.tensor_copy(o_sb[:, p, :], bank(2)).then_inc(s_sdv, 1)

                lo(u + SB_R)
                softplus(0)
                rows(u + SB_R, a + SB_R, sgr[:, 0, :])
                if p == 0:
                    normed(2)
                lo(u + SB_G)
                softplus(1)
                rows(u + SB_G, a + SB_G, gate(KD + 2 * p))
                if p == 0:
                    normed(3)
                if p == 3:
                    for k in range(2):
                        split(*ogla_pair(k), o_gla[:, k, :], s_r)
                dve.wait_ge(s_sac, A + 3)
                chain(dve.tensor_tensor(sgr[:, 1, :], sgr[:, 1, :], sgr[:, 0, :], ALU.mult))
                dve.wait_ge(s_gdn, p + 1)
                chain(dve.tensor_tensor(o_gla[:, p, :], o_gla[:, p, :], sgr[:, 1, :], ALU.mult))
                lo(u + SB_G + 1)
                weights(0)
                rows(u + SB_G + 1, a + SB_G + 1, gate(KD + 2 * p + 1))
                if p < 3:
                    weights(1)
                    qk(u + SB_Q, a + SB_Q, p + 1)
                    lo(u + SB_V)
                    output()
                    rows(u + SB_V, a + SB_V, svf[:, :])
                else:
                    for k in range(2, 4):
                        split(*ogla_pair(k), o_gla[:, k, :], s_r)
                    lo(U0["branch"])
                    weights(1)
            for j in range(KD):
                u = U0["branch"] + j
                if 1 <= j < 4:
                    lo(u)
                dve.wait_ge(s_unit, u + 1)
                for m in range(2):
                    f, a = 2 * j + m, A0["branch"] + 2 * j + m
                    dve.wait_ge(s_sig, f + 1)
                    g = gate((f + KD) % (2 * KD))
                    dve.tensor_tensor(g, g, bank(BRANCH_BANKS[a % 4]), ALU.mult).then_inc(s_free, 1)
                if j >= 4:
                    lo(u)
                    for m in range(2):
                        f = 2 * j + m - KD
                        dve.wait_ge(s_yad, f + 1)
                        split(yr[:, 0, f, :], yr[:, 1, f, :], yf[:, m, :], s_r)
                if j == 1:
                    output()
                    dve.wait_ge(s_sdv, 32)
                    for k in range(4):
                        split(xhi[:, k, :], xlo[:, k, :], o_sb[:, k, :], s_r)
            residual("wout", 2, 4, 4, G_FFN)
            inverse_rms("wout")
            chain(dve.memset(apad[:, 0:2], 0.0))
            with dve.Fori(0, KF // 2, 1) as i:
                chain.loop(i, 2 * 4)
                for m in range(2):
                    u, a = U0["ffin"] + 2 * m, A0["ffin"] + 2 * m
                    tap = lambda k: par[:, bass.ds(i * 8 + (C_CONV + 4 * m + k), 1)]
                    lo(u, i, 4)
                    rows(u, a, apad[:, 2:], i=i, us=4)
                    dve.wait_ge(s_free, at(a + 1, i, 4))
                    t = cv[:, m, :]
                    chain(dve.tensor_scalar(t, apad[:, 2:], tap(2), tap(3), ALU.mult, ALU.add))
                    chain(dve.scalar_tensor_tensor(t, apad[:, 1:T + 1], tap(1), t, ALU.mult, ALU.add))
                    dve.scalar_tensor_tensor(t, apad[:, 0:T], tap(0), t, ALU.mult, ALU.add).then_inc(s_cv, 1)
                    lo(u + 1, i, 4)
                    rows(u + 1, a + 1, gs[:, :], i=i, us=4)
                    dve.wait_ge(s_ge, at(m + 1, i, 2))
                    dve.wait_ge(s_free, at(a + 2, i, 4))
                    chain(dve.tensor_tensor(gl[:, m, :], gl[:, m, :], gs[:, :], ALU.mult))
                    k = i * 2 + m
                    split(hid[:, 0, k, :], hid[:, 1, k, :], gl[:, m, :], s_r)
                chain.end(KF // 2)
            residual("ffout", 2, 12, 4, None)
            inverse_rms("ffout")
            dve.wait_ge(s_sqd, S0["final1"])
            for m in range(KD):
                dve.scalar_tensor_tensor(h[:, m, :], h[:, m, :], par[:, 8 * G_FIN + m:8 * G_FIN + m + 1], rbc[:, :],
                                         ALU.mult, ALU.mult).then_inc(s_cv, 1)
                if m:
                    dve.wait_ge(s_cv, KF + m)
                    x_lo(m - 1, X0["final1"] + m - 1, G_MIX2)
            dve.wait_ge(s_cv, KF + KD)
            x_lo(KD - 1, X0["final1"] + KD - 1, G_MIX2)
            lo(U0["cgv"])
            inverse_rms("final1")
            for j in range(1, 4):
                lo(U0["cgv"] + j)
            dve.wait_ge(s_cpe, 1)
            for t in range(NT):
                ins = dve.tensor_copy(rtok[:, t:t + 1], bank(7)[:, t * P:t * P + 1])
            ins.then_inc(s_cdv, 1)
            dve.wait_ge(s_cpo, 1)
            split(wsr[:, 0, :, :], wsr[:, 1, :, :], wsf[:, :, :], s_cdv)
            dve.wait_ge(s_cld, 48)
            for f in range(2):
                if f:
                    for j in range(4, 8):
                        lo(U0["cgv"] + j)
                for t in range(NT):
                    dve.wait_ge(s_cac, NT * f + t + 1)
                    chain(dve.bn_stats(st6[:, t, f, :], vt[:, t, f * T:(f + 1) * T]))
            for t in range(NT):
                ins = dve.bn_aggr(mv[:, t, 0:2], st6[:, t, :, :].rearrange("p a b -> p (a b)"))
                if t < NT - 1:
                    chain(ins)
                else:
                    ins.then_inc(s_cdv, 1)

            def layer_norm(t):
                dve.wait_ge(s_cac, 8 + t + 1)
                v = vt[:, t, :]
                chain(dve.reciprocal(mv[:, t, 3:4], mv[:, t, 2:3]))
                dve.tensor_scalar(v, v, mv[:, t, 0:1], mv[:, t, 3:4], ALU.subtract, ALU.mult).then_inc(s_lnd, 1)

            for m in range(KD):
                lo(U0["cgu"] + m)
                rows(U0["cgu"] + m, A0["cgu"] + m, uf[:, m, :])
                if m < NT:
                    layer_norm(m)
                if m >= NT:
                    t = m - NT
                    dve.wait_ge(s_lng, t + 1)
                    split(vr[:, 0, t, :], vr[:, 1, t, :], vt[:, t, :], s_r)
            for g in range(KD):
                dve.wait_ge(s_cpe, 2 + g)
                dve.wait_ge(s_cac, 12 + g + 1)
                b4 = bank(2 + g % 4).rearrange("p (t c) -> p t c", c=P)
                m4 = rtm[:, g % 2, :].rearrange("p (t c) -> p t c", c=P)
                row = bsb[:, g:g + 1, :].to_broadcast([P, NT, P])
                dve.tensor_tensor(m4, b4, row, ALU.add).then_inc(s_cdv, 1)
                dve.wait_ge(s_cdv, 4 + g)
                chain(dve.tensor_tensor(rtm[:, g % 2, :], uf[:, g, :], rtm[:, g % 2, :], ALU.mult))
                split(ugh[:, g, :], ugl[:, g, :], rtm[:, g % 2, :], s_r)
            residual("cgout", 2, 4, 4, G_MLP2)
            inverse_rms("cgout")

            def mlp(layer, g):
                for half in range(2):
                    up, dn = f"up{layer}{half}", f"down{layer}{half}"
                    k0 = 32 * layer + 16 * half
                    with dve.Fori(0, 4, 1) as i:
                        chain.loop(i, 4)
                        for m in range(4):
                            lo(U0[up] + m, i, 4)
                            dve.wait_ge(s_unit, at(U0[up] + m + 1, i, 4))
                            dve.scalar_tensor_tensor(mr[:, m % 2, :], bank((A0[up] + m) % 2), 0.0, rbc[:, :], ALU.max,
                                                     ALU.mult).then_inc(s_free, 1)
                            dve.wait_ge(s_ms, at(k0 + m + 1, i, 4))
                            k = i * 4 + m
                            split(mh[:, 0, k, :], mh[:, 1, k, :], ms[:, m % 2, :], s_r)
                        chain.end(4)
                    if half == 0:
                        if layer == 0:
                            dve.wait_ge(s_bmm, 1)
                            dve.tensor_copy(fsb[:, :], bank(2, 2)[0:8, :]).then_inc(s_bdv, 1)
                        residual(dn, 2, 8, 4, None)
                    elif layer == 0:
                        residual_x(dn, g, "down01")
                    else:
                        for m in range(KD):
                            lo(U0[dn] + 2 * m)
                            lo(U0[dn] + 2 * m + 1)
                            dve.wait_ge(s_unit, U0[dn] + 2 * m + 2)
                            hm = h[:, m, :]
                            dve.tensor_tensor(hm, hm, bank((A0[dn] + m) % 2), ALU.add).then_inc(s_free, 1)
                inverse_rms("down01" if layer == 0 else "down11")

            def residual_x(dn, g, name):
                residual(dn, 2, 8, 4, g)

            dve.memset(ohs[32:33, 0:24], NEG).then_inc(s_bdv, 1)
            mlp(0, G_MIX2 + 1)
            def out_of_bank(k):
                p, g, j = k // 9, k // 3 % 3, k % 3
                u, a = U0["dil"] + k, A0["dil"] + k
                if j == 2:
                    rows(u, a, dvf[:, :])
                    return
                dve.wait_ge(s_unit, u + 1)
                dst = mtmp[:, j, :]
                back = dst if j else dst[:, ::-1]
                dve.scalar_tensor_tensor(back, bank(a % 2), DH ** -0.5 if j == 0 else 1.0, rbc[:, :], ALU.mult,
                                         ALU.mult).then_inc(s_free, 1)
                dve.wait_ge(s_free, a + 1)
                if p and j == 0:
                    dve.wait_ge(s_dlo, 16 * p - (0 if g else 8))
                split(dqk[:, g, 2 * j, :], dqk[:, g, 2 * j + 1, :], dst, s_dqk)

            def merge(x, p0, p1):
                ps = slice(p0, p1)
                dve.wait_ge(s_perm, 64 * (x + 1))

                def c(k):
                    return cAB[:, k, :, ps, :]

                nA, nB = oA[:, :, ps, NMAX:ROW], oP[:, :, ps, NMAX:ROW]
                dA, dB = oA[:, :, ps, DEN:NMAX], oP[:, :, ps, DEN:NMAX]
                chain(dve.tensor_tensor(c(0), nA, nB, ALU.min))
                chain(dve.tensor_tensor(c(1), c(0), nA, ALU.subtract))
                dve.tensor_tensor(c(2), c(0), nB, ALU.subtract).then_inc(s_min, 1)
                dve.wait_ge(s_mex, x + 1)
                chain(dve.tensor_tensor(dA, dA, c(1), ALU.mult))
                chain(dve.tensor_tensor(dB, dB, c(2), ALU.mult))
                chain(dve.tensor_tensor(dA, dA, dB, ALU.add))
                chain(dve.reciprocal(c(3), dA))
                chain(dve.tensor_tensor(c(1), c(1), c(3), ALU.mult))
                ins = dve.tensor_tensor(c(2), c(2), c(3), ALU.mult)
                if x == 0:
                    ins.then_inc(s_fac, 1)
                    return
                chain(ins)
                chain(weigh(dve, p0)[1])
                ins = dve.tensor_tensor(oA[:, :, p0, 0:DEN], oA[:, :, p0, 0:DEN], oP[:, :, p0, 0:DEN], ALU.add)
                ins.then_inc(s_mrg, 1)

            def add_part(m, part):
                if m < KD - 1:
                    dve.wait_ge(s_dop, (KD - 1) * part + m + 1)
                else:
                    dve.wait_ge(s_unit, U0["dilout"] + 3 + part)
                if part and m == 0:
                    dve.wait_ge(s_free, A0["dilout"] + KD)
                dve.tensor_tensor(h[:, m, :], h[:, m, :], bank((A0["dilout"] + m) % 2), ALU.add).then_inc(s_free, 1)

            def outputs_split(j, b):
                dve.wait_ge(s_otr, j + 1)
                b3 = bank(b).rearrange("p (t q) -> p t q", q=P)[:, :, ::-1]
                o_hi, o_lo = (o.rearrange("p (t q) -> p t q", q=P) for o in out_pair(j))
                split(o_hi, o_lo, b3, s_r)

            def attend(k, q):
                if k and k % 3 == 0 and q == (1 if k == 36 else 2):
                    v = k // 3 - 1
                    dve.wait_ge(s_dtv, v + 1)
                    if v >= 3:
                        dve.wait_ge(s_dpv, 16 * (v // 3) - (0 if v % 3 else 8))
                    split(dvt[:, v % 3, 0, :], dvt[:, v % 3, 1, :], bank(7), s_dvs)
                n = STEP_AT.get(TICKS * k + q)
                if n is None:
                    return
                if n < STEPS:
                    p, part, x, t = step_of(n)
                    o, tt = (oB, 3 - t) if part else (oA, t)
                    c0 = 0 if t or part else 128
                    b0 = 256 * part
                    dve.wait_ge(s_dlo, n + 1)
                    if n >= 4:
                        dve.wait_ge(s_dac, n - 3)
                    chain(dve.tensor_tensor(dl[:, n % 4, c0:], bank(2 + n % 2)[:, c0:256], bias[:, 2 * p + x, b0 + c0:b0 + 256], ALU.add))
                    dve.tensor_reduce(o[:, tt, p, NMAX + x:NMAX + x + 1], dl[:, n % 4, c0:], AX, ALU.max, negate=True).then_inc(s_dlg, 1)
                if LAG_T <= n < STEPS + LAG_T:
                    m = n - LAG_T
                    c0 = 0 if m % 4 or m // 8 % 2 else 128
                    dve.wait_ge(s_dhi, m + 1)
                    dve.tensor_tensor(dpt[:, m % 4, 1, c0:], bank(4 + m % 2)[:, c0:256], dpt[:, m % 4, 0, c0:].bitcast(F32),
                                      ALU.subtract).then_inc(s_dsp, 1)
                if LAG_V <= n < STEPS + LAG_V and n % 4 == 3:
                    m = n - LAG_V
                    p, part, x, t = step_of(m)
                    dve.wait_ge(s_dpv, m + 1)
                    o3 = bank(6)[:, 0:256].rearrange("p (t d) -> p t d", d=DH)
                    o = oB[:, ::-1] if part else oA
                    dve.tensor_copy(o[:, :, p, x * DH:(x + 1) * DH], o3).then_inc(s_dof, 1)
                if n in OUT_UNITS:
                    lo(U0["dilout"] + OUT_UNITS.index(n))
                if OUT_AT < n <= OUT_AT + KD:
                    add_part(n - OUT_AT - 1, 0)
                if n == MERGE_AT:
                    merge(0, 0, 3)
                if n in SPLIT_AT:
                    j = SPLIT_AT.index(n)
                    outputs_split(j, (0, 1, 7)[j])

            dve.wait_ge(s_bld, 64)
            for k in range(37):
                for q in range(TICKS):
                    if q == 0 and k:
                        out_of_bank(k - 1)
                    if q == 1 and k < 36:
                        lo(U0["dil"] + k)
                    attend(k, q)
            for tick in range(TICKS * 37, LAST_TICK):
                attend(tick // TICKS, tick % TICKS)
            merge(1, 3, 4)
            outputs_split(3, 2)
            add_part(0, 1)
            for m in range(KD):
                if m < KD - 1:
                    add_part(m + 1, 1)
                x_lo(m, X0["dilout"] + m, G_MLP2 + 1)
            lo(U0["dilout"] + 3)
            inverse_rms("dilout")
            mlp(1, None)
            for m in range(KD):
                dve.scalar_tensor_tensor(h[:, m, :], h[:, m, :], par[:, 8 * G_FIN2 + m:8 * G_FIN2 + m + 1], rbc[:, :],
                                         ALU.mult, ALU.mult).then_inc(s_fin, 1)

        @block.gpsimd
        def _(pool):
            chain = Chain(pool, s_pch)

            def sum_squares(name):
                for m in range(KD):
                    n = S0[name] + m
                    pool.wait_ge(s_sqd, n + 1)
                    if m == 0:
                        ins = pool.tensor_copy(ssum[:, :], sq[:, 0, :])
                    else:
                        pool.wait_ge(s_ss, n)
                        ins = pool.tensor_tensor(ssum[:, :], ssum[:, :], sq[:, n % 2, :], ALU.add)
                    ins.then_inc(s_ss, 1)

            pool.memset(eps[:, :], EPS).then_inc(s_con, 1)
            sum_squares("start")
            for p in range(2):
                for x in range(2):
                    pool.wait_ge(s_gat, 2 * p + x + 1)
                    a3 = gatt[:, x, :].rearrange("p (t c) -> p t c", c=P)
                    chain(pool.affine_select(out=a3, in_=a3, pattern=[[0, NT], [1, P]], compare_op=ALU.is_ge, fill=0.0,
                                             base=0, channel_multiplier=-1))
                    pool.memset(a3[0:GCH, :, GCH:P], 0.0).then_inc(s_gpo, 1)
            pool.wait_ge(s_gdv, 17)
            pool.memset(svp[:, :, :, :, :].bitcast(F32), 0.0).then_inc(s_svz, 1)
            for p in range(4):
                for n in range(4):
                    x = n % 2
                    if n < 2:
                        pool.wait_ge(s_sdv, 8 * p + 2 + 2 * x)
                    else:
                        pool.wait_ge(s_sac, 5 * p + 4 + x)
                    for c in range(NT):
                        d = ssp[:, x, CO[c]:CO[c] + P]
                        ins = pool.affine_select(out=d, in_=d, pattern=[[1, P]], compare_op=ALU.is_gt, fill=0.0, base=0,
                                                 channel_multiplier=-1)
                    ins.then_inc(s_spo, 1)
            for f in range(KD):
                pool.wait_ge(s_free, A0["branch"] + KD + f + 1)
                if f >= 2:
                    pool.wait_ge(s_r, R0["y"] + f - 1)
                pool.tensor_tensor(yf[:, f % 2, :], gate(f), gate(KD + f), ALU.add).then_inc(s_yad, 1)
            sum_squares("wout")
            sum_squares("ffout")
            pool.wait_ge(s_cld, 48)
            pool.affine_select(out=wsf[:, :, :], in_=wsf[:, :, :], pattern=[[0, KD], [1, P]], compare_op=ALU.is_ge, fill=0.0,
                               base=0, channel_multiplier=-1).then_inc(s_cpo, 1)
            sum_squares("final1")
            pool.wait_ge(s_cld, 48)
            for t in range(NT):
                v = vt[:, t, :]
                pool.wait_ge(s_lnd, t + 1)
                chain(pool.tensor_tensor(v, v, lgb[:, 0, :], ALU.mult))
                pool.tensor_tensor(v, v, lgb[:, 1, :], ALU.add).then_inc(s_lng, 1)
            sum_squares("cgout")
            sum_squares("down01")
            pool.wait_ge(s_fac, 1)
            for p in range(3):
                chain(weigh(pool, p)[1])
                o = oA[:, :, p, 0:DEN]
                pool.tensor_tensor(o, o, oP[:, :, p, 0:DEN], ALU.add).then_inc(s_pmr, 1)
            sum_squares("dilout")
            sum_squares("down11")


def bucket(distance):
    n, exact = 32, 16
    nf = np.maximum(distance, 1).astype(np.float32)
    large = exact + (np.log(nf / np.float32(exact)) / np.float32(math.log(2048 / exact)) * np.float32(n - exact)).astype(np.int32)
    return np.where(distance < exact, distance, np.minimum(large, n - 1))


def one_hot():
    col = np.arange(256)
    out = np.zeros((33, 4, 256), np.float32)
    for g in range(4):
        rel = (P if g == 0 else 0) + P - 1 - col
        ok = (rel >= 0) & (rel <= P)
        if g == 3:
            ok &= rel % 4 == 0
        row = np.where(ok, bucket(np.clip(rel, 0, P) * (1 if g < 2 else 4)), 32)
        out[row, g, col] = 1.0
    return out.reshape(33, 1024)


def constants():
    i = np.arange(P)
    keep = np.tile((np.arange(T) % GCH != 0).astype(np.float32), (P, 1))
    tri = -(i[:, None] >= i[None, :]).astype(np.float32)
    one = np.ones((P, P), np.float32)
    return np.concatenate([np.eye(P, dtype=np.float32), tri, -one, one, keep], 1)


def units(w, k_tiles=UT):
    K, M = w.shape
    n = -(-K // (P * k_tiles))
    if K < n * P * k_tiles:
        w = np.concatenate([w, np.zeros((n * P * k_tiles - K, M), w.dtype)], 0)
    return w.reshape(n, k_tiles, P, M // P, P).transpose(3, 0, 2, 1, 4).reshape(n * M // P, P, k_tiles * P)


def wide_units(w):
    return w.reshape(4, P, -1, 2, P).transpose(2, 1, 3, 0, 4).reshape(-1, P, UT * P)


def stream(a):
    w = a["w_in"][0]
    out = [units(w[:, OFF_GA:OFF_GA + P])]
    first = {"q": lambda p: OFF_GQ + P * p, "k": lambda p: OFF_GK + P * p, "va": lambda p: OFF_GV + 2 * P * p,
             "vb": lambda p: OFF_GV + 2 * P * p + P, "gate": lambda f: OFF_G0 + P * f}
    cols = [first[what](p) for what, p in GLA_UNITS] + [o for o in (OFF_Q, OFF_K, OFF_V)]
    for p in range(4):
        cols += [OFF_GR + P * p, OFF_G1 + 2 * P * p, OFF_G1 + 2 * P * p + P]
        cols += [o + P * (p + 1) for o in (OFF_Q, OFF_K, OFF_V)] if p < 3 else []
    out += [units(w[:, c:c + P]) for c in cols]
    out += [wide_units(a["w_branch_gla"][0]), wide_units(a["w_branch_sb"][0]), units(a["w_out"][0])]
    f = a["w_ffn_in"][0]
    out += [np.stack([units(f[:, :FF]), units(f[:, FF:])], 1).reshape(-1, P, UT * P), units(a["w_ffn_out"][0])]
    w = a["a_w_in_2"][0]
    v = w[:, D:].reshape(4, 2, P, 2, T).transpose(3, 0, 2, 1, 4).reshape(8, P, UT * P)
    out += [v, units(w[:, :D]), units(a["a_w_out_2"][0])]

    def mlp(n):
        up, down = a["w_up_2"][n], a["w_down_2"][n]
        return [x for s in (0, FF2 // 2) for x in (units(up[:, s:s + FF2 // 2]), units(down[s:s + FF2 // 2]))]

    out += mlp(0)
    w = a["b_w_qkv_2"][0]
    for p in range(4):
        for g in range(3):
            out += [units(w[:, 1536 * c + 512 * g + P * p:1536 * c + 512 * g + P * (p + 1)]) for c in range(3)]
    t = wide_units(a["b_w_out_2"][0]).reshape(4, P, 2, 4, P).transpose(0, 2, 3, 1, 4).reshape(KD, 4, P, P)
    t = np.concatenate([t[:, :3].reshape(-1, P, P), t[:, 3]], 0)
    out += [t.reshape(4, UT, P, P).transpose(0, 2, 1, 3).reshape(4, P, UT * P)] + mlp(1)
    out = np.concatenate(out, 0)
    assert out.shape[0] == NU
    return out


def columns(v):
    return v.reshape(-1, P).T


def params(a):
    g2 = a["mix_norm_g_2"], a["mlp_norm_g_2"]
    rows = [a["norm_mix_g"][0], a["norm_ffn_g"][0], a["norm_final_g"], g2[0][0], g2[0][1], g2[1][0], g2[1][1],
            a["final_norm_g_2"], a["b_gate"][0, 0], a["b_gate"][0, 1]]
    conv = np.concatenate([a["conv_w"][0], a["conv_b"]], 0).reshape(4, KF, P).transpose(2, 1, 0).reshape(P, 4 * KF)
    return np.concatenate([columns(r) for r in rows] + [conv, columns(a["b_alpha"][0]), columns(a["gla_norm_g"][0])], 1)


def kernel(**inputs):
    import concourse.bacc as bacc
    from concourse.bass_utils import run_bass_kernel_spmd

    a = {k: np.asarray(v) for k, v in inputs.items()}
    arrays = {
        "wst": stream(a),
        "xT": a["x"][0].T.reshape(KD, P, T),
        "prm": params(a),
        "cst": constants(),
        "wup": a["w_alpha_up"][0],
        "wsT": a["a_w_s_2"][0].transpose(2, 0, 1),
        "bs": a["a_b_s_2"][0],
        "lngb": np.stack([a["a_ln_g_2"][0], a["a_ln_b_2"][0]]),
        "rb": a["rel_bias_2"],
        "onehot": one_hot(),
    }
    arrays = {k: np.ascontiguousarray(v) for k, v in arrays.items()}
    nc = bacc.Bacc("TRN2", target_bir_lowering=False, num_devices=1)
    args = [nc.dram_tensor(n, v.shape, mybir.dt.from_np(v.dtype), kind="ExternalInput").ap() for n, v in arrays.items()]
    fdram = nc.dram_tensor("bias_rows", (8, 1024), F32, kind="Internal").ap()
    out = nc.dram_tensor("out", (KD, P, T), F32, kind="ExternalOutput").ap()
    build(nc, *args, fdram, out)
    r = run_bass_kernel_spmd(nc, [arrays], core_ids=[0])
    got = r.results[0]["out"]
    return np.ascontiguousarray(got.reshape(D, T).T).reshape(1, T, D)
```
